# Optimizing a Trainium2 kernel written in Bass

```python
import math
import jax
import jax.numpy as jnp
from jax import lax
import numpy as np

D_MODEL = 1024
BATCH = 1
SEQ = 512
DEPTH = 2

MLA_HEADS = 8
MLA_Q_LORA = 256
MLA_KV_LORA = 128
MLA_NOPE = 64
MLA_ROPE = 32
MLA_V = 64
DIFF_HEADS = 8
DIFF_HEAD_DIM = 32
DIFF_ROT = DIFF_HEAD_DIM // 4
DIFF_QK = DIFF_HEADS * 2 * DIFF_HEAD_DIM
DIFF_V = DIFF_HEADS * 2 * DIFF_HEAD_DIM
SSM_GROUP = 16
SSM_GROUPS = 32
SSM_WIDTH = SSM_GROUP * SSM_GROUPS
SSM_STATE = 64
N_BRANCH = 3
IN_WIDTH = MLA_Q_LORA + MLA_KV_LORA + MLA_ROPE + 2 * DIFF_QK + DIFF_V + SSM_WIDTH + N_BRANCH * D_MODEL
ROPE_THETA = 500000.0
Q_BLOCK = 128
N_EXPERTS = 32
N_GROUPS = 8
EXPERTS_PER_GROUP = N_EXPERTS // N_GROUPS
TOP_K = 2
EXPERT_FF = 512
MOE_BLOCK = 128
DN_ALPHA = (2 * DEPTH) ** 0.25
DN_BETA = (8 * DEPTH) ** -0.25
LN_EPS = 1e-5
RMS_EPS = 1e-6

kernel_name = "hybrid_mla_diff_s5_moe_deepnorm"

def _rmsnorm(x, g, eps=RMS_EPS):
    xf = x.astype(jnp.float32)
    y = xf * lax.rsqrt(jnp.mean(xf * xf, axis=-1, keepdims=True) + eps)
    return (y * g.astype(jnp.float32)).astype(x.dtype)

def _layernorm(x, g, b):
    xf = x.astype(jnp.float32)
    mu = jnp.mean(xf, axis=-1, keepdims=True)
    xc = xf - mu
    var = jnp.mean(xc * xc, axis=-1, keepdims=True)
    y = xc * lax.rsqrt(var + LN_EPS) * g.astype(jnp.float32) + b.astype(jnp.float32)
    return y.astype(x.dtype)

def _rope_tables(positions, rot_dim):
    inv = ROPE_THETA ** (-jnp.arange(0, rot_dim, 2, dtype=jnp.float32) / rot_dim)
    ang = positions.astype(jnp.float32)[..., None] * inv
    return jnp.cos(ang)[:, :, None, :], jnp.sin(ang)[:, :, None, :]

def _apply_rope(x, cos, sin):
    half = cos.shape[-1]
    rot = 2 * half
    xf = x[..., :rot].astype(jnp.float32)
    x1, x2 = xf[..., :half], xf[..., half:]
    r = jnp.concatenate([x1 * cos - x2 * sin, x2 * cos + x1 * sin], axis=-1).astype(x.dtype)
    return jnp.concatenate([r, x[..., rot:]], axis=-1)

def _causal_attention(q, k, v, scale):
    B, S, H, dq = q.shape
    nb = S // Q_BLOCK
    qb = jnp.moveaxis(q.reshape(B, nb, Q_BLOCK, H, dq), 1, 0)
    kpos = jnp.arange(S)

    def block(args):
        qi, bi = args
        s = jnp.einsum('bqhd,bkhd->bhqk', qi, k, preferred_element_type=jnp.float32) * scale
        qpos = bi * Q_BLOCK + jnp.arange(Q_BLOCK)
        s = jnp.where(kpos[None, :] <= qpos[:, None], s, -1e30)
        p = jax.nn.softmax(s, axis=-1).astype(v.dtype)
        return jnp.einsum('bhqk,bkhd->bqhd', p, v)

    o = lax.map(block, (qb, jnp.arange(nb)))
    return jnp.moveaxis(o, 0, 1).reshape(B, S, H, v.shape[-1])

def _split_in(u):
    sizes = (MLA_Q_LORA, MLA_KV_LORA, MLA_ROPE, DIFF_QK, DIFF_QK, DIFF_V, SSM_WIDTH, N_BRANCH * D_MODEL)
    cuts = [int(c) for c in np.cumsum(sizes)[:-1]]
    return jnp.split(u, cuts, axis=-1)

def _mla_branch(c_q, c_kv, k_r, cos, sin, q_norm, w_uq, kv_norm, w_ukv, w_out):
    B, S, _ = c_q.shape
    q = (_rmsnorm(c_q, q_norm) @ w_uq).reshape(B, S, MLA_HEADS, MLA_NOPE + MLA_ROPE)
    q = jnp.concatenate([q[..., :MLA_NOPE], _apply_rope(q[..., MLA_NOPE:], cos, sin)], axis=-1)
    kv = (_rmsnorm(c_kv, kv_norm) @ w_ukv).reshape(B, S, MLA_HEADS, MLA_NOPE + MLA_V)
    k_nope, v = kv[..., :MLA_NOPE], kv[..., MLA_NOPE:]
    k_rope = _apply_rope(k_r[:, :, None, :], cos, sin)
    k = jnp.concatenate([k_nope, jnp.broadcast_to(k_rope, (B, S, MLA_HEADS, MLA_ROPE))], axis=-1)
    o = _causal_attention(q, k, v, (MLA_NOPE + MLA_ROPE) ** -0.5)
    return o.reshape(B, S, MLA_HEADS * MLA_V) @ w_out

def _diff_branch(q, k, v, cos, sin, lam, subln, w_out, lambda_init):
    B, S, _ = q.shape
    q = q.reshape(B, S, DIFF_HEADS, 2, DIFF_HEAD_DIM)
    k = k.reshape(B, S, DIFF_HEADS, 2, DIFF_HEAD_DIM)
    v = v.reshape(B, S, DIFF_HEADS, 2 * DIFF_HEAD_DIM)
    q1, q2 = _apply_rope(q[:, :, :, 0], cos, sin), _apply_rope(q[:, :, :, 1], cos, sin)
    k1, k2 = _apply_rope(k[:, :, :, 0], cos, sin), _apply_rope(k[:, :, :, 1], cos, sin)
    lf = lam.astype(jnp.float32)
    lam_val = jnp.exp(jnp.sum(lf[0] * lf[1])) - jnp.exp(jnp.sum(lf[2] * lf[3])) + lambda_init
    scale = DIFF_HEAD_DIM ** -0.5
    o = _causal_attention(q1, k1, v, scale) - lam_val.astype(v.dtype) * _causal_attention(q2, k2, v, scale)
    o = _rmsnorm(o, subln, 1e-5) * (1.0 - lambda_init)
    return o.reshape(B, S, DIFF_V) @ w_out

def _ssm_branch(u, a_re, a_im, log_dt, b_re, b_im, c_re, c_im, d, w_glu):
    B, S, _ = u.shape
    uf = u.astype(jnp.float32).reshape(B, S, SSM_GROUPS, SSM_GROUP)
    A = lax.complex(a_re.astype(jnp.float32), a_im.astype(jnp.float32))
    dt = jnp.exp(log_dt.astype(jnp.float32))[:, None]
    a_bar = jnp.exp(A * dt)
    b_bar = ((a_bar - 1.0) / A)[..., None] * lax.complex(b_re.astype(jnp.float32), b_im.astype(jnp.float32))
    bu = jnp.einsum('bsgp,gnp->sbgn', uf.astype(jnp.complex64), b_bar)
    a_seq = jnp.broadcast_to(a_bar[None, None], (S, 1, SSM_GROUPS, SSM_STATE))

    def combine(left, right):
        a_l, b_l = left
        a_r, b_r = right
        return a_r * a_l, a_r * b_l + b_r

    _, h = lax.associative_scan(combine, (a_seq, bu), axis=0)
    C = lax.complex(c_re.astype(jnp.float32), c_im.astype(jnp.float32))
    y = jnp.real(jnp.einsum('sbgn,gpn->bsgp', h, C)) + d.astype(jnp.float32).reshape(SSM_GROUPS, SSM_GROUP) * uf
    y = jax.nn.gelu(y.reshape(B, S, SSM_WIDTH)).astype(u.dtype)
    gl = y @ w_glu
    return gl[..., :D_MODEL] * jax.nn.sigmoid(gl[..., D_MODEL:])

def _moe(x, router_w, router_bias, w_gate, w_up, w_down):
    B, S, D = x.shape
    T = B * S
    xt = x.reshape(T, D)
    scores = jax.nn.sigmoid((xt @ router_w).astype(jnp.float32))
    biased = scores + router_bias.astype(jnp.float32)
    grouped = biased.reshape(T, N_GROUPS, EXPERTS_PER_GROUP)
    group_score = jnp.sum(lax.top_k(grouped, TOP_K)[0], axis=-1)
    g_sel = jnp.argmax(group_score, axis=-1)
    in_group = jnp.take_along_axis(grouped, g_sel[:, None, None], axis=1)[:, 0]
    _, loc = lax.top_k(in_group, TOP_K)
    idx = g_sel[:, None] * EXPERTS_PER_GROUP + loc
    w = jnp.take_along_axis(scores, idx, axis=1)
    w = w / jnp.sum(w, axis=-1, keepdims=True)
    A = T * TOP_K
    e_flat = idx.reshape(A)
    tok_flat = jnp.arange(A, dtype=jnp.int32) // TOP_K
    order = jnp.argsort(e_flat)
    e_sorted, tok_sorted, w_sorted = e_flat[order], tok_flat[order], w.reshape(A)[order]
    counts = jnp.zeros((N_EXPERTS,), jnp.int32).at[e_flat].add(1)
    starts = jnp.cumsum(counts) - counts
    padded = (counts + MOE_BLOCK - 1) // MOE_BLOCK * MOE_BLOCK
    pad_ends = jnp.cumsum(padded)
    pad_starts = pad_ends - padded
    dest = pad_starts[e_sorted] + jnp.arange(A, dtype=jnp.int32) - starts[e_sorted]
    n_blocks = -(-A // MOE_BLOCK) + N_EXPERTS
    R = n_blocks * MOE_BLOCK
    row_tok = jnp.full((R,), T, jnp.int32).at[dest].set(tok_sorted)
    row_w = jnp.zeros((R,), jnp.float32).at[dest].set(w_sorted)
    block_e = jnp.minimum(jnp.searchsorted(pad_ends, jnp.arange(n_blocks, dtype=jnp.int32) * MOE_BLOCK, side='right'), N_EXPERTS - 1)
    x_pad = jnp.concatenate([xt, jnp.zeros((1, D), xt.dtype)], axis=0)
    xb = x_pad[row_tok].reshape(n_blocks, MOE_BLOCK, D)

    def expert_block(args):
        xi, e = args
        hdn = jax.nn.silu(xi @ w_gate[e]) * (xi @ w_up[e])
        return hdn @ w_down[e]

    yb = lax.map(expert_block, (xb, block_e)).reshape(R, D)
    y = jnp.zeros((T + 1, D), jnp.float32).at[row_tok].add(yb.astype(jnp.float32) * row_w[:, None])[:T]
    return y.astype(x.dtype).reshape(B, S, D)

def setup_inputs(seed: int = 0) -> dict:
    key = jax.random.key(seed)
    keys = jax.random.split(key, 40)
    counter = [0]

    def nxt():
        counter[0] += 1
        return keys[counter[0] - 1]

    def nrm(shape, scale):
        return jax.random.normal(nxt(), shape, jnp.float32) * scale

    L = DEPTH
    x = nrm((BATCH, SEQ, D_MODEL), 1.0)
    positions = (jax.random.randint(nxt(), (BATCH, 1), 0, 1024) + jnp.arange(SEQ)[None, :]).astype(jnp.int32)
    w_in = nrm((L, D_MODEL, IN_WIDTH), D_MODEL ** -0.5)
    b_gate = nrm((L, N_BRANCH, D_MODEL), 0.01)
    mla_q_norm = 1.0 + nrm((L, MLA_Q_LORA), 0.01)
    mla_w_uq = nrm((L, MLA_Q_LORA, MLA_HEADS * (MLA_NOPE + MLA_ROPE)), MLA_Q_LORA ** -0.5)
    mla_kv_norm = 1.0 + nrm((L, MLA_KV_LORA), 0.01)
    mla_w_ukv = nrm((L, MLA_KV_LORA, MLA_HEADS * (MLA_NOPE + MLA_V)), MLA_KV_LORA ** -0.5)
    mla_w_out = nrm((L, MLA_HEADS * MLA_V, D_MODEL), (MLA_HEADS * MLA_V) ** -0.5)
    diff_lambda = nrm((L, 4, DIFF_HEAD_DIM), 0.1)
    diff_subln = 1.0 + nrm((L, 2 * DIFF_HEAD_DIM), 0.01)
    diff_w_out = nrm((L, DIFF_V, D_MODEL), DIFF_V ** -0.5)
    ssm_a_re = -0.5 + nrm((L, SSM_GROUPS, SSM_STATE), 0.01)
    ssm_a_im = jnp.pi * jnp.arange(SSM_STATE, dtype=jnp.float32) + nrm((L, SSM_GROUPS, SSM_STATE), 0.01)
    ssm_log_dt = jax.random.uniform(nxt(), (L, SSM_GROUPS), jnp.float32, math.log(1e-3), math.log(1e-1))
    ssm_b_re = nrm((L, SSM_GROUPS, SSM_STATE, SSM_GROUP), (2 * SSM_GROUP) ** -0.5)
    ssm_b_im = nrm((L, SSM_GROUPS, SSM_STATE, SSM_GROUP), (2 * SSM_GROUP) ** -0.5)
    ssm_c_re = nrm((L, SSM_GROUPS, SSM_GROUP, SSM_STATE), (2 * SSM_STATE) ** -0.5)
    ssm_c_im = nrm((L, SSM_GROUPS, SSM_GROUP, SSM_STATE), (2 * SSM_STATE) ** -0.5)
    ssm_d = nrm((L, SSM_WIDTH), 1.0)
    ssm_w_glu = nrm((L, SSM_WIDTH, 2 * D_MODEL), SSM_WIDTH ** -0.5)
    w_o = nrm((L, D_MODEL, D_MODEL), D_MODEL ** -0.5 * DN_BETA)
    ln_gain = 1.0 + nrm((L, 2, D_MODEL), 0.01)
    ln_bias = nrm((L, 2, D_MODEL), 0.01)
    router_w = nrm((D_MODEL, N_EXPERTS), D_MODEL ** -0.5)
    router_bias = nrm((N_EXPERTS,), 0.01)
    moe_w_gate = nrm((L, N_EXPERTS, D_MODEL, EXPERT_FF), D_MODEL ** -0.5)
    moe_w_up = nrm((L, N_EXPERTS, D_MODEL, EXPERT_FF), D_MODEL ** -0.5)
    moe_w_down = nrm((L, N_EXPERTS, EXPERT_FF, D_MODEL), EXPERT_FF ** -0.5 * DN_BETA)
    return {"x": x, "positions": positions, "w_in": w_in, "b_gate": b_gate,
            "mla_q_norm": mla_q_norm, "mla_w_uq": mla_w_uq, "mla_kv_norm": mla_kv_norm,
            "mla_w_ukv": mla_w_ukv, "mla_w_out": mla_w_out, "diff_lambda": diff_lambda,
            "diff_subln": diff_subln, "diff_w_out": diff_w_out, "ssm_a_re": ssm_a_re,
            "ssm_a_im": ssm_a_im, "ssm_log_dt": ssm_log_dt, "ssm_b_re": ssm_b_re,
            "ssm_b_im": ssm_b_im, "ssm_c_re": ssm_c_re, "ssm_c_im": ssm_c_im, "ssm_d": ssm_d,
            "ssm_w_glu": ssm_w_glu, "w_o": w_o, "ln_gain": ln_gain, "ln_bias": ln_bias,
            "router_w": router_w, "router_bias": router_bias, "moe_w_gate": moe_w_gate,
            "moe_w_up": moe_w_up, "moe_w_down": moe_w_down}

def reference(x, positions, w_in, b_gate, mla_q_norm, mla_w_uq, mla_kv_norm, mla_w_ukv, mla_w_out,
              diff_lambda, diff_subln, diff_w_out, ssm_a_re, ssm_a_im, ssm_log_dt, ssm_b_re, ssm_b_im,
              ssm_c_re, ssm_c_im, ssm_d, ssm_w_glu, w_o, ln_gain, ln_bias, router_w, router_bias,
              moe_w_gate, moe_w_up, moe_w_down):
    B, S, _ = x.shape
    cos_a, sin_a = _rope_tables(positions, MLA_ROPE)
    cos_b, sin_b = _rope_tables(positions, DIFF_ROT)
    for l in range(DEPTH):
        u = x @ w_in[l]
        c_q, c_kv, k_r, q_d, k_d, v_d, u_s, g_logit = _split_in(u)
        y_a = _mla_branch(c_q, c_kv, k_r, cos_a, sin_a, mla_q_norm[l], mla_w_uq[l],
                          mla_kv_norm[l], mla_w_ukv[l], mla_w_out[l])
        lambda_init = 0.8 - 0.6 * math.exp(-0.3 * l)
        y_b = _diff_branch(q_d, k_d, v_d, cos_b, sin_b, diff_lambda[l], diff_subln[l],
                           diff_w_out[l], lambda_init)
        y_c = _ssm_branch(u_s, ssm_a_re[l], ssm_a_im[l], ssm_log_dt[l], ssm_b_re[l], ssm_b_im[l],
                          ssm_c_re[l], ssm_c_im[l], ssm_d[l], ssm_w_glu[l])
        gates = jax.nn.sigmoid((g_logit.reshape(B, S, N_BRANCH, D_MODEL) + b_gate[l]).astype(jnp.float32)).astype(x.dtype)
        merged = gates[:, :, 0] * y_a + gates[:, :, 1] * y_b + gates[:, :, 2] * y_c
        x = _layernorm(DN_ALPHA * x + merged @ w_o[l], ln_gain[l, 0], ln_bias[l, 0])
        x = _layernorm(DN_ALPHA * x + _moe(x, router_w, router_bias, moe_w_gate[l], moe_w_up[l], moe_w_down[l]),
                       ln_gain[l, 1], ln_bias[l, 1])
    return x


_drawn_inputs = setup_inputs


def setup_inputs(seed=0):
    import zlib

    import numpy as np

    out = dict(_drawn_inputs(seed))
    spreads = {}
    factors = {'b_gate': 6.655,
     'mla_q_norm': 8.0,
     'mla_kv_norm': 5.738,
     'diff_subln': 3.183,
     'ssm_a_re': 64.0,
     'ssm_log_dt': 2.892,
     'ssm_b_re': 25.743,
     'ssm_b_im': 9.883,
     'ssm_c_re': 20.969,
     'ssm_c_im': 16.367,
     'ssm_a_im': 4.3}
    for name, (base, spread) in spreads.items():
        noise = np.random.default_rng([zlib.crc32(name.encode()), seed]).standard_normal(out[name].shape)
        drawn = base * np.exp(spread * noise) if base else spread * noise
        out[name] = jnp.asarray(drawn.astype(out[name].dtype))
    for name, factor in factors.items():
        out[name] = (out[name] * factor).astype(out[name].dtype)
    return out
```

```python
import math
from contextlib import ExitStack

import numpy as np

import concourse.bass as bass
from concourse import mybir

F32 = mybir.dt.float32
I32 = mybir.dt.int32
U32 = mybir.dt.uint32
ALU = mybir.AluOpType
ACT = mybir.ActivationFunctionType
AXX = mybir.AxisListType.X

P = 128
BANK = 512
DEPTH = 2
SEQ = 512
D_MODEL = 1024
TT = SEQ // P
KD = D_MODEL // P
Q_LORA, KV_LORA, ROPE_A, NOPE, V_DIM = 256, 128, 32, 64, 64
HEADS = 8
HD = 32
ROT_B = HD // 4
MLA_COLS = Q_LORA + KV_LORA + ROPE_A
DIFF_COLS = HEADS * 2 * HD
OFF_DIFF = MLA_COLS
OFF_SSM = OFF_DIFF + 3 * DIFF_COLS
SSM_W, GROUP, GROUPS, STATES = 512, 16, 32, 64
OFF_GATE = OFF_SSM + SSM_W
STILES = GROUPS * STATES // P
FINE = 32
COARSE = SEQ // FINE
DOUBLINGS = 10
EXPERTS, EGROUPS, EPER, FF = 32, 8, 4, 512
KF = FF // P
PASSES = SEQ // P
ALPHA = (2 * DEPTH) ** 0.25
LN_EPS, RMS_EPS, SUB_EPS = 1e-5, 1e-6, 1e-5
THETA = 500000.0
NEG = -1e30
FAR = 4096.0
ROUND = 12582912.0
TWO_PI = 2 * math.pi
PI_HI = 6.28125
PI_LO = TWO_PI - PI_HI
PI_MAX = 3.1415925
SCALE_A = (NOPE + ROPE_A) ** -0.5
SCALE_B = HD ** -0.5

CONST_W = dict(ident=P, upper=P, ones=P, slot=P, causal=P, gmask=8, bmask=32, inv=20, eprio=32,
               gprio=8, tok=TT, fine=FINE, coarse=COARSE)
CONST_AT, _n = {}, 0
for _k, _w in CONST_W.items():
    CONST_AT[_k] = _n
    _n += _w
CONST_COLS = _n


def constant_table():
    c = np.zeros((P, CONST_COLS), np.float32)
    p = np.arange(P)

    def put(name, v):
        c[:, CONST_AT[name]:CONST_AT[name] + CONST_W[name]] = v

    put("ident", np.eye(P))
    put("upper", p[:, None] < p[None, :])
    put("ones", 1.0)
    put("slot", p[None, :])
    put("causal", np.where(p[None, :] > p[:, None], NEG, 0.0))
    put("gmask", (p[:, None] // GROUP) == np.arange(8)[None, :])
    jj, g = np.divmod(np.arange(32), 8)
    put("bmask", g[None, :] == 2 * jj[None, :] + (p[:, None] >= STATES))
    inv = [np.float32(THETA) ** (-np.arange(0, r, 2, dtype=np.float32) / np.float32(r)) for r in (ROPE_A, ROT_B)]
    put("inv", np.concatenate(inv)[None, :])
    put("eprio", EXPERTS - np.arange(EXPERTS)[None, :])
    put("gprio", EGROUPS - np.arange(EGROUPS)[None, :])
    put("tok", np.arange(TT)[None, :] * P + p[:, None])
    put("fine", np.arange(FINE)[None, :])
    put("coarse", np.arange(COARSE)[None, :] * FINE)
    return c


def layer_table():
    li = np.array([0.8 - 0.6 * math.exp(-0.3 * l) for l in range(DEPTH)])
    return np.broadcast_to(np.stack([li, 1.0 - li], 1)[:, None, :], (DEPTH, P, 2)).astype(np.float32).copy()


STEPS = dict(front=1, heads=4, join=1, merge=2, tail=1, last=1)
RAISED = dict(
    b0=(3, 6, 1, 6, 4, 0), b1=(3, 6, 1, 6, 4, 0), b2=(3, 6, 1, 6, 3, 0), b3=(2, 6, 1, 6, 3, 0),
    b4=(2, 15, 0, 2, 3, 0), b5=(2, 14, 0, 2, 3, 0), b6=(2, 20, 0, 0, 3, 0), full7=(2, 0, 0, 0, 3, 0),
    b7=(2, 1, 0, 0, 3, 0),
    sq_sums=(1, 0, 0, 0, 0, 0), rms_mean=(1, 0, 1, 0, 0, 0), rms_root=(1, 0, 1, 0, 0, 0),
    lora_ready=(1, 0, 0, 0, 0, 0),
    q_ready=(0, 2, 0, 0, 0, 0), kv_ready=(0, 2, 0, 0, 0, 0), diff_copied=(0, 2, 0, 0, 0, 0),
    diff_ready=(0, 2, 0, 0, 0, 0), max_ready=(0, 6, 0, 0, 0, 0), mix_ready=(0, 8, 0, 0, 0, 0),
    oa_ready=(0, 2, 0, 0, 0, 0), pads_ready=(0, 1, 0, 0, 0, 0), rot_ready=(0, 4, 0, 0, 0, 0),
    scan_ready=(0, 4, 0, 0, 0, 0), h_ready=(0, 4, 0, 0, 0, 0),
    h_used=(0, 4, 0, 0, 0, 0), wd_ready=(0, 1, 0, 0, 0, 0),
    ob_ready=(0, 0, 4, 0, 0, 0), gelu_done=(0, 0, 1, 0, 0, 0),
    y_ready=(0, 1, 0, 0, 0, 0), g_used=(0, 4, 0, 0, 0, 0),
    merged_ready=(0, 0, 0, 12, 0, 0),
    ln_var=(0, 0, 0, 0, 4, 4), ln_root=(0, 0, 0, 0, 4, 4), ln_ready=(0, 0, 0, 0, 4, 4),
)
for _b in range(7):
    RAISED[f"full{_b}"] = RAISED[f"b{_b}"]
    RAISED[f"free{_b}"] = RAISED[f"b{_b}"]
RAISED["free7"] = RAISED["b7"]


def at(name, phase, n, step=0):
    v = n
    for k, (ph, steps) in enumerate(STEPS.items()):
        if ph == phase:
            return v + step * RAISED[name][k]
        v += steps * RAISED[name][k]


class Chain:

    def __init__(self, eng, sem):
        self.eng, self.sem, self.n = eng, sem, 0

    def reset(self):
        self.eng.sem_clear(self.sem)
        self.n = 0

    def add(self, ins):
        ins.then_inc(self.sem, 1)
        self.n += 1
        return ins

    def wait(self):
        if self.n:
            self.eng.wait_ge(self.sem, self.n)

    def then(self, ins):
        self.add(ins)
        self.wait()


def build(nc, t_in, consts, layer_consts, out):
    ctx = ExitStack()
    sb = ctx.enter_context(nc.sbuf_tensor("sb", [P, 53100], F32))
    psum = ctx.enter_context(nc.psum_tensor("psum", [P, 8, BANK], F32))
    pos_i = ctx.enter_context(nc.sbuf_tensor("pos_i", [P, TT], I32))
    idx = [ctx.enter_context(nc.sbuf_tensor(f"idx{i}", [P, 2], U32)) for i in range(2)]
    idx_none = ctx.enter_context(nc.sbuf_tensor("idx_none", [P, 2], U32))
    most = ctx.enter_context(nc.sbuf_tensor("most", [P, 1], I32))
    x_old = nc.dram_tensor("x_old", [SEQ, D_MODEL], F32, kind="Internal").ap()
    x_mid = nc.dram_tensor("x_mid", [SEQ, D_MODEL], F32, kind="Internal").ap()
    y_moe = nc.dram_tensor("y_moe", [2 * SEQ, D_MODEL], F32, kind="Internal").ap()

    class Area:
        def __init__(self, start, end):
            self.at, self.end = start, end

        def take(self, *dims):
            n = int(np.prod(dims))
            v = sb[:, self.at:self.at + n]
            self.at += n
            assert self.at <= self.end, (self.at, self.end)
            if len(dims) > 1:
                names = "abcd"[:len(dims)]
                spec = " ".join(names)
                v = v.rearrange(f"p ({spec}) -> p {spec}", **dict(zip(names, dims)))
            return v

    kept = Area(0, 53100)
    cst = kept.take(CONST_COLS)

    def const(name):
        return cst[:, CONST_AT[name]:CONST_AT[name] + CONST_W[name]]

    ident, ones = const("ident"), const("ones")
    xT = kept.take(KD, SEQ)
    uT = kept.take(4, SEQ)
    yT = kept.take(4, SEQ)
    x_at = kept.at
    x_tok = kept.take(TT, D_MODEL)
    oT = Area(x_at, x_at + 4096)
    oaT, obT = oT.take(4, SEQ), oT.take(4, SEQ)
    cc_a, ss_a = kept.take(TT, 2, 16), kept.take(TT, 2, 16)
    cc_b, ss_b = kept.take(TT, 8), kept.take(TT, 8)
    router_w = kept.take(KD, EXPERTS)
    router_b = kept.take(EXPERTS)
    lyr = kept.take(2)
    small = kept.take(64)
    lam = small[:, 0:4]
    rope_pos = kept.take(TT)
    half_pi = kept.take(1)
    base = kept.at

    a1 = Area(base, 53100)
    wd = a1.take(2, KD, 3 * P)
    uq, ukv = a1.take(2, HEADS * 96), a1.take(HEADS * 128)
    loraT = a1.take(3, SEQ)
    krope = a1.take(TT, ROPE_A)
    qn_bc, kvn_bc, subln = a1.take(Q_LORA), a1.take(KV_LORA), a1.take(2 * HD)
    lam_in = a1.take(4, HD)
    a_re, a_im, dt_, inv_a = (a1.take(STILES) for _ in range(4))
    radius, phi = a1.take(STILES), a1.take(STILES)
    bbar = a1.take(2, STILES, GROUP)
    c_nat = a1.take(2, 4, STATES)
    d_col = a1.take(4)
    fine, coarse = a1.take(2, STILES, FINE), a1.take(2, STILES, COARSE)
    ms_b = a1.take(TT, HEADS)
    ob_tok = a1.take(TT, HEADS, 2 * HD)
    heads_at = a1.at
    rope = Area(base, 53100)
    rope_ang, rope_sc = rope.take(2, TT, 20), rope.take(2, TT, 20)
    a2 = Area(heads_at, 53100)
    w_ssm, w_mla = a2.take(KD, SSM_W), a2.take(KD, MLA_COLS)
    lora = a2.take(TT, Q_LORA + KV_LORA)
    b_in = a2.take(2, STILES, GROUP)
    sqs, ssum, rrt = a2.take(P * 2), a2.take(TT, 2), a2.take(TT, 2)
    rtmp = a2.take(3, TT, 32)
    sm = a2.take(16, STILES)
    ang = a2.take(3, STILES * FINE)
    angc = a2.take(3, STILES * COARSE)
    btmp = a2.take(2, STILES, GROUP)
    a3 = Area(heads_at, 53100)
    q_h, k_h, v_h = a3.take(TT, 96), a3.take(TT, 96), a3.take(TT, 64)
    qT, kT = a3.take(SEQ), a3.take(SEQ)
    d_h = a3.take(TT, 3 * 64)
    dqT, dkT = a3.take(SEQ), a3.take(SEQ)
    p1, p2, pT = a3.take(TT, SEQ), a3.take(TT, SEQ), a3.take(TT, SEQ)
    oa_tok = a3.take(TT, P)
    tmp_h = a3.take(4, TT * 32)
    tmp_o = a3.take(TT, 64)
    soft = a3.take(12, TT)
    pads = Area(x_at + 2048, x_at + 4096).take(4, 512)
    bT, cT = a3.take(2, 512), a3.take(2, 4, 32)
    rot = a3.take(2, 2, SEQ)
    rtm = a3.take(2, SEQ)
    bu = a3.take(2, 2, SEQ)
    xab, xrot = a3.take(2, SEQ), a3.take(2, SEQ)
    gsc = a3.take(2, SEQ)
    hst = a3.take(2, 2, SEQ)
    a4 = Area(base, 53100)
    merged = a4.take(TT, D_MODEL)
    w_o = a4.take(KD, D_MODEL)
    m_at = a4.at
    wg = [a4.take(KD, BANK) for _ in range(3)]
    wy = [a4.take(4, BANK) for _ in range(4)]
    sg = a4.take(4, BANK)
    mtmp = a4.take(BANK)
    bias_g = Area(x_at - 4096, x_at).take(3, BANK)
    a5 = Area(m_at, 53100)
    ln_g, ln_b = a5.take(D_MODEL), a5.take(D_MODEL)
    ln_st = a5.take(TT, 16)
    a6 = Area(base, 53100)
    e_gate = [a6.take(KD, FF) for _ in range(2)]
    e_up = [a6.take(KD, FF) for _ in range(2)]
    e_down = [a6.take(KF, D_MODEL) for _ in range(2)]
    xgT = [a6.take(KD, P) for _ in range(2)]
    h_e = [a6.take(FF) for _ in range(2)]
    hT = [a6.take(KF, P) for _ in range(2)]
    yb = [a6.take(D_MODEL) for _ in range(2)]
    xg = [a6.take(D_MODEL) for _ in range(2)]
    sel = [a6.take(TT, P) for _ in range(2)]
    a7 = Area(x_at - 4096, x_at)
    EP = EXPERTS + 1
    sc, bs, rt = a7.take(TT, EXPERTS), a7.take(TT, EXPERTS), a7.take(6, TT * EXPERTS)
    oh1, oh2, chosen = a7.take(TT, EXPERTS), a7.take(TT, EXPERTS), a7.take(TT, EXPERTS)
    slot_of, payload = a7.take(TT, EP), a7.take(TT, EP, 2)
    slots_now = a7.take(P)
    w_tok = a7.take(2, TT)
    rs = a7.take(8, TT)
    silu = a7.take(BANK)
    a8 = Area(base, 53100)
    y_in = a8.take(TT, 2 * D_MODEL)
    ln2_g, ln2_b = a8.take(D_MODEL), a8.take(D_MODEL)
    ln2_st = a8.take(TT, 16)

    sems = {}

    def sem(name):
        sems[name] = ctx.enter_context(nc.semaphore(name))
        return sems[name]

    setup_in = sem("setup_in")
    setup_ang = sem("setup_ang")
    setup_trig = sem("setup_trig")
    setup_zero = sem("setup_zero")
    layer_first = sem("layer_first").num
    full = [sem(f"full{b}") for b in range(8)]
    free = [sem(f"free{b}") for b in range(8)]
    L = {n: sem(n) for n in RAISED if n[0:4] not in ("full", "free") and not (n[0] == "b" and n[1:].isdigit())}
    small_in, wssm_in, wmla_in, wuq_in = sem("small_in"), sem("wssm_in"), sem("wmla_in"), sem("wuq_in")
    wd_in = [sem(f"wd_in{i}") for i in range(2)]
    x_saved, wo_in, x_back, ln_in, ln2_in, y_in_s = (sem(n) for n in ("x_saved", "wo_in", "x_back", "ln_in", "ln2_in", "y_in_s"))
    wg_in = [sem(f"wg_in{i}") for i in range(3)]
    wy_in = [sem(f"wy_in{i}") for i in range(4)]
    bg_in = sem("bg_in")
    dt_ready, lam_ready, lam_exp, ang_ready, trig_ready, inv_ready, coef_ready = (
        sem(n) for n in ("dt_ready", "lam_ready", "lam_exp", "ang_ready", "trig_ready", "inv_ready", "coef_ready"))
    krope_ready, subln_ready = sem("krope_ready"), sem("subln_ready")
    score_ready, pick_ready, slots_ready, xmid_ready = (sem(n) for n in ("score_ready", "pick_ready", "slots_ready", "xmid_ready"))
    layer_last = sem("layer_last").num
    pass_first = sem("pass_first").num
    efull = [sem(f"efull{b}") for b in range(8)]
    efree = [sem(f"efree{b}") for b in range(8)]
    sel_ready, he_ready, silu_ready = sem("sel_ready"), sem("he_ready"), sem("silu_ready")
    eg_in, eu_in, ed_in = ([sem(f"{n}_in{i}") for i in range(2)] for n in ("eg", "eu", "ed"))
    pass_last = sem("pass_last").num
    gathered = [sem(f"gathered{i}") for i in range(2)]
    scattered = [sem(f"scattered{i}") for i in range(2)]
    arr = {n: sem(f"arrive_{n}") for n in ("layer", "moe", "pass", "passed", "end")}
    go = {n: sem(f"go_{n}") for n in ("layer", "moe", "pass", "passed", "end")}
    tick = sem("tick")
    chains = {n: sem(f"chain_{n}") for n in ("pe", "act", "dve", "pool")}
    out_done = sem("out_done")

    def meet(eng, name):
        eng.drain().then_inc(arr[name], 1)
        eng.wait_ge(go[name], 1)
        eng.sem_inc(tick, 1)

    def host(sp, name, clears, start=True):
        sp.wait_ge(arr[name], 4)
        sp.sem_clear(arr[name])
        for r in clears:
            sp.sem_clear(r)
        if start:
            sp.sem_inc(go[name], 1)

    def claim(pe, b, phase, u, step=0):
        v = at(f"free{b}", phase, u, step)
        if not (isinstance(v, int) and v == 0):
            pe.wait_ge(free[b], v)

    def filled(eng, b, phase, u, step=0):
        eng.wait_ge(full[b], at(f"full{b}", phase, u + 1, step))

    def emptied(eng, b, phase, u, step=0):
        eng.wait_ge(free[b], at(f"free{b}", phase, u + 1, step))

    x_d, w_in = t_in["x"], t_in["w_in"]
    tok3 = lambda d: d.rearrange("(t p) d -> p t d", p=P)
    rows = lambda d: d.rearrange("(k p) n -> p k n", p=P)
    bcast = lambda d: d.partition_broadcast(P)
    S3 = lambda v, *shape: v.to_broadcast(list(shape))

    ctx.enter_context(nc.allow_non_contiguous_dma(reason="small parameters, a number for each partition"))
    block = ctx.enter_context(nc.Block())

    @block.sync
    def _(sp):
        sp.dma_start(cst, consts).then_inc(setup_in, 16)
        sp.dma_start(x_tok, tok3(x_d[0])).then_inc(setup_in, 16)
        sp.dma_start(pos_i[:], t_in["positions"].rearrange("a (t p) -> p (a t)", p=P)).then_inc(setup_in, 16)
        sp.dma_start(router_w, rows(t_in["router_w"])).then_inc(setup_in, 16)
        sp.dma_start(router_b, bcast(t_in["router_bias"])).then_inc(setup_in, 16)
        sp.wait_ge(setup_in, 80)
        with sp.Fori(0, DEPTH) as l:
            host(sp, "layer", [range(layer_first, layer_last + 1), go["moe"], go["end"]])
            wl = w_in[l]
            loads = [
                (lyr, layer_consts[l]), (qn_bc, bcast(t_in["mla_q_norm"][l])), (kvn_bc, bcast(t_in["mla_kv_norm"][l])),
                (subln, bcast(t_in["diff_subln"][l])),
                (lam_in, bcast(t_in["diff_lambda"][l].rearrange("a b -> (a b)")).rearrange("p (a b) -> p a b", a=4)),
                (a_re, t_in["ssm_a_re"][l].rearrange("(t h) n -> (h n) t", h=2)),
                (a_im, t_in["ssm_a_im"][l].rearrange("(t h) n -> (h n) t", h=2)),
                (b_in[:, 0], t_in["ssm_b_re"][l].rearrange("(t h) n q -> (h n) t q", h=2)),
                (b_in[:, 1], t_in["ssm_b_im"][l].rearrange("(t h) n q -> (h n) t q", h=2)),
                (c_nat[:, 0], t_in["ssm_c_re"][l].rearrange("(c g) q n -> (g q) c n", g=8)),
                (c_nat[:, 1], t_in["ssm_c_im"][l].rearrange("(c g) q n -> (g q) c n", g=8)),
                (d_col, t_in["ssm_d"][l].rearrange("(c p) -> p c", p=P)),
            ]
            for h in range(2):
                dt_src = t_in["ssm_log_dt"][l].rearrange("(t h) -> h t", h=2)[h]
                loads.append((dt_[h * 64:h * 64 + 64, :], dt_src.partition_broadcast(64)))
            assert len(loads) == 14
            sp.dma_start(w_ssm, rows(wl[:, OFF_SSM:OFF_SSM + SSM_W])).then_inc(wssm_in, 16)
            for dst, src in loads:
                sp.dma_start(dst, src).then_inc(small_in, 16)
            sp.dma_start(w_mla, rows(wl[:, 0:MLA_COLS])).then_inc(wmla_in, 16)
            sp.dma_start(uq, rows(t_in["mla_w_uq"][l])).then_inc(wuq_in, 16)
            sp.dma_start(ukv, t_in["mla_w_ukv"][l]).then_inc(wuq_in, 16)
            sp.dma_start(tok3(x_old), x_tok).then_inc(x_saved, 16)
            diff_w = wl[:, OFF_DIFF:OFF_SSM].rearrange("(k p) (s c n) -> c s p k n", p=P, s=3, n=P)
            for c in range(4):
                srcs = [diff_w[c, s] for s in range(3)]
                if c >= 2:
                    sp.wait_ge(wd_in[c % 2], 48)
                    sp.sem_inc(L["wd_ready"], 1)
                    filled(sp, 4, "heads", 8, c - 2)
                for s in range(3):
                    sp.dma_start(wd[:, c % 2, :, s * P:(s + 1) * P], srcs[s]).then_inc(wd_in[c % 2], 16)
            for c in (2, 3):
                sp.wait_ge(wd_in[c % 2], 96)
                sp.sem_inc(L["wd_ready"], 1)
            sp.wait_ge(L["gelu_done"], at("gelu_done", "join", 1))
            for b in range(4):
                emptied(sp, b, "join", 0)
            for n in range(2):
                half = slice(n * BANK, (n + 1) * BANK)
                for i in range(3):
                    if n:
                        filled(sp, 1, "merge", 2 * i + 1, 0)
                        filled(sp, 3, "merge", 2 * i + 1, 0)
                    col = OFF_GATE + i * D_MODEL + n * BANK
                    sp.dma_start(wg[i], rows(wl[:, col:col + BANK])).then_inc(wg_in[i], 16)
                    sp.dma_start(bias_g[0:1, i, :], t_in["b_gate"][l][i:i + 1, half]).then_inc(bg_in, 16)
                    w2 = [rows(t_in["mla_w_out"][l]), rows(t_in["diff_w_out"][l]), rows(t_in["ssm_w_glu"][l])][i]
                    sp.dma_start(wy[i], w2[:, :, half]).then_inc(wy_in[i], 16)
                    if i == 2:
                        if n:
                            filled(sp, 5, "merge", 1, 0)
                        sp.dma_start(wy[3], w2[:, :, D_MODEL + n * BANK:D_MODEL + (n + 1) * BANK]).then_inc(wy_in[3], 16)
                if n == 0:
                    sp.dma_start(w_o, rows(t_in["w_o"][l])).then_inc(wo_in, 16)
            filled(sp, 3, "merge", 5, 1)
            sp.wait_ge(x_saved, 16)
            sp.dma_start(x_tok, tok3(x_old)).then_inc(x_back, 16)
            filled(sp, 5, "merge", 1, 1)
            sp.wait_ge(L["merged_ready"], at("merged_ready", "merge", 12, 1))
            sp.dma_start(ln_g, bcast(t_in["ln_gain"][l][0])).then_inc(ln_in, 16)
            sp.dma_start(ln_b, bcast(t_in["ln_bias"][l][0])).then_inc(ln_in, 16)
            sp.wait_ge(L["ln_ready"], at("ln_ready", "tail", 4))
            sp.dma_start(tok3(x_mid), x_tok).then_inc(xmid_ready, 16)
            sp.wait_ge(xmid_ready, 16)
            host(sp, "moe", [go["layer"]])
            most_chosen = sp.value_load(most[0:1, 0:1], min_val=0, max_val=SEQ)
            with sp.Fori(0, PASSES) as ps:
                with sp.If(most_chosen > ps * P):
                    host(sp, "pass", [range(pass_first, pass_last + 1), go["passed"]], start=False)
                    for b in range(8):
                        sp.sem_inc(efree[b], 1)
                    sp.sem_inc(go["pass"], 1)

                    def expert_loads(e2, first):
                        for par in range(2):
                            e = e2 + par
                            g_src, u_src, d_src = (t_in[n][l][e] for n in ("moe_w_gate", "moe_w_up", "moe_w_down"))
                            g_ap, u_ap, d_ap = rows(g_src), rows(u_src), rows(d_src)
                            if not first:
                                sp.wait_ge(efull[4], e2 + par - 1)
                            sp.dma_start(e_gate[par], g_ap).then_inc(eg_in[par], 16)
                            sp.dma_start(e_up[par], u_ap).then_inc(eu_in[par], 16)
                            if not first:
                                sp.wait_ge(efull[7], e2 + par - 1)
                            sp.dma_start(e_down[par], d_ap).then_inc(ed_in[par], 16)

                    expert_loads(0, True)
                    with sp.Fori(1, EXPERTS // 2) as pair:
                        e2 = pair * 2
                        expert_loads(e2, False)
                    host(sp, "passed", [go["pass"]])
                sp.sem_inc(tick, 1)
            for t in range(TT):
                sp.dma_start(y_in[:, t, :], y_moe.rearrange("(t p k) d -> t p (k d)", p=P, k=2)[t]).then_inc(y_in_s, 16)
            sp.dma_start(ln2_g, bcast(t_in["ln_gain"][l][1])).then_inc(ln2_in, 16)
            sp.dma_start(ln2_b, bcast(t_in["ln_bias"][l][1])).then_inc(ln2_in, 16)
            host(sp, "end", [])
        sp.dma_start(tok3(out[0]), x_tok).then_inc(out_done, 16)
        sp.wait_ge(out_done, 16)

    @block.tensor
    def _(pe):
        ch = Chain(pe, chains["pe"])
        pe.wait_ge(setup_in, 80)
        with pe.Fori(0, DEPTH) as l:
            meet(pe, "layer")

            def transpose_x(phase, u):
                for k in range(KD):
                    claim(pe, k, phase, u)
                    for t in range(TT):
                        mm = pe.transpose(psum[:, k, t * P:(t + 1) * P], x_tok[:, t, k * P:(k + 1) * P], ident)
                    mm.then_inc(full[k], 1)

            transpose_x("front", 0)
            pe.wait_ge(wssm_in, 16)
            for c in range(4):
                if c == 0:
                    for k in range(KD):
                        emptied(pe, k, "front", 0)
                for k in range(KD):
                    mm = pe.matmul(psum[:, c, :], w_ssm[:, k, c * P:(c + 1) * P], xT[:, k, :], start=(k == 0), stop=(k == KD - 1))
                mm.then_inc(full[c], 1)
            pe.wait_ge(wmla_in, 16)
            for t in range(TT):
                for k in range(KD):
                    mm = pe.matmul(psum[:, 4 + t, 0:MLA_COLS], xT[:, k, t * P:(t + 1) * P], w_mla[:, k, :], start=(k == 0), stop=(k == KD - 1))
                mm.then_inc(full[4 + t], 1)
            pe.wait_ge(L["lora_ready"], 1)
            for j in range(3):
                claim(pe, j, "front", 2)
                for t in range(TT):
                    mm = pe.transpose(psum[:, j, t * P:(t + 1) * P], lora[:, t, j * P:(j + 1) * P], ident)
                mm.then_inc(full[j], 1)
            for j in range(3):
                emptied(pe, j, "front", 2)
            pe.wait_ge(wuq_in, 32)

            with pe.Fori(0, 4) as c:
                par_w = c % 2
                pe.wait_ge(L["pads_ready"], at("pads_ready", "heads", 1, c))
                for i in range(4):
                    claim(pe, 6, "heads", i, c)
                    for j in range(4):
                        mm = pe.transpose(psum[:, 6, j * P:(j + 1) * P], pads[:, i, j * P:(j + 1) * P], ident)
                    mm.then_inc(full[6], 1)
                for hh in range(2):
                    h = 2 * c + hh
                    u4, u5, u6, us = 7 * hh, 7 * hh, 4 + 8 * hh, 3 * hh
                    claim(pe, 4, "heads", u4, c)
                    for t in range(TT):
                        for k in range(2):
                            mm = pe.matmul(psum[:, 4, t * 96:(t + 1) * 96], loraT[:, k, t * P:(t + 1) * P],
                                           uq[:, k, bass.ds(h * 96, 96)], start=(k == 0), stop=(k == 1))
                    mm.then_inc(full[4], 1)
                    claim(pe, 5, "heads", u5, c)
                    for t in range(TT):
                        mm = pe.matmul(psum[:, 5, t * P:(t + 1) * P], loraT[:, 2, t * P:(t + 1) * P],
                                       ukv[:, bass.ds(h * P, P)], start=True, stop=True)
                    mm.then_inc(full[5], 1)
                    if hh == 0:
                        pe.wait_ge(L["wd_ready"], at("wd_ready", "heads", 1, c))
                    for i, b in enumerate((6, 4)):
                        claim(pe, b, "heads", (u6, u4 + 1)[i], c)
                        for t in (2 * i, 2 * i + 1):
                            for k in range(KD):
                                wv = wd[:, bass.ds(par_w, 1), k, :].rearrange("p a (s n) -> p (a s) n", s=3)[:, :, hh * 64:hh * 64 + 64]
                                mm = pe.matmul(psum[:, b, (t % 2) * 192:(t % 2) * 192 + 192].rearrange("p (s n) -> p s n", s=3),
                                               xT[:, k, t * P:(t + 1) * P], wv, start=(k == 0), stop=(k == KD - 1))
                        mm.then_inc(full[b], 1)
                    pe.wait_ge(L["q_ready"], at("q_ready", "heads", hh + 1, c))
                    claim(pe, 5, "heads", u5 + 1, c)
                    for t in range(TT):
                        mm = pe.transpose(psum[0:96, 5, t * P:(t + 1) * P], q_h[:, t, :], ident)
                    mm.then_inc(full[5], 1)
                    pe.wait_ge(L["kv_ready"], at("kv_ready", "heads", hh + 1, c))
                    claim(pe, 6, "heads", u6 + 1, c)
                    for t in range(TT):
                        mm = pe.transpose(psum[0:96, 6, t * P:(t + 1) * P], k_h[:, t, :], ident)
                    mm.then_inc(full[6], 1)

                    def scores(q, k, u):
                        for t in range(TT):
                            claim(pe, t, "heads", us + u, c)
                            pe.matmul(psum[:, t, 0:(t + 1) * P], q[:, t * P:(t + 1) * P], k[:, 0:(t + 1) * P],
                                      start=True, stop=True).then_inc(full[t], 1)

                    def attend(p, v, first4, first5, last6, ready):
                        for t in range(TT):
                            b, u = (4, first4 + t // 2) if t % 2 == 0 else (5, first5 + t // 2)
                            ready(t)
                            claim(pe, b, "heads", u, c)
                            for kb in range(t + 1):
                                mm = pe.transpose(psum[:, b, kb * P:(kb + 1) * P], p[:, t, kb * P:(kb + 1) * P], ident)
                            mm.then_inc(full[b], 1)
                        claim(pe, 6, "heads", last6, c)
                        for t in range(TT):
                            b, u = (4, first4 + t // 2) if t % 2 == 0 else (5, first5 + t // 2)
                            emptied(pe, b, "heads", u, c)
                            for kb in range(t + 1):
                                mm = pe.matmul(psum[:, 6, t * 64:(t + 1) * 64], pT[:, t, kb * P:(kb + 1) * P], v(kb),
                                               start=(kb == 0), stop=(kb == t))
                        mm.then_inc(full[6], 1)

                    emptied(pe, 5, "heads", u5 + 1, c)
                    emptied(pe, 6, "heads", u6 + 1, c)
                    scores(qT[0:96, :], kT[0:96, :], 0)
                    pe.wait_ge(L["diff_ready"], at("diff_ready", "heads", hh + 1, c))
                    for i, b, u in ((0, 4, u4 + 2), (1, 5, u5 + 2)):
                        claim(pe, b, "heads", u, c)
                        pe.sem_inc(tick, 1)
                        for t in range(TT):
                            mm = pe.transpose(psum[0:64, b, t * P:(t + 1) * P], d_h[:, t, i * 64:(i + 1) * 64], ident)
                        mm.then_inc(full[b], 1)
                    for j in range(2):
                        for i in range(2):
                            claim(pe, 6, "heads", u6 + 2 + 2 * j + i, c)
                            if hh == 0 and j == 0 and i == 0:
                                emptied(pe, 6, "heads", 3, c)
                            tile = 2 * hh + j
                            pe.matmul(psum[:, 6, :], bT[:, i, tile * P:(tile + 1) * P], uT[:, bass.ds(c, 1), :].rearrange("p a n -> p (a n)"),
                                      start=True, stop=True).then_inc(full[6], 1)
                    attend(p1, lambda kb: v_h[:, kb, :], u4 + 3, u5 + 3, u6 + 6,
                           lambda t: emptied(pe, t, "heads", us, c))
                    emptied(pe, 4, "heads", u4 + 2, c)
                    emptied(pe, 5, "heads", u5 + 2, c)
                    scores(dqT[0:32, :], dkT[0:32, :], 1)
                    scores(dqT[32:64, :], dkT[32:64, :], 2)

                    def c_products(j):
                        tile = 2 * hh + j
                        pe.wait_ge(L["h_ready"], at("h_ready", "heads", tile + 1, c))
                        if tile == 0:
                            claim(pe, 7, "heads", 0, c)
                        for i in range(2):
                            mm = pe.matmul(psum[32 * tile:32 * tile + 32, 7, :], cT[:, i, tile, :], hst[:, tile % 2, i, :],
                                           start=(i == 0), stop=(i == 1))
                        mm.then_inc(L["h_used"], 1)

                    c_products(0)
                    attend(p1, lambda kb: d_h[:, kb, 128:192], u4 + 5, u5 + 5, u6 + 7,
                           lambda t: pe.wait_ge(L["mix_ready"], at("mix_ready", "heads", 4 * hh + t + 1, c)))
                    c_products(1)
                pe.wait_ge(L["oa_ready"], at("oa_ready", "heads", 2, c))
                claim(pe, 4, "heads", 14, c)
                for t in range(TT):
                    mm = pe.transpose(psum[:, 4, t * P:(t + 1) * P], oa_tok[:, t, :], ident)
                mm.then_inc(full[4], 1)

            for i in range(4):
                claim(pe, i, "join", 0)
                for t in range(TT):
                    pe.wait_ge(L["ob_ready"], at("ob_ready", "join", t + 1))
                    mm = pe.transpose(psum[:, i, t * P:(t + 1) * P], ob_tok[:, t, 2 * i:2 * i + 2, :].rearrange("p a b -> p (a b)"), ident)
                mm.then_inc(full[i], 1)
            for i in range(4):
                emptied(pe, i, "join", 0)
            emptied(pe, 4, "heads", 14, 3)
            pe.wait_ge(L["gelu_done"], at("gelu_done", "join", 1))

            with pe.Fori(0, 2) as n:
                pe.wait_ge(bg_in, n * 48 + 48)
                for i in range(3):
                    pe.wait_ge(wg_in[i], n * 16 + 16)
                    pe.wait_ge(wy_in[i], n * 16 + 16)
                    if i == 2:
                        pe.wait_ge(wy_in[3], n * 16 + 16)
                    for t in range(TT):
                        tok = slice(t * P, (t + 1) * P)
                        b, u = t % 2, 2 * i + t // 2
                        claim(pe, b, "merge", u, n)
                        for k in range(KD):
                            pe.matmul(psum[:, b, :], xT[:, k, tok], wg[i][:, k, :], start=(k == 0), stop=False)
                        pe.matmul(psum[:, b, :], ones[0:1, :], bias_g[0:1, i, :], start=False, stop=True).then_inc(full[b], 1)
                        src = (oaT, obT, yT)[i]
                        if i == 2:
                            claim(pe, 4 + b, "merge", t // 2, n)
                            for k in range(4):
                                mm = pe.matmul(psum[:, 4 + b, :], src[:, k, tok], wy[3][:, k, :], start=(k == 0), stop=(k == 3))
                            mm.then_inc(full[4 + b], 1)
                        claim(pe, 2 + b, "merge", u, n)
                        for k in range(4):
                            mm = pe.matmul(psum[:, 2 + b, :], src[:, k, tok], wy[i][:, k, :], start=(k == 0), stop=(k == 3))
                        mm.then_inc(full[2 + b], 1)

            for k in range(KD):
                claim(pe, k, "tail", 0)
                for t in range(TT):
                    pe.wait_ge(L["merged_ready"], at("merged_ready", "merge", 9 + t, 1))
                    mm = pe.transpose(psum[:, k, t * P:(t + 1) * P], merged[:, t, k * P:(k + 1) * P], ident)
                mm.then_inc(full[k], 1)
            for k in range(KD):
                emptied(pe, k, "tail", 0)
            pe.wait_ge(wo_in, 16)
            for t in range(TT):
                for n in range(2):
                    b = 2 * t + n
                    for k in range(KD):
                        mm = pe.matmul(psum[:, b, :], xT[:, k, t * P:(t + 1) * P], w_o[:, k, n * BANK:(n + 1) * BANK], start=(k == 0), stop=(k == KD - 1))
                    mm.then_inc(full[b], 1)
            for k in range(KD):
                claim(pe, k, "tail", 2)
                for t in range(TT):
                    pe.wait_ge(L["ln_ready"], at("ln_ready", "tail", t + 1))
                    mm = pe.transpose(psum[:, k, t * P:(t + 1) * P], x_tok[:, t, k * P:(k + 1) * P], ident)
                mm.then_inc(full[k], 1)
            for k in range(KD):
                emptied(pe, k, "tail", 2)
            for t in range(TT):
                for k in range(KD):
                    mm = pe.matmul(psum[:, 0, t * EXPERTS:(t + 1) * EXPERTS], xT[:, k, t * P:(t + 1) * P], router_w[:, k, :], start=(k == 0), stop=(k == KD - 1))
            mm.then_inc(full[0], 1)
            pe.wait_ge(pick_ready, 1)
            for t in range(TT + 1):
                for s in range(min(t, TT - 1) + 1):
                    lhs = const("upper") if s == t else ones
                    mm = pe.matmul(psum[:, 1, t * EXPERTS:(t + 1) * EXPERTS], lhs, chosen[:, s, :], start=(s == 0), stop=(s == min(t, TT - 1)))
            mm.then_inc(full[1], 1)
            meet(pe, "moe")
            most_chosen = pe.value_load(most[0:1, 0:1], min_val=0, max_val=SEQ)
            with pe.Fori(0, PASSES) as ps:
                with pe.If(most_chosen > ps * P):
                    meet(pe, "pass")

                    def indices(e, par):
                        pe.wait_ge(sel_ready, e + 1)
                        pe.wait_ge(efree[0], e + 1)
                        for t in range(TT):
                            mm = pe.matmul(psum[:, 0, 0:2], sel[par][:, t, :], payload[:, t, bass.ds(e, 1), :].rearrange("p a b -> p (a b)"), start=(t == 0), stop=(t == TT - 1))
                        mm.then_inc(efull[0], 1)

                    def turn_x(e, par, landings):
                        pe.wait_ge(gathered[par], landings)
                        for i in range(2):
                            pe.wait_ge(efree[1 + i], e + 1)
                            for j in range(4):
                                k = 4 * i + j
                                mm = pe.transpose(psum[:, 1 + i, j * P:(j + 1) * P], xg[par][:, k * P:(k + 1) * P], ident)
                            mm.then_inc(efull[1 + i], 1)

                    indices(0, 0)
                    turn_x(0, 0, 16)
                    with pe.Fori(0, EXPERTS // 2) as pair:
                        e2 = pair * 2
                        for par in range(2):
                            e = e2 + par
                            indices(e + 1, 1 - par)
                            for i, (w, landed) in enumerate(((e_gate, eg_in), (e_up, eu_in))):
                                pe.wait_ge(landed[par], e2 * 8 + 16)
                                if i == 0:
                                    pe.wait_ge(efree[1], e + 2)
                                    pe.wait_ge(efree[2], e + 2)
                                pe.wait_ge(efree[3 + i], e + 1)
                                for k in range(KD):
                                    mm = pe.matmul(psum[:, 3 + i, :], xgT[par][:, k, :], w[par][:, k, :], start=(k == 0), stop=(k == KD - 1))
                                mm.then_inc(efull[3 + i], 1)
                            turn_x(e + 1, 1 - par, e2 * 8 + 16 + 16 * par)
                            pe.wait_ge(he_ready, e + 1)
                            pe.wait_ge(efree[5], e + 1)
                            for j in range(KF):
                                mm = pe.transpose(psum[:, 5, j * P:(j + 1) * P], h_e[par][:, j * P:(j + 1) * P], ident)
                            mm.then_inc(efull[5], 1)
                            pe.wait_ge(ed_in[par], e2 * 8 + 16)
                            pe.wait_ge(efree[5], e + 2)
                            for n in range(2):
                                pe.wait_ge(efree[6 + n], e + 1)
                                for j in range(KF):
                                    mm = pe.matmul(psum[:, 6 + n, :], hT[par][:, j, :], e_down[par][:, j, n * BANK:(n + 1) * BANK], start=(j == 0), stop=(j == KF - 1))
                                mm.then_inc(efull[6 + n], 1)
                    meet(pe, "passed")
                pe.sem_inc(tick, 1)
            meet(pe, "end")

    @block.scalar
    def _(act):
        ch = Chain(act, chains["act"])
        copy = lambda o, i: act.copy(o, i)
        act.wait_ge(setup_ang, 1)
        act.activation(rope_sc[:, 1], rope_ang[:, 0], ACT.Sin).then_inc(setup_trig, 1)
        act.activation(rope_sc[:, 0], rope_ang[:, 1], ACT.Sin, bias=half_pi, scale=-1.0).then_inc(setup_trig, 1)
        with act.Fori(0, DEPTH) as l:
            meet(act, "layer")
            ch.reset()
            for k in range(0, KD, 2):
                filled(act, k, "front", 0)
                copy(xT[:, k, :], psum[:, k, :]).then_inc(free[k], 1)
            act.wait_ge(small_in, 224)
            act.activation(dt_, dt_, ACT.Exp).then_inc(dt_ready, 1)
            act.wait_ge(lam_ready, 1)
            act.activation(lam[:, 0:2], lam[:, 2:4], ACT.Exp).then_inc(lam_exp, 1)
            for c in range(4):
                filled(act, c, "front", 1)
                copy(uT[:, c, :], psum[:, c, :]).then_inc(free[c], 1)
            for t in range(TT):
                filled(act, 4 + t, "front", 1)
                for i, (a, b) in enumerate(((0, Q_LORA), (Q_LORA, Q_LORA + KV_LORA))):
                    ch.then(act.activation(sqs[:, 0:b - a], psum[:, 4 + t, a:b], ACT.Square, accum_out=ssum[:, t, i:i + 1]))
            act.sem_inc(tick, 1)
            act.drain().then_inc(L["sq_sums"], 1)
            act.wait_ge(L["rms_mean"], 1)
            act.activation(rrt, rrt, ACT.Sqrt).then_inc(L["rms_root"], 1)
            act.wait_ge(ang_ready, 1)
            for an, tab in ((ang, fine), (angc, coarse)):
                flat = tab.rearrange("p s a b -> p s (a b)")
                ch.add(act.activation(an[:, 1], an[:, 0], ACT.Abs))
                ch.wait()
                ch.add(act.activation(flat[:, 1], an[:, 0], ACT.Sin, scale=TWO_PI))
                ch.add(act.activation(flat[:, 0], an[:, 1], ACT.Sin, bias=half_pi, scale=-TWO_PI))
            act.drain().then_inc(trig_ready, 1)
            for j in range(3):
                filled(act, j, "front", 2)
                copy(loraT[:, j, :], psum[:, j, :]).then_inc(free[j], 1)

            with act.Fori(0, 4) as c:
                ch.reset()
                for i in range(2):
                    filled(act, 6, "heads", i, c)
                    copy(bT[:, i, :], psum[:, 6, :]).then_inc(free[6], 1)
                for i in range(2):
                    filled(act, 6, "heads", 2 + i, c)
                    for j in range(4):
                        ins = copy(cT[:, i, j, :], psum[:, 6, j * 160:j * 160 + 32])
                        if j < 3:
                            ch.add(ins)
                    ins.then_inc(free[6], 1)
                for hh in range(2):
                    u4, u5, u6, us = 7 * hh, 7 * hh, 4 + 8 * hh, 3 * hh
                    filled(act, 5, "heads", u5, c)
                    kv = psum[:, 5, :].rearrange("p (t n) -> p t n", t=TT)
                    if hh == 0:
                        act.wait_ge(krope_ready, 1)
                    ch.add(copy(k_h[:, :, 0:NOPE], kv[:, :, 0:NOPE]))
                    ch.add(copy(k_h[:, :, NOPE:96], krope))
                    copy(v_h, kv[:, :, NOPE:P]).then_inc(free[5], 1)
                    act.drain().then_inc(L["kv_ready"], 1)
                    for i, b in enumerate((6, 4)):
                        filled(act, b, "heads", (u6, u4 + 1)[i], c)
                        copy(d_h[:, 2 * i:2 * i + 2, :], psum[:, b, 0:384].rearrange("p (t n) -> p t n", t=2)).then_inc(free[b], 1)
                    act.drain().then_inc(L["diff_copied"], 1)
                    filled(act, 5, "heads", u5 + 1, c)
                    copy(qT[0:96, :], psum[0:96, 5, :]).then_inc(free[5], 1)
                    filled(act, 4, "heads", u4 + 2, c)
                    copy(dqT[0:64, :], psum[0:64, 4, :]).then_inc(free[4], 1)

                    def take_bu(j):
                        tile = 2 * hh + j
                        for i in range(2):
                            filled(act, 6, "heads", u6 + 2 + 2 * j + i, c)
                            copy(bu[:, tile % 2, i, :], psum[:, 6, :]).then_inc(free[6], 1)

                    def exps(n, p, scale):
                        act.wait_ge(L["max_ready"], at("max_ready", "heads", us + n + 1, c))
                        for t in range(TT):
                            act.activation(p[:, t, 0:(t + 1) * P], psum[:, t, 0:(t + 1) * P], ACT.Exp, bias=soft[:, n, t:t + 1],
                                           scale=scale, accum_out=soft[:, 3 + n, t:t + 1]).then_inc(free[t], 1)

                    def take_p(b, u, t):
                        filled(act, b, "heads", u, c)
                        copy(pT[:, t, 0:(t + 1) * P], psum[:, b, 0:(t + 1) * P]).then_inc(free[b], 1)

                    take_bu(0)
                    exps(0, p1, SCALE_A)
                    take_bu(1)
                    for t in range(TT):
                        take_p(4 + t % 2, 7 * hh + 3 + t // 2, t)
                    exps(1, p1, SCALE_B)
                    exps(2, p2, SCALE_B)
                    filled(act, 6, "heads", u6 + 6, c)
                    for t in (1, 3):
                        take_p(5, u5 + 5 + t // 2, t)
                filled(act, 4, "heads", 14, c)
                act.wait_ge(x_saved, 16)
                copy(oaT[:, bass.ds(c, 1), :].rearrange("p a n -> p (a n)"), psum[:, 4, :]).then_inc(free[4], 1)

            ch.reset()
            act.wait_ge(L["rms_mean"], at("rms_mean", "join", 1))
            act.activation(ms_b, ms_b, ACT.Sqrt).then_inc(L["rms_root"], 1)
            act.wait_ge(L["y_ready"], at("y_ready", "join", 0))
            act.activation(yT, yT, ACT.Gelu_apprx_tanh).then_inc(L["gelu_done"], 1)

            with act.Fori(0, 2) as n:
                for i in range(3):
                    for t in range(TT):
                        b, u = t % 2, 2 * i + t // 2
                        g = 4 * i + t
                        filled(act, b, "merge", u, n)
                        if g >= 2:
                            act.wait_ge(L["merged_ready"], at("merged_ready", "merge", g - 1, n))
                        act.activation(sg[:, b, :], psum[:, b, :], ACT.Sigmoid).then_inc(free[b], 1)
                        if i == 2:
                            filled(act, 4 + b, "merge", t // 2, n)
                            act.activation(sg[:, 2 + b, :], psum[:, 4 + b, :], ACT.Sigmoid).then_inc(free[4 + b], 1)
                act.wait_ge(L["merged_ready"], at("merged_ready", "merge", 12, n))

            def roots(st, phase):
                for t in range(TT):
                    act.wait_ge(L["ln_var"], at("ln_var", phase, t + 1))
                    act.activation(st[:, t, 14:15], st[:, t, 13:14], ACT.Sqrt).then_inc(L["ln_root"], 1)

            for k in range(0, KD, 2):
                filled(act, k, "tail", 0)
                copy(xT[:, k, :], psum[:, k, :]).then_inc(free[k], 1)
            roots(ln_st, "tail")
            for k in range(0, KD, 2):
                filled(act, k, "tail", 2)
                copy(xT[:, k, :], psum[:, k, :]).then_inc(free[k], 1)
            filled(act, 0, "tail", 3)
            act.activation(sc, psum[:, 0, 0:TT * EXPERTS].rearrange("p (t e) -> p t e", t=TT), ACT.Sigmoid).then_inc(free[0], 1)
            meet(act, "moe")
            most_chosen = act.value_load(most[0:1, 0:1], min_val=0, max_val=SEQ)
            with act.Fori(0, PASSES) as ps:
                with act.If(most_chosen > ps * P):
                    meet(act, "pass")

                    def take_x(e, par):
                        act.wait_ge(efull[1], e + 1)
                        copy(xgT[par][:, 0:4, :].rearrange("p a b -> p (a b)"), psum[:, 1, :]).then_inc(efree[1], 1)

                    take_x(0, 0)
                    with act.Fori(0, EXPERTS // 2) as pair:
                        e2 = pair * 2
                        for par in range(2):
                            e = e2 + par
                            act.wait_ge(efull[3], e + 1)
                            act.wait_ge(efree[4], e + 1)
                            act.activation(silu, psum[:, 3, :], ACT.Silu).then_inc(silu_ready, 1)
                            take_x(e + 1, 1 - par)
                            act.wait_ge(efull[5], e + 1)
                            copy(hT[par].rearrange("p a b -> p (a b)"), psum[:, 5, :]).then_inc(efree[5], 1)
                            act.wait_ge(efull[6], e + 1)
                            act.wait_ge(scattered[par], e2 * 8 + 16)
                            copy(yb[par][:, 0:BANK], psum[:, 6, :]).then_inc(efree[6], 1)
                    meet(act, "passed")
                act.sem_inc(tick, 1)
            roots(ln2_st, "last")
            meet(act, "end")

    @block.vector
    def _(v):
        ch = Chain(v, chains["dve"])
        tt, ts, stt = v.tensor_tensor, v.tensor_scalar, v.scalar_tensor_tensor
        v.wait_ge(setup_in, 80)
        ch.then(v.tensor_copy(rope_pos, pos_i[:]))
        ch.then(tt(rope_ang[:, 0], S3(rope_pos.unsqueeze(2), P, TT, 20), S3(const("inv").unsqueeze(1), P, TT, 20), ALU.mult))
        ch.then(ts(rope_ang[:, 1], rope_ang[:, 0], 1 / TWO_PI, ROUND, ALU.mult, ALU.add))
        ch.then(ts(rope_ang[:, 1], rope_ang[:, 1], -ROUND, None, ALU.add))
        ch.then(stt(out=rope_ang[:, 0], in0=rope_ang[:, 1], scalar=-PI_HI, in1=rope_ang[:, 0], op0=ALU.mult, op1=ALU.add))
        ch.then(stt(out=rope_ang[:, 0], in0=rope_ang[:, 1], scalar=-PI_LO, in1=rope_ang[:, 0], op0=ALU.mult, op1=ALU.add))
        ch.then(ts(rope_ang[:, 0], rope_ang[:, 0], PI_MAX, -PI_MAX, ALU.min, ALU.max))
        ch.then(ts(rope_ang[:, 1], rope_ang[:, 0], -1.0, None, ALU.mult))
        ch.then(tt(rope_ang[:, 1], rope_ang[:, 1], rope_ang[:, 0], ALU.max))
        v.memset(half_pi, math.pi / 2).then_inc(setup_ang, 1)
        v.wait_ge(setup_trig, 2)
        for tab, i in (((cc_a, cc_b), 0), ((ss_a, ss_b), 1)):
            for s in range(2):
                ch.add(v.tensor_copy(tab[0][:, :, s, :], rope_sc[:, i, :, 0:16]))
                ch.add(v.tensor_copy(tab[1][:, :, 4 * s:4 * s + 4], rope_sc[:, i, :, 16:20]))
        for i in range(2):
            ch.add(v.memset(xg[i], 0.0))
        with v.Fori(0, DEPTH) as l:
            meet(v, "layer")
            ch.reset()
            for k in range(1, KD, 2):
                filled(v, k, "front", 0)
                v.tensor_copy(xT[:, k, :], psum[:, k, :]).then_inc(free[k], 1)
            v.wait_ge(small_in, 224)
            ch.then(tt(rtmp[:, 0, 0:2, :], lam_in[:, 0:4:2, :], lam_in[:, 1:4:2, :], ALU.mult))
            v.tensor_reduce(lam[:, 2:4], rtmp[:, 0, 0:2, :], AXX, ALU.add).then_inc(lam_ready, 1)
            ch.add(tt(sm[:, 14], a_re, a_re, ALU.mult))
            ch.then(tt(sm[:, 15], a_im, a_im, ALU.mult))
            ch.then(tt(sm[:, 14], sm[:, 14], sm[:, 15], ALU.add))
            v.reciprocal(inv_a, sm[:, 14]).then_inc(inv_ready, 1)
            ts(subln, subln, lyr[:, 1:2], None, ALU.mult).then_inc(subln_ready, 1)
            v.wait_ge(lam_exp, 1)
            ch.then(tt(lam[:, 2:3], lam[:, 0:1], lam[:, 1:2], ALU.subtract))
            ch.then(tt(lam[:, 0:1], lam[:, 2:3], lyr[:, 0:1], ALU.add))
            v.wait_ge(L["sq_sums"], 1)
            ch.add(ts(rrt[:, :, 0:1], ssum[:, :, 0:1], 1 / Q_LORA, RMS_EPS, ALU.mult, ALU.add))
            ch.then(ts(rrt[:, :, 1:2], ssum[:, :, 1:2], 1 / KV_LORA, RMS_EPS, ALU.mult, ALU.add))
            v.sem_inc(L["rms_mean"], 1)
            v.wait_ge(L["rms_root"], 1)
            ch.then(v.reciprocal(ssum, rrt))
            for t in range(TT):
                ch.add(stt(out=lora[:, t, 0:Q_LORA], in0=psum[:, 4 + t, 0:Q_LORA], scalar=ssum[:, t, 0:1], in1=qn_bc, op0=ALU.mult, op1=ALU.mult))
                ch.add(stt(out=lora[:, t, Q_LORA:384], in0=psum[:, 4 + t, Q_LORA:384], scalar=ssum[:, t, 1:2], in1=kvn_bc, op0=ALU.mult, op1=ALU.mult))
            kr = psum[:, 4:8, 384:416]
            ch.add(tt(rtmp[:, 0], kr, cc_a.rearrange("p t a b -> p t (a b)"), ALU.mult))
            ch.then(tt(rtmp[:, 1], kr, ss_a.rearrange("p t a b -> p t (a b)"), ALU.mult))
            for t in range(TT):
                v.sem_inc(free[4 + t], 1)
            v.sem_inc(L["lora_ready"], 1)
            ch.add(tt(krope[:, :, 0:16], rtmp[:, 0, :, 0:16], rtmp[:, 1, :, 16:32], ALU.subtract))
            ch.then(tt(krope[:, :, 16:32], rtmp[:, 0, :, 16:32], rtmp[:, 1, :, 0:16], ALU.add))
            v.sem_inc(krope_ready, 1)

            with v.Fori(0, 4) as c:
                ch.reset()
                for hh in range(2):
                    u4, u5, u6, us = 7 * hh, 7 * hh, 4 + 8 * hh, 3 * hh
                    filled(v, 4, "heads", u4, c)
                    q = psum[:, 4, 0:384].rearrange("p (t n) -> p t n", t=TT)
                    t0, t1 = (tmp_h[:, i].rearrange("p (t n) -> p t n", t=TT) for i in range(2))
                    ch.add(v.tensor_copy(q_h[:, :, 0:NOPE], q[:, :, 0:NOPE]))
                    ch.add(tt(t0, q[:, :, NOPE:96], cc_a.rearrange("p t a b -> p t (a b)"), ALU.mult))
                    ch.then(tt(t1, q[:, :, NOPE:96], ss_a.rearrange("p t a b -> p t (a b)"), ALU.mult))
                    v.sem_inc(free[4], 1)
                    ch.add(tt(q_h[:, :, 64:80], t0[:, :, 0:16], t1[:, :, 16:32], ALU.subtract))
                    ch.then(tt(q_h[:, :, 80:96], t0[:, :, 16:32], t1[:, :, 0:16], ALU.add))
                    v.sem_inc(L["q_ready"], 1)
                    v.wait_ge(L["diff_copied"], at("diff_copied", "heads", hh + 1, c))
                    dq = d_h[:, :, 0:128].rearrange("p t (s n) -> p t s n", n=HD)
                    t2, t3 = (tmp_h[:, 2 + i].rearrange("p (t s n) -> p t s n", t=TT, n=8) for i in range(2))
                    ch.add(tt(t2, dq[:, :, :, 0:8], S3(cc_b.unsqueeze(2), P, TT, 4, 8), ALU.mult))
                    ch.then(tt(t3, dq[:, :, :, 0:8], S3(ss_b.unsqueeze(2), P, TT, 4, 8), ALU.mult))
                    ch.add(tt(dq[:, :, :, 0:4], t2[:, :, :, 0:4], t3[:, :, :, 4:8], ALU.subtract))
                    ch.then(tt(dq[:, :, :, 4:8], t2[:, :, :, 4:8], t3[:, :, :, 0:4], ALU.add))
                    v.sem_inc(L["diff_ready"], 1)
                    filled(v, 6, "heads", u6 + 1, c)
                    v.tensor_copy(kT[0:96, :], psum[0:96, 6, :]).then_inc(free[6], 1)

                    def maxima(n, scale):
                        for t in range(TT):
                            filled(v, t, "heads", us + n, c)
                            d = psum[:, t, t * P:(t + 1) * P]
                            ch.add(tt(d, d, const("causal"), ALU.add))
                        ch.wait()
                        for t in range(TT):
                            ch.add(v.tensor_reduce(soft[:, 6 + n, t:t + 1], psum[:, t, 0:(t + 1) * P], AXX, ALU.max))
                        ch.wait()
                        ch.then(ts(soft[:, n, :], soft[:, 6 + n, :], -scale, None, ALU.mult))
                        v.sem_inc(L["max_ready"], 1)

                    def scans(j):
                        tile = 2 * hh + j
                        v.wait_ge(L["rot_ready"], at("rot_ready", "heads", tile + 1, c))
                        emptied(v, 6, "heads", u6 + 3 + 2 * j, c)
                        cos, sin, br, bi = rot[:, tile % 2, 0], rot[:, tile % 2, 1], bu[:, tile % 2, 0], bu[:, tile % 2, 1]
                        ch.add(tt(xab[:, 0], br, cos, ALU.mult))
                        ch.then(tt(xab[:, 1], bi, sin, ALU.mult))
                        ch.then(tt(xrot[:, 0], xab[:, 0], xab[:, 1], ALU.add))
                        ch.add(tt(xab[:, 0], bi, cos, ALU.mult))
                        ch.then(tt(xab[:, 1], br, sin, ALU.mult))
                        ch.then(tt(xrot[:, 1], xab[:, 0], xab[:, 1], ALU.subtract))
                        if tile > 0:
                            v.wait_ge(L["g_used"], at("g_used", "heads", tile, c))
                        r = S3(radius[:, bass.ds(4 * c + tile, 1)], P, SEQ)
                        for i in range(2):
                            ch.add(v.tensor_tensor_scan(gsc[:, i, :], r, xrot[:, i, :], 0.0, ALU.mult, ALU.add))
                        ch.wait()
                        v.sem_inc(L["scan_ready"], 1)

                    maxima(0, SCALE_A)
                    filled(v, 5, "heads", u5 + 2, c)
                    v.tensor_copy(dkT[0:64, :], psum[0:64, 5, :]).then_inc(free[5], 1)
                    scans(0)
                    emptied(v, 3, "heads", us, c)
                    ch.then(v.reciprocal(soft[:, 9, :], soft[:, 3, :]))
                    filled(v, 6, "heads", u6 + 6, c)
                    ch.then(tt(oa_tok[:, :, hh * 64:hh * 64 + 64], psum[:, 6, 0:256].rearrange("p (t n) -> p t n", t=TT),
                               S3(soft[:, 9, :].unsqueeze(2), P, TT, 64), ALU.mult))
                    v.sem_inc(free[6], 1)
                    v.sem_inc(L["oa_ready"], 1)
                    maxima(1, SCALE_B)
                    maxima(2, SCALE_B)
                    scans(1)
                    emptied(v, 3, "heads", us + 2, c)
                    ch.then(v.reciprocal(soft[:, 9:11, :], soft[:, 4:6, :]))
                    ch.then(ts(soft[:, 11, :], soft[:, 10, :], lam[:, 0:1], None, ALU.mult))
                    for t in range(TT):
                        w = (t + 1) * P
                        ch.then(ts(p2[:, t, 0:w], p2[:, t, 0:w], soft[:, 11, t:t + 1], None, ALU.mult))
                        ch.then(stt(out=p1[:, t, 0:w], in0=p1[:, t, 0:w], scalar=soft[:, 9, t:t + 1], in1=p2[:, t, 0:w], op0=ALU.mult, op1=ALU.subtract))
                        v.sem_inc(L["mix_ready"], 1)
                    for t in (0, 2):
                        filled(v, 4, "heads", u4 + 5 + t // 2, c)
                        v.tensor_copy(pT[:, t, 0:(t + 1) * P], psum[:, 4, 0:(t + 1) * P]).then_inc(free[4], 1)
                    filled(v, 6, "heads", u6 + 7, c)
                    o = psum[:, 6, 0:256].rearrange("p (t n) -> p t n", t=TT)
                    ob = ob_tok[:, :, bass.ds(2 * c + hh, 1), :].rearrange("p t a n -> p t (a n)")
                    ch.then(v.tensor_copy(tmp_o, o))
                    v.sem_inc(free[6], 1)
                    ch.add(v.tensor_copy(ob, tmp_o))
                    t4 = tmp_h[:, 0:2].rearrange("p a (t n) -> p (a t) n", t=2)
                    ch.then(tt(t4, tmp_o, tmp_o, ALU.mult))
                    ch.then(v.tensor_reduce(ms_b[:, :, bass.ds(2 * c + hh, 1)].rearrange("p t a -> p (t a)"), t4, AXX, ALU.add))
                v.wait_ge(L["h_used"], at("h_used", "heads", 4, c))
                yc, uc = (a[:, bass.ds(c, 1), :].rearrange("p a n -> p (a n)") for a in (yT, uT))
                ch.then(stt(out=yc, in0=uc, scalar=d_col[:, bass.ds(c, 1)], in1=psum[:, 7, :], op0=ALU.mult, op1=ALU.add))
                v.sem_inc(free[7], 1)
                v.sem_inc(L["y_ready"], 1)

            ch.reset()
            ch.then(ts(ms_b, ms_b, 1 / 64, SUB_EPS, ALU.mult, ALU.add))
            v.sem_inc(L["rms_mean"], 1)
            v.wait_ge(L["rms_root"], at("rms_root", "join", 1))
            ch.then(v.reciprocal(ms_b, ms_b))
            for t in range(TT):
                ch.then(tt(ob_tok[:, t], ob_tok[:, t], S3(ms_b[:, t, :].unsqueeze(2), P, HEADS, 64), ALU.mult))
                ch.then(tt(ob_tok[:, t], ob_tok[:, t], S3(subln.unsqueeze(1), P, HEADS, 64), ALU.mult))
                v.sem_inc(L["ob_ready"], 1)
            for i in range(4):
                filled(v, i, "join", 0)
                v.tensor_copy(obT[:, i, :], psum[:, i, :]).then_inc(free[i], 1)

            with v.Fori(0, 2) as n:
                ch.reset()
                for i in range(3):
                    for t in range(TT):
                        b, u = t % 2, 2 * i + t // 2
                        m = merged[:, t, bass.ds(n * BANK, BANK)]
                        emptied(v, b, "merge", u, n)
                        filled(v, 2 + b, "merge", u, n)
                        if i == 0:
                            tt(m, sg[:, b, :], psum[:, 2 + b, :], ALU.mult).then_inc(free[2 + b], 1)
                            v.wait_ge(free[2 + b], at(f"free{2 + b}", "merge", u + 1, n))
                        else:
                            ch.then(tt(mtmp, sg[:, b, :], psum[:, 2 + b, :], ALU.mult))
                            v.sem_inc(free[2 + b], 1)
                            if i == 2:
                                emptied(v, 4 + b, "merge", t // 2, n)
                                ch.then(tt(mtmp, mtmp, sg[:, 2 + b, :], ALU.mult))
                            ch.then(tt(m, m, mtmp, ALU.add))
                        v.sem_inc(L["merged_ready"], 1)

            def layernorm(st, g, b, t, phase):
                x = x_tok[:, t, :]
                for i in range(2):
                    ch.add(v.bn_stats(st[:, t, 6 * i:6 * i + 6], x[:, i * BANK:(i + 1) * BANK]))
                ch.wait()
                ch.then(v.bn_aggr(st[:, t, 12:14], st[:, t, 0:12]))
                ch.then(ts(st[:, t, 13:14], st[:, t, 13:14], LN_EPS, None, ALU.add))
                v.sem_inc(L["ln_var"], 1)
                v.wait_ge(L["ln_root"], at("ln_root", phase, t + 1))
                ch.then(v.reciprocal(st[:, t, 15:16], st[:, t, 14:15]))
                ch.then(ts(x, x, st[:, t, 12:13], st[:, t, 15:16], ALU.subtract, ALU.mult))
                ch.then(tt(x, x, g, ALU.mult))
                ch.then(tt(x, x, b, ALU.add))
                v.sem_inc(L["ln_ready"], 1)

            ch.reset()
            for k in range(1, KD, 2):
                filled(v, k, "tail", 0)
                v.tensor_copy(xT[:, k, :], psum[:, k, :]).then_inc(free[k], 1)
            v.wait_ge(x_back, 16)
            v.wait_ge(ln_in, 32)
            for t in range(TT):
                for n in range(2):
                    filled(v, 2 * t + n, "tail", 1)
                    xs = x_tok[:, t, n * BANK:(n + 1) * BANK]
                    ch.then(stt(out=xs, in0=xs, scalar=ALPHA, in1=psum[:, 2 * t + n, :], op0=ALU.mult, op1=ALU.add))
                    v.sem_inc(free[2 * t + n], 1)
                layernorm(ln_st, ln_g, ln_b, t, "tail")
            for k in range(1, KD, 2):
                filled(v, k, "tail", 2)
                v.tensor_copy(xT[:, k, :], psum[:, k, :]).then_inc(free[k], 1)
            emptied(v, 0, "tail", 3)
            E4 = lambda a: a.rearrange("p t (g j) -> p t g j", j=EPER)
            r0, r1, r2, r3, r4, r5 = (rt[:, i].rearrange("p (t e) -> p t e", t=TT) for i in range(6))
            g0, g1, g2, g3 = (r[:, :, 0:8] for r in (r0, r1, r2, r3))
            g4, g5 = r4[:, :, 0:8], r4[:, :, 8:16]
            ch.then(tt(bs, sc, S3(router_b.unsqueeze(1), P, TT, EXPERTS), ALU.add))
            a, b, c_, d = (E4(bs)[:, :, :, j] for j in range(4))
            ch.add(tt(g0, a, b, ALU.max))
            ch.add(tt(g1, a, b, ALU.min))
            ch.add(tt(g2, c_, d, ALU.max))
            ch.then(tt(g3, c_, d, ALU.min))
            ch.add(tt(g4, g0, g2, ALU.max))
            ch.add(tt(g5, g0, g2, ALU.min))
            ch.then(tt(g1, g1, g3, ALU.max))
            ch.then(tt(g5, g5, g1, ALU.max))
            ch.then(tt(g0, g4, g5, ALU.add))

            def first_best(values, prio, width, val, tmp, onehot):
                ch.then(v.tensor_reduce(val, values, AXX, ALU.max))
                ch.then(tt(tmp, values, S3(val.unsqueeze(2), P, TT, width), ALU.is_equal))
                ch.then(tt(tmp, tmp, S3(prio.unsqueeze(1), P, TT, width), ALU.mult))
                ch.then(v.tensor_reduce(val, tmp, AXX, ALU.max))
                ch.then(tt(onehot, tmp, S3(val.unsqueeze(2), P, TT, width), ALU.is_equal))

            first_best(g0, const("gprio"), 8, rs[:, 0], g1, g2)
            group = S3(g2.unsqueeze(3), P, TT, EGROUPS, EPER)
            ch.add(tt(E4(r3), E4(bs), group, ALU.mult))
            ch.wait()
            ch.then(ts(g1, g2, -1.0, -NEG, ALU.add, ALU.mult))
            ch.then(tt(E4(r3), E4(r3), S3(g1.unsqueeze(3), P, TT, EGROUPS, EPER), ALU.add))
            first_best(r3, const("eprio"), EXPERTS, rs[:, 1], r4, oh1)
            ch.then(stt(out=r3, in0=oh1, scalar=2 * NEG, in1=r3, op0=ALU.mult, op1=ALU.add))
            first_best(r3, const("eprio"), EXPERTS, rs[:, 2], r4, oh2)
            ch.then(tt(chosen, oh1, oh2, ALU.add))
            v.sem_inc(pick_ready, 1)
            for i, oh in enumerate((oh1, oh2)):
                ch.then(tt(r3, oh, sc, ALU.mult))
                ch.then(v.tensor_reduce(rs[:, 3 + i], r3, AXX, ALU.add))
            ch.then(tt(rs[:, 5], rs[:, 3], rs[:, 4], ALU.add))
            ch.then(v.reciprocal(rs[:, 6], rs[:, 5]))
            for i in range(2):
                ch.add(tt(w_tok[:, i], rs[:, 3 + i], rs[:, 6], ALU.mult))
            ch.add(v.memset(payload, 0.0))
            ch.add(v.memset(slot_of, -1.0))
            ch.add(v.tensor_copy(slots_now, const("slot")))
            ch.then(ts(rs[:, 7], const("tok"), -FAR, None, ALU.add))
            ch.add(ts(payload[:, :, 0:EXPERTS, 0], S3(rs[:, 7].unsqueeze(2), P, TT, EXPERTS), 1.0, None, ALU.mult))
            ch.then(ts(rs[:, 0], const("tok"), 2.0, -FAR, ALU.mult, ALU.add))
            ch.then(tt(payload[:, :, 0:EXPERTS, 1], S3(rs[:, 0].unsqueeze(2), P, TT, EXPERTS), oh2, ALU.add))
            filled(v, 1, "tail", 3)
            before = psum[:, 1, 0:TT * EXPERTS].rearrange("p (t e) -> p t e", t=TT)
            ch.then(stt(out=r3, in0=before, scalar=1.0, in1=chosen, op0=ALU.add, op1=ALU.mult))
            ch.add(ts(slot_of[:, :, 0:EXPERTS], r3, -1.0, None, ALU.add))
            ch.then(v.tensor_reduce(rs[:, 1, 0:1], psum[:, 1, TT * EXPERTS:(TT + 1) * EXPERTS], AXX, ALU.max))
            ch.then(v.tensor_copy(most[:], rs[:, 1, 0:1]))
            v.sem_inc(free[1], 1)
            meet(v, "moe")
            most_chosen = v.value_load(most[0:1, 0:1], min_val=0, max_val=SEQ)
            with v.Fori(0, PASSES) as ps:
                with v.If(most_chosen > ps * P):
                    meet(v, "pass")

                    def select(e, par):
                        tt(sel[par], S3(slots_now.unsqueeze(1), P, TT, P), S3(slot_of[:, :, bass.ds(e, 1)], P, TT, P),
                           ALU.is_equal).then_inc(sel_ready, 1)

                    def take_indices(e, par):
                        v.wait_ge(efull[0], e + 1)
                        ts(idx[par][:], psum[:, 0, 0:2], FAR, None, ALU.add).then_inc(efree[0], 1)

                    def take_x(e, par):
                        v.wait_ge(efull[2], e + 1)
                        v.tensor_copy(xgT[par][:, 4:8, :].rearrange("p a b -> p (a b)"), psum[:, 2, :]).then_inc(efree[2], 1)

                    select(0, 0)
                    take_indices(0, 0)
                    take_x(0, 0)
                    with v.Fori(0, EXPERTS // 2) as pair:
                        e2 = pair * 2
                        for par in range(2):
                            e = e2 + par
                            select(e + 1, 1 - par)
                            v.wait_ge(scattered[1 - par], e2 * 8 + 16 + 16 * par)
                            take_indices(e + 1, 1 - par)
                            v.wait_ge(silu_ready, e + 1)
                            v.wait_ge(efull[4], e + 1)
                            tt(h_e[par], silu, psum[:, 4, :], ALU.mult).then_inc(he_ready, 1)
                            v.wait_ge(he_ready, e + 1)
                            v.sem_inc(efree[4], 1)
                            v.sem_inc(efree[3], 1)
                            take_x(e + 1, 1 - par)
                            v.wait_ge(efull[7], e + 1)
                            v.wait_ge(scattered[par], e2 * 8 + 16)
                            v.tensor_copy(yb[par][:, BANK:], psum[:, 7, :]).then_inc(efree[7], 1)
                    meet(v, "passed")
                    ch.reset()
                    ch.then(ts(slots_now, slots_now, float(P), None, ALU.add))
                v.sem_inc(tick, 1)
            ch.reset()
            v.wait_ge(y_in_s, 64)
            v.wait_ge(ln2_in, 32)
            for t in range(TT):
                x = x_tok[:, t, :]
                y1, y2 = y_in[:, t, 0:D_MODEL], y_in[:, t, D_MODEL:]
                ch.add(ts(y1, y1, w_tok[:, 0, t:t + 1], None, ALU.mult))
                ch.wait()
                ch.then(stt(out=y1, in0=y2, scalar=w_tok[:, 1, t:t + 1], in1=y1, op0=ALU.mult, op1=ALU.add))
                ch.then(stt(out=x, in0=x, scalar=ALPHA, in1=y1, op0=ALU.mult, op1=ALU.add))
                layernorm(ln2_st, ln2_g, ln2_b, t, "last")
            meet(v, "end")

    @block.gpsimd
    def _(g):
        ch = Chain(g, chains["pool"])
        tt, ts = g.tensor_tensor, g.tensor_scalar
        g.wait_ge(setup_in, 80)
        ch.then(ts(idx_none[:], const("tok")[:, 0:2], FAR, None, ALU.add))
        with g.Fori(0, DEPTH) as l:
            meet(g, "layer")
            ch.reset()
            S = lambda i: sm[:, i]
            zr, zi, pr, pi, a, b, c_, d, rho, wr, wi = (S(i) for i in range(11))
            g.wait_ge(small_in, 224)
            g.wait_ge(dt_ready, 1)
            ch.add(tt(zr, a_re, dt_, ALU.mult))
            ch.then(tt(zi, a_im, dt_, ALU.mult))
            ch.add(ts(phi, zi, 1 / TWO_PI, None, ALU.mult))
            ch.add(ts(zr, zr, 2.0 ** -DOUBLINGS, None, ALU.mult))
            ch.then(ts(zi, zi, 2.0 ** -DOUBLINGS, None, ALU.mult))
            ch.add(ts(pr, zr, 1 / 6, 1.0, ALU.mult, ALU.add))
            ch.add(ts(rho, zr, 1 / 6, 1.0, ALU.mult, ALU.add))
            ch.then(ts(pi, zi, 1 / 6, None, ALU.mult))
            for k in (5, 4, 3, 2, 1):
                ch.add(tt(a, zr, pr, ALU.mult))
                ch.add(tt(b, zi, pi, ALU.mult))
                ch.add(tt(c_, zr, pi, ALU.mult))
                ch.add(tt(d, zi, pr, ALU.mult))
                ch.then(tt(rho, zr, rho, ALU.mult))
                o_r, o_i = (pr, pi) if k > 1 else (wr, wi)
                ch.add(tt(a, a, b, ALU.subtract))
                ch.then(tt(c_, c_, d, ALU.add))
                if k > 1:
                    ch.add(ts(rho, rho, 1 / k, 1.0, ALU.mult, ALU.add))
                    ch.add(ts(o_r, a, 1 / k, 1.0, ALU.mult, ALU.add))
                    ch.then(ts(o_i, c_, 1 / k, None, ALU.mult))
                else:
                    ch.add(ts(o_r, a, 1.0, None, ALU.mult))
                    ch.then(ts(o_i, c_, 1.0, None, ALU.mult))
            for _k in range(DOUBLINGS):
                ch.add(tt(a, wr, wr, ALU.mult))
                ch.add(tt(b, wi, wi, ALU.mult))
                ch.add(tt(c_, wr, wi, ALU.mult))
                ch.add(ts(d, wr, 2.0, None, ALU.mult))
                ch.add(tt(zr, rho, rho, ALU.mult))
                ch.then(ts(zi, rho, 2.0, None, ALU.mult))
                ch.add(tt(a, a, b, ALU.subtract))
                ch.add(tt(c_, c_, wi, ALU.add))
                ch.then(tt(rho, zr, zi, ALU.add))
                ch.add(tt(wr, a, d, ALU.add))
                ch.then(ts(wi, c_, 2.0, None, ALU.mult))
            ch.add(ts(radius, rho, 1.0, None, ALU.add))
            for an, steps, width in ((ang, const("fine"), FINE), (angc, const("coarse"), COARSE)):
                x0, x1 = (an[:, i].rearrange("p (s n) -> p s n", n=width) for i in (0, 1))
                ch.then(tt(x0, S3(phi.unsqueeze(2), P, STILES, width), S3(steps.unsqueeze(1), P, STILES, width), ALU.mult))
                ch.then(ts(x1, x0, ROUND, None, ALU.add))
                ch.then(ts(x1, x1, -ROUND, None, ALU.add))
                ch.then(tt(x0, x0, x1, ALU.subtract))
            g.sem_inc(ang_ready, 1)
            g.wait_ge(inv_ready, 1)
            ch.add(tt(a, wr, a_re, ALU.mult))
            ch.add(tt(b, wi, a_im, ALU.mult))
            ch.add(tt(c_, wi, a_re, ALU.mult))
            ch.then(tt(d, wr, a_im, ALU.mult))
            ch.add(tt(a, a, b, ALU.add))
            ch.then(tt(c_, c_, d, ALU.subtract))
            ch.add(tt(wr, a, inv_a, ALU.mult))
            ch.then(tt(wi, c_, inv_a, ALU.mult))
            qr, qi = (S3(w.unsqueeze(2), P, STILES, GROUP) for w in (wr, wi))
            ch.add(tt(btmp[:, 0], b_in[:, 0], qr, ALU.mult))
            ch.then(tt(btmp[:, 1], b_in[:, 1], qi, ALU.mult))
            ch.then(tt(bbar[:, 0], btmp[:, 0], btmp[:, 1], ALU.subtract))
            ch.add(tt(btmp[:, 0], b_in[:, 1], qr, ALU.mult))
            ch.then(tt(btmp[:, 1], b_in[:, 0], qi, ALU.mult))
            ch.then(tt(bbar[:, 1], btmp[:, 0], btmp[:, 1], ALU.add))
            ch.then(ts(c_nat[:, 1], c_nat[:, 1], -1.0, None, ALU.mult))
            g.wait_ge(trig_ready, 1)
            for j in range(3):
                g.wait_ge(free[j], at(f"free{j}", "front", 3))
            g.wait_ge(x_saved, 16)

            with g.Fori(0, 4) as c:
                ch.reset()

                def turns(tile):
                    def tab(which, i, width):
                        return which[:, i, bass.ds(4 * c + tile, 1), :].rearrange("p a n -> p (a n)")
                    cf, sf = (S3(tab(fine, i, FINE).unsqueeze(1), P, COARSE, FINE) for i in range(2))
                    cc, sc_ = (S3(tab(coarse, i, COARSE).unsqueeze(2), P, COARSE, FINE) for i in range(2))
                    V = lambda x: x.rearrange("p (a b) -> p a b", b=FINE)
                    ch.add(tt(V(rtm[:, 0]), cc, cf, ALU.mult))
                    ch.then(tt(V(rtm[:, 1]), sc_, sf, ALU.mult))
                    ch.then(tt(rot[:, tile % 2, 0], rtm[:, 0], rtm[:, 1], ALU.subtract))
                    ch.add(tt(V(rtm[:, 0]), sc_, cf, ALU.mult))
                    ch.then(tt(V(rtm[:, 1]), cc, sf, ALU.mult))
                    ch.then(tt(rot[:, tile % 2, 1], rtm[:, 0], rtm[:, 1], ALU.add))
                    g.sem_inc(L["rot_ready"], 1)

                def back(tile):
                    g.wait_ge(L["scan_ready"], at("scan_ready", "heads", tile + 1, c))
                    cos, sin, gr, gi = rot[:, tile % 2, 0], rot[:, tile % 2, 1], gsc[:, 0], gsc[:, 1]
                    ch.add(tt(rtm[:, 0], gr, cos, ALU.mult))
                    ch.then(tt(rtm[:, 1], gi, sin, ALU.mult))
                    if tile >= 2:
                        g.wait_ge(L["h_used"], at("h_used", "heads", tile - 1, c))
                    ch.then(tt(hst[:, tile % 2, 0], rtm[:, 0], rtm[:, 1], ALU.subtract))
                    ch.add(tt(rtm[:, 0], gr, sin, ALU.mult))
                    ch.then(tt(rtm[:, 1], gi, cos, ALU.mult))
                    g.sem_inc(L["g_used"], 1)
                    ch.then(tt(hst[:, tile % 2, 1], rtm[:, 0], rtm[:, 1], ALU.add))
                    g.sem_inc(L["h_ready"], 1)

                for i in range(2):
                    src = bbar[:, i, bass.ds(4 * c, 4), :]
                    ch.add(tt(pads[:, i].rearrange("p (j g q) -> p j g q", j=4, q=GROUP), S3(src.unsqueeze(2), P, 4, 8, GROUP),
                              S3(const("bmask").rearrange("p (j g) -> p j g", j=4).unsqueeze(3), P, 4, 8, GROUP), ALU.mult))
                    cn = c_nat[:, i, bass.ds(c, 1), :]
                    ch.add(tt(pads[:, 2 + i].rearrange("p (g n) -> p g n", g=8), S3(cn, P, 8, STATES),
                              S3(const("gmask").unsqueeze(2), P, 8, STATES), ALU.mult))
                ch.wait()
                g.sem_inc(L["pads_ready"], 1)
                turns(0)
                turns(1)
                back(0)
                turns(2)
                back(1)
                turns(3)
                back(2)
                back(3)
                filled(g, 6, "heads", 3, c)

            meet(g, "moe")
            most_chosen = g.value_load(most[0:1, 0:1], min_val=0, max_val=SEQ)
            with g.Fori(0, PASSES) as ps:
                with g.If(most_chosen > ps * P):
                    dma_sems = range(gathered[0].num, scattered[1].num + 1)
                    g.dma_reset(dma_sems)
                    g.sem_clear(dma_sems)
                    meet(g, "pass")

                    def gather(e, par):
                        g.wait_ge(efree[0], e + 2)
                        g.sem_inc(tick, 1)
                        g.indirect_dma_start(out=xg[par], out_offset=None, in_=x_mid,
                                             in_offset=bass.IndirectOffsetOnAxis(ap=idx[par][:, 0:1], axis=0),
                                             bounds_check=SEQ - 1, oob_is_err=False).then_inc(gathered[par], 16)

                    for i in range(2):
                        g.indirect_dma_start(out=y_moe, out_offset=bass.IndirectOffsetOnAxis(ap=idx_none[:, 0:1], axis=0),
                                             in_=x_tok[:, 0, :], in_offset=None,
                                             bounds_check=2 * SEQ - 1, oob_is_err=False).then_inc(scattered[i], 16)
                    gather(0, 0)
                    with g.Fori(0, EXPERTS // 2) as pair:
                        e2 = pair * 2
                        for par in range(2):
                            e = e2 + par
                            gather(e + 1, 1 - par)
                            for b in (6, 7):
                                g.wait_ge(efree[b], e + 2)
                            g.sem_inc(tick, 1)
                            g.indirect_dma_start(out=y_moe, out_offset=bass.IndirectOffsetOnAxis(ap=idx[par][:, 1:2], axis=0),
                                                 in_=yb[par], in_offset=None,
                                                 bounds_check=2 * SEQ - 1, oob_is_err=False).then_inc(scattered[par], 16)
                    for i in range(2):
                        g.wait_ge(scattered[i], 16 * (EXPERTS // 2 + 1))
                    g.wait_ge(gathered[0], 16 * (EXPERTS // 2 + 1))
                    g.wait_ge(gathered[1], 16 * (EXPERTS // 2))
                    meet(g, "passed")
                g.sem_inc(tick, 1)
            meet(g, "end")

    ctx.close()


_INS = ["x", "positions", "w_in", "b_gate", "mla_q_norm", "mla_w_uq", "mla_kv_norm", "mla_w_ukv", "mla_w_out",
        "diff_lambda", "diff_subln", "diff_w_out", "ssm_a_re", "ssm_a_im", "ssm_log_dt", "ssm_b_re", "ssm_b_im",
        "ssm_c_re", "ssm_c_im", "ssm_d", "ssm_w_glu", "w_o", "ln_gain", "ln_bias", "router_w", "router_bias",
        "moe_w_gate", "moe_w_up", "moe_w_down"]


def kernel(**inputs):
    import concourse.bacc as _bacc
    from concourse.bass_utils import run_bass_kernel_spmd as _run

    nc = _bacc.Bacc("TRN2", target_bir_lowering=False, num_devices=1)
    arrays, aps = {}, {}
    for name in _INS:
        a = np.ascontiguousarray(inputs[name])
        arrays[f"in_{name}"] = a
        aps[name] = nc.dram_tensor(f"in_{name}", a.shape, mybir.dt.from_np(a.dtype), kind="ExternalInput").ap()
    tables = {}
    for name, a in (("constants", constant_table()), ("layers", layer_table())):
        arrays[name] = a
        tables[name] = nc.dram_tensor(name, a.shape, F32, kind="ExternalInput").ap()
    out = nc.dram_tensor("out", (1, SEQ, D_MODEL), F32, kind="ExternalOutput").ap()
    build(nc, aps, tables["constants"], tables["layers"], out)
    r = _run(nc, [arrays], core_ids=[0])
    return r.results[0]["out"]
```

```python
import math
from contextlib import ExitStack

import numpy as np

import concourse.bass as bass
from concourse import mybir

F32 = mybir.dt.float32
I32 = mybir.dt.int32
U32 = mybir.dt.uint32
ALU = mybir.AluOpType
ACT = mybir.ActivationFunctionType
AXX = mybir.AxisListType.X

P = 128
BANK = 512
DEPTH = 2
SEQ = 512
D_MODEL = 1024
TT = SEQ // P
KD = D_MODEL // P
Q_LORA, KV_LORA, ROPE_A, NOPE, V_DIM = 256, 128, 32, 64, 64
HEADS = 8
HD = 32
ROT_B = HD // 4
MLA_COLS = Q_LORA + KV_LORA + ROPE_A
DIFF_COLS = HEADS * 2 * HD
OFF_DIFF = MLA_COLS
OFF_SSM = OFF_DIFF + 3 * DIFF_COLS
SSM_W, GROUP, GROUPS, STATES = 512, 16, 32, 64
OFF_GATE = OFF_SSM + SSM_W
STILES = GROUPS * STATES // P
FINE = 32
COARSE = SEQ // FINE
DOUBLINGS = 10
EXPERTS, EGROUPS, EPER, FF = 32, 8, 4, 512
KF = FF // P
SLOTS = P // 2
PASSES = SEQ // SLOTS
GATE_W = 3 * D_MODEL // HEADS
PAIRS = EXPERTS // 2
ALPHA = (2 * DEPTH) ** 0.25
LN_EPS, RMS_EPS, SUB_EPS = 1e-5, 1e-6, 1e-5
THETA = 500000.0
NEG = -1e30
FAR = 4096.0
ROUND = 12582912.0
TWO_PI = 2 * math.pi
PI_HI = 6.28125
PI_LO = TWO_PI - PI_HI
PI_MAX = 3.1415925
SCALE_A = (NOPE + ROPE_A) ** -0.5
SCALE_B = HD ** -0.5

CONST_W = dict(ident=P, upper=P, ones=P, slot=SLOTS, causal=P, gmask=8, bmask=32, inv=20, eprio=32,
               gprio=8, tok=TT, fine=FINE, coarse=COARSE)
CONST_AT, _n = {}, 0
for _k, _w in CONST_W.items():
    CONST_AT[_k] = _n
    _n += _w
CONST_COLS = _n


def constant_table():
    c = np.zeros((P, CONST_COLS), np.float32)
    p = np.arange(P)

    def put(name, v):
        c[:, CONST_AT[name]:CONST_AT[name] + CONST_W[name]] = v

    put("ident", np.eye(P))
    put("upper", p[:, None] < p[None, :])
    put("ones", 1.0)
    put("slot", p[None, :SLOTS])
    put("causal", np.where(p[None, :] > p[:, None], NEG, 0.0))
    put("gmask", (p[:, None] // GROUP) == np.arange(8)[None, :])
    jj, g = np.divmod(np.arange(32), 8)
    put("bmask", g[None, :] == 2 * jj[None, :] + (p[:, None] >= STATES))
    inv = [np.float32(THETA) ** (-np.arange(0, r, 2, dtype=np.float32) / np.float32(r)) for r in (ROPE_A, ROT_B)]
    put("inv", np.concatenate(inv)[None, :])
    put("eprio", EXPERTS - np.arange(EXPERTS)[None, :])
    put("gprio", EGROUPS - np.arange(EGROUPS)[None, :])
    put("tok", np.arange(TT)[None, :] * P + p[:, None])
    put("fine", np.arange(FINE)[None, :])
    put("coarse", np.arange(COARSE)[None, :] * FINE)
    return c


def layer_table():
    li = np.array([0.8 - 0.6 * math.exp(-0.3 * l) for l in range(DEPTH)])
    return np.broadcast_to(np.stack([li, 1.0 - li], 1)[:, None, :], (DEPTH, P, 2)).astype(np.float32).copy()


STEPS = dict(front=1, heads=4, join=1, merge=2, tail=1, last=1)
RAISED = dict(
    b0=(3, 6, 1, 0, 4, 0), b1=(3, 6, 1, 0, 4, 0), b2=(3, 6, 1, 6, 3, 0), b3=(2, 6, 1, 6, 3, 0),
    b4=(2, 17, 0, 2, 3, 0), b5=(2, 18, 0, 2, 3, 0), b6=(2, 22, 0, 0, 3, 0), full7=(2, 0, 0, 0, 3, 0),
    b7=(2, 1, 0, 0, 3, 0),
    sq_sums=(1, 0, 0, 0, 0, 0), rms_mean=(1, 0, 1, 0, 0, 0), rms_root=(1, 0, 1, 0, 0, 0),
    lora_ready=(1, 0, 0, 0, 0, 0),
    q_ready=(0, 2, 0, 0, 0, 0), kv_ready=(0, 2, 0, 0, 0, 0), diff_copied=(0, 2, 0, 0, 0, 0),
    diff_ready=(0, 2, 0, 0, 0, 0), max_ready=(0, 6, 0, 0, 0, 0), mix_ready=(0, 8, 0, 0, 0, 0),
    oa_ready=(0, 2, 0, 0, 0, 0), pads_ready=(0, 1, 0, 0, 0, 0), rot_ready=(0, 4, 0, 0, 0, 0),
    scan_ready=(0, 4, 0, 0, 0, 0), h_ready=(0, 4, 0, 0, 0, 0),
    h_used=(0, 4, 0, 0, 0, 0), wd_ready=(0, 1, 0, 0, 0, 0),
    ob_ready=(0, 0, 4, 0, 0, 0), gelu_done=(0, 0, 1, 0, 0, 0),
    y_ready=(0, 1, 0, 0, 0, 0), g_used=(0, 4, 0, 0, 0, 0),
    gate_room=(2, 8, 0, 0, 0, 0),
    merged_ready=(0, 0, 0, 12, 0, 0),
    ln_var=(0, 0, 0, 0, 4, 4), ln_root=(0, 0, 0, 0, 4, 4), ln_ready=(0, 0, 0, 0, 4, 4),
)
for _b in range(7):
    RAISED[f"full{_b}"] = RAISED[f"b{_b}"]
    RAISED[f"free{_b}"] = RAISED[f"b{_b}"]
RAISED["free7"] = RAISED["b7"]


def at(name, phase, n, step=0):
    v = n
    for k, (ph, steps) in enumerate(STEPS.items()):
        if ph == phase:
            return v + step * RAISED[name][k]
        v += steps * RAISED[name][k]


BASE4, BASE5, BASE6 = (0, 8), (0, 9), (4, 13)
GATE_AT = ((5, 3), (4, 5), (5, 6), (6, 7))


def gate_at(hh, t):
    b, u = GATE_AT[t]
    return b, {4: BASE4, 5: BASE5, 6: BASE6}[b][hh] + u


class Chain:

    def __init__(self, eng, sem):
        self.eng, self.sem, self.n = eng, sem, 0

    def reset(self):
        self.eng.sem_clear(self.sem)
        self.n = 0

    def add(self, ins):
        ins.then_inc(self.sem, 1)
        self.n += 1
        return ins

    def wait(self):
        if self.n:
            self.eng.wait_ge(self.sem, self.n)

    def then(self, ins):
        self.add(ins)
        self.wait()


def build(nc, t_in, consts, layer_consts, out):
    ctx = ExitStack()
    sb = ctx.enter_context(nc.sbuf_tensor("sb", [P, 53100], F32))
    psum = ctx.enter_context(nc.psum_tensor("psum", [P, 8, BANK], F32))
    pos_i = ctx.enter_context(nc.sbuf_tensor("pos_i", [P, TT], I32))
    row_x = [ctx.enter_context(nc.sbuf_tensor(f"row_x{i}", [P, 1], U32)) for i in range(2)]
    row_y = [ctx.enter_context(nc.sbuf_tensor(f"row_y{i}", [P, 1], U32)) for i in range(2)]
    row_none = ctx.enter_context(nc.sbuf_tensor("row_none", [P, 1], U32))
    most = ctx.enter_context(nc.sbuf_tensor("most", [P, 1], I32))
    x_old = nc.dram_tensor("x_old", [SEQ, D_MODEL], F32, kind="Internal").ap()
    x_mid = nc.dram_tensor("x_mid", [SEQ, D_MODEL], F32, kind="Internal").ap()
    gates_d = nc.dram_tensor("gates_d", [SEQ, 3 * D_MODEL], F32, kind="Internal").ap()
    y_moe = nc.dram_tensor("y_moe", [2 * SEQ, D_MODEL], F32, kind="Internal").ap()

    class Area:
        def __init__(self, start, end):
            self.at, self.end = start, end

        def take(self, *dims):
            n = int(np.prod(dims))
            v = sb[:, self.at:self.at + n]
            self.at += n
            assert self.at <= self.end, (self.at, self.end)
            if len(dims) > 1:
                names = "abcd"[:len(dims)]
                spec = " ".join(names)
                v = v.rearrange(f"p ({spec}) -> p {spec}", **dict(zip(names, dims)))
            return v

    kept = Area(0, 53100)
    cst = kept.take(CONST_COLS)

    def const(name):
        return cst[:, CONST_AT[name]:CONST_AT[name] + CONST_W[name]]

    ident, ones = const("ident"), const("ones")
    xT = kept.take(KD, SEQ)
    uT = kept.take(4, SEQ)
    yT = kept.take(4, SEQ)
    x_at = kept.at
    x_tok = kept.take(TT, D_MODEL)
    oT = Area(x_at, x_at + 4096)
    oaT, obT = oT.take(4, SEQ), oT.take(4, SEQ)
    cc_a, ss_a = kept.take(TT, 2, 16), kept.take(TT, 2, 16)
    cc_b, ss_b = kept.take(TT, 8), kept.take(TT, 8)
    router_w = kept.take(KD, EXPERTS)
    router_b = kept.take(EXPERTS)
    lyr = kept.take(2)
    small = kept.take(64)
    lam = small[:, 0:4]
    rope_pos = kept.take(TT)
    half_pi = kept.take(1)
    base = kept.at

    a1 = Area(base, 53100)
    wd = a1.take(2, KD, 3 * P)
    uq, ukv = a1.take(2, HEADS * 96), a1.take(HEADS * 128)
    loraT = a1.take(3, SEQ)
    krope = a1.take(TT, ROPE_A)
    norms_at = a1.at
    qn_bc, kvn_bc, subln = a1.take(Q_LORA), a1.take(KV_LORA), a1.take(2 * HD)
    lam_in = a1.take(4, HD)
    a_re, a_im, dt_, inv_a = (a1.take(STILES) for _ in range(4))
    radius, phi = a1.take(STILES), a1.take(STILES)
    bbar = a1.take(2, STILES, GROUP)
    c_nat = a1.take(2, 4, STATES)
    d_col = a1.take(4)
    fine, coarse = a1.take(2, STILES, FINE), a1.take(2, STILES, COARSE)
    ms_b = a1.take(TT, HEADS)
    ob_tok = a1.take(TT, HEADS, 2 * HD)
    heads_at = a1.at
    rope = Area(base, 53100)
    rope_ang, rope_sc = rope.take(2, TT, 20), rope.take(2, TT, 20)
    a2 = Area(heads_at, 53100)
    w_ssm, w_mla = a2.take(KD, SSM_W), a2.take(KD, MLA_COLS)
    lora = a2.take(TT, Q_LORA + KV_LORA)
    b_in = a2.take(2, STILES, GROUP)
    sqs, ssum, rrt = a2.take(P * 2), a2.take(TT, 2), a2.take(TT, 2)
    rtmp = a2.take(3, TT, 32)
    sm = a2.take(16, STILES)
    ang = a2.take(3, STILES * FINE)
    angc = a2.take(3, STILES * COARSE)
    btmp = a2.take(2, STILES, GROUP)
    a3 = Area(heads_at, 53100)
    q_h, k_h, v_h = a3.take(TT, 96), a3.take(TT, 96), a3.take(TT, 64)
    qT, kT = a3.take(SEQ), a3.take(SEQ)
    d_h = a3.take(TT, 3 * 64)
    dqT, dkT = a3.take(SEQ), a3.take(SEQ)
    p1, p2, pT = (a3.take(P * TT * (TT + 1) // 2) for _ in range(3))

    def causal_part(p, t, a=0, b=None):
        start = P * t * (t + 1) // 2
        return p[:, start + a:start + (b if b else (t + 1) * P)]

    gw = a3.take(KD, GATE_W)
    gb = Area(norms_at, norms_at + Q_LORA + KV_LORA).take(GATE_W)
    gout = a3.take(2, GATE_W)
    oa_tok = a3.take(TT, P)
    tmp_h = a3.take(4, TT * 32)
    tmp_o = a3.take(TT, 64)
    soft = a3.take(12, TT)
    pads = Area(x_at + 2048, x_at + 4096).take(4, 512)
    bT, cT = a3.take(2, 512), a3.take(2, 4, 32)
    rot = a3.take(2, 2, SEQ)
    rtm = a3.take(2, SEQ)
    bu = a3.take(2, 2, SEQ)
    xab = a3.take(2, SEQ)
    gsc = a3.take(2, SEQ)
    hst = a3.take(2, 2, SEQ)
    a4 = Area(base, 53100)
    merged = a4.take(TT, D_MODEL)
    w_o = a4.take(KD, D_MODEL)
    m_at = a4.at
    gates = a4.take(TT, 3 * D_MODEL)
    wy = [a4.take(4, BANK) for _ in range(4)]
    sg = a4.take(2, BANK)
    mtmp = a4.take(BANK)
    a5 = Area(a4.at, 53100)
    ln_g, ln_b = a5.take(D_MODEL), a5.take(D_MODEL)
    ln_st, ln2_st = a5.take(TT, 16), a5.take(TT, 16)
    a6 = Area(base, 53100)
    e_down = [a6.take(KF, D_MODEL) for _ in range(2)]
    xg = [a6.take(D_MODEL) for _ in range(2)]
    yb = [a6.take(D_MODEL) for _ in range(2)]
    assert a6.at == m_at
    e_gate = [a6.take(KD, FF) for _ in range(2)]
    e_up = [a6.take(KD, FF) for _ in range(2)]
    assert a6.at <= a4.at
    e_misc = Area(a6.at, a4.at)
    sel = [e_misc.take(TT, 2, SLOTS) for _ in range(2)]
    hT = e_misc.take(KF, P)
    h_e, silu = e_misc.take(FF), e_misc.take(FF)
    xgT = e_misc.take(KD, P)
    a7 = Area(x_at - 4096, x_at)
    EP = EXPERTS + 2
    sc, bs, rt = a7.take(TT, EXPERTS), a7.take(TT, EXPERTS), a7.take(6, TT * EXPERTS)
    oh1, oh2, chosen = a7.take(TT, EXPERTS), a7.take(TT, EXPERTS), a7.take(TT, EXPERTS)
    slot_of, payload = a7.take(TT, EP), a7.take(TT, EP, 2)
    slots_now = a7.take(SLOTS)
    w_tok = a7.take(2, TT)
    rs = a7.take(8, TT)
    ln2_g, ln2_b = a7.take(D_MODEL), a7.take(D_MODEL)
    y_in = Area(base, 53100).take(TT, 2 * D_MODEL)

    sems = {}

    def sem(name):
        sems[name] = ctx.enter_context(nc.semaphore(name))
        return sems[name]

    setup_in = sem("setup_in")
    setup_ang = sem("setup_ang")
    setup_trig = sem("setup_trig")
    setup_zero = sem("setup_zero")
    layer_first = sem("layer_first").num
    full = [sem(f"full{b}") for b in range(8)]
    free = [sem(f"free{b}") for b in range(8)]
    L = {n: sem(n) for n in RAISED if n[0:4] not in ("full", "free") and not (n[0] == "b" and n[1:].isdigit())}
    small_in, wssm_in, wmla_in, wuq_in = sem("small_in"), sem("wssm_in"), sem("wmla_in"), sem("wuq_in")
    wd_in = [sem(f"wd_in{i}") for i in range(2)]
    x_saved, wo_in, x_back, ln_in, ln2_in, y_in_s = (sem(n) for n in ("x_saved", "wo_in", "x_back", "ln_in", "ln2_in", "y_in_s"))
    gw_in, gates_saved = sem("gw_in"), sem("gates_saved")
    gates_in = [sem(f"gates_in{i}") for i in range(3)]
    wy_in = [sem(f"wy_in{i}") for i in range(4)]
    dt_ready, lam_ready, lam_exp, ang_ready, trig_ready, inv_ready, coef_ready = (
        sem(n) for n in ("dt_ready", "lam_ready", "lam_exp", "ang_ready", "trig_ready", "inv_ready", "coef_ready"))
    krope_ready, subln_ready = sem("krope_ready"), sem("subln_ready")
    score_ready, pick_ready, slots_ready, xmid_ready = (sem(n) for n in ("score_ready", "pick_ready", "slots_ready", "xmid_ready"))
    layer_last = sem("layer_last").num
    pass_first = sem("pass_first").num
    STAGES = ("idx", "x0", "x1", "gate", "up", "h", "y0", "y1")
    efull = {b: sem(f"efull_{b}") for b in STAGES}
    efree = {b: sem(f"efree_{b}") for b in STAGES}
    ebank = {b: k for k, b in enumerate(STAGES)}
    sel_ready, he_ready, silu_ready, rows_ready = sem("sel_ready"), sem("he_ready"), sem("silu_ready"), sem("rows_ready")
    eg_in, eu_in, ed_in = ([sem(f"{n}_in{i}") for i in range(2)] for n in ("eg", "eu", "ed"))
    pass_last = sem("pass_last").num
    gathered = [sem(f"gathered{i}") for i in range(2)]
    scattered = [sem(f"scattered{i}") for i in range(2)]
    arr = {n: sem(f"arrive_{n}") for n in ("layer", "moe", "pass", "passed", "end")}
    go = {n: sem(f"go_{n}") for n in ("layer", "moe", "pass", "passed", "end")}
    tick = sem("tick")
    chains = {n: sem(f"chain_{n}") for n in ("pe", "act", "dve", "pool")}
    out_done = sem("out_done")

    def meet(eng, name):
        eng.drain().then_inc(arr[name], 1)
        eng.wait_ge(go[name], 1)
        eng.sem_inc(tick, 1)

    def host(sp, name, clears, start=True):
        sp.wait_ge(arr[name], 4)
        sp.sem_clear(arr[name])
        for r in clears:
            sp.sem_clear(r)
        if start:
            sp.sem_inc(go[name], 1)

    def claim(pe, b, phase, u, step=0):
        v = at(f"free{b}", phase, u, step)
        if not (isinstance(v, int) and v == 0):
            pe.wait_ge(free[b], v)

    def filled(eng, b, phase, u, step=0):
        eng.wait_ge(full[b], at(f"full{b}", phase, u + 1, step))

    def emptied(eng, b, phase, u, step=0):
        eng.wait_ge(free[b], at(f"free{b}", phase, u + 1, step))

    x_d, w_in = t_in["x"], t_in["w_in"]
    b_gate_flat = t_in["b_gate"].rearrange("l a b -> l (a b)")
    tok3 = lambda d: d.rearrange("(t p) d -> p t d", p=P)
    rows = lambda d: d.rearrange("(k p) n -> p k n", p=P)
    bcast = lambda d: d.partition_broadcast(P)
    S3 = lambda v, *shape: v.to_broadcast(list(shape))

    ctx.enter_context(nc.allow_non_contiguous_dma(reason="small parameters, a number for each partition"))
    block = ctx.enter_context(nc.Block())

    @block.sync
    def _(sp):
        sp.dma_start(cst, consts).then_inc(setup_in, 16)
        sp.dma_start(x_tok, tok3(x_d[0])).then_inc(setup_in, 16)
        sp.dma_start(pos_i[:], t_in["positions"].rearrange("a (t p) -> p (a t)", p=P)).then_inc(setup_in, 16)
        sp.dma_start(router_w, rows(t_in["router_w"])).then_inc(setup_in, 16)
        sp.dma_start(router_b, bcast(t_in["router_bias"])).then_inc(setup_in, 16)
        sp.wait_ge(setup_in, 80)
        with sp.Fori(0, DEPTH) as l:
            host(sp, "layer", [range(layer_first, layer_last + 1), go["moe"], go["end"]])
            wl = w_in[l]
            loads = [
                (lyr, layer_consts[l]), (qn_bc, bcast(t_in["mla_q_norm"][l])), (kvn_bc, bcast(t_in["mla_kv_norm"][l])),
                (subln, bcast(t_in["diff_subln"][l])),
                (lam_in, bcast(t_in["diff_lambda"][l].rearrange("a b -> (a b)")).rearrange("p (a b) -> p a b", a=4)),
                (a_re, t_in["ssm_a_re"][l].rearrange("(t h) n -> (h n) t", h=2)),
                (a_im, t_in["ssm_a_im"][l].rearrange("(t h) n -> (h n) t", h=2)),
                (b_in[:, 0], t_in["ssm_b_re"][l].rearrange("(t h) n q -> (h n) t q", h=2)),
                (b_in[:, 1], t_in["ssm_b_im"][l].rearrange("(t h) n q -> (h n) t q", h=2)),
                (c_nat[:, 0], t_in["ssm_c_re"][l].rearrange("(c g) q n -> (g q) c n", g=8)),
                (c_nat[:, 1], t_in["ssm_c_im"][l].rearrange("(c g) q n -> (g q) c n", g=8)),
                (d_col, t_in["ssm_d"][l].rearrange("(c p) -> p c", p=P)),
            ]
            for h in range(2):
                dt_src = t_in["ssm_log_dt"][l].rearrange("(t h) -> h t", h=2)[h]
                loads.append((dt_[h * 64:h * 64 + 64, :], dt_src.partition_broadcast(64)))
            assert len(loads) == 14
            sp.dma_start(w_ssm, rows(wl[:, OFF_SSM:OFF_SSM + SSM_W])).then_inc(wssm_in, 16)
            for dst, src in loads:
                sp.dma_start(dst, src).then_inc(small_in, 16)
            sp.dma_start(w_mla, rows(wl[:, 0:MLA_COLS])).then_inc(wmla_in, 16)
            sp.dma_start(uq, rows(t_in["mla_w_uq"][l])).then_inc(wuq_in, 16)
            sp.dma_start(ukv, t_in["mla_w_ukv"][l]).then_inc(wuq_in, 16)
            sp.dma_start(tok3(x_old), x_tok).then_inc(x_saved, 16)
            diff_w = wl[:, OFF_DIFF:OFF_SSM].rearrange("(k p) (s c n) -> c s p k n", p=P, s=3, n=P)

            def load_diff(c, par):
                for i in range(3):
                    sp.dma_start(wd[:, par, :, i * P:(i + 1) * P], diff_w[c, i]).then_inc(wd_in[par], 16)

            def load_gate(b):
                sp.dma_start(gw, rows(wl[:, bass.ds(b * GATE_W + OFF_GATE, GATE_W)])).then_inc(gw_in, 16)
                sp.dma_start(gb[0:1, :], b_gate_flat[bass.ds(l, 1), bass.ds(b * GATE_W, GATE_W)]).then_inc(gw_in, 16)

            def serve_heads(c, par, last):
                sp.wait_ge(wd_in[par], 48 * (c // 2 + 1))
                sp.sem_inc(L["wd_ready"], 1)
                for hh in range(2):
                    for t in range(TT):
                        b, u = gate_at(hh, t)
                        emptied(sp, b, "heads", u, c)
                        sp.dma_start(gates_d[t * P:(t + 1) * P, bass.ds(c * 2 * GATE_W + hh * GATE_W, GATE_W)], gout[:, t % 2, :]).then_inc(gates_saved, 16)
                        if hh == 1 and t == 0 and not last:
                            load_diff(c + 2, par)
                        if t == TT - 1 and not (last and par == 1 and hh == 1):
                            load_gate(2 * c + hh + 1)
                        sp.wait_ge(gates_saved, c * 128 + 16 * (4 * hh + t + 1))
                        sp.sem_inc(L["gate_room"], 1)

            for c in range(2):
                load_diff(c, c)
            sp.wait_ge(L["pads_ready"], at("pads_ready", "heads", 1))
            sp.wait_ge(krope_ready, 1)
            load_gate(0)
            for _i in range(2):
                sp.sem_inc(L["gate_room"], 1)
            for c in range(4):
                serve_heads(c, c % 2, c >= 2)
            def load_branch(i, n):
                w2 = [rows(t_in["mla_w_out"][l]), rows(t_in["diff_w_out"][l]), rows(t_in["ssm_w_glu"][l])][i]
                if n:
                    filled(sp, 3, "merge", 2 * i + 1, 0)
                sp.dma_start(wy[i], w2[:, :, n * BANK:(n + 1) * BANK]).then_inc(wy_in[i], 16)
                if i == 2:
                    sp.dma_start(wy[3], w2[:, :, D_MODEL + n * BANK:D_MODEL + (n + 1) * BANK]).then_inc(wy_in[3], 16)

            sp.wait_ge(L["gelu_done"], at("gelu_done", "join", 1))
            for b in range(4):
                emptied(sp, b, "join", 0)
            for i in range(3):
                col = slice(i * D_MODEL, (i + 1) * D_MODEL)
                if i == 0:
                    load_branch(0, 0)
                sp.dma_start(gates[:, :, col], tok3(gates_d[:, col])).then_inc(gates_in[i], 16)
                if i:
                    load_branch(i, 0)
            sp.dma_start(w_o, rows(t_in["w_o"][l])).then_inc(wo_in, 16)
            for i in range(3):
                load_branch(i, 1)
            filled(sp, 3, "merge", 5, 1)
            sp.wait_ge(x_saved, 16)
            sp.dma_start(x_tok, tok3(x_old)).then_inc(x_back, 16)
            filled(sp, 5, "merge", 1, 1)
            sp.wait_ge(L["merged_ready"], at("merged_ready", "merge", 12, 1))
            sp.dma_start(ln_g, bcast(t_in["ln_gain"][l][0])).then_inc(ln_in, 16)
            sp.dma_start(ln_b, bcast(t_in["ln_bias"][l][0])).then_inc(ln_in, 16)
            sp.dma_start(ln2_g, bcast(t_in["ln_gain"][l][1])).then_inc(ln2_in, 16)
            sp.dma_start(ln2_b, bcast(t_in["ln_bias"][l][1])).then_inc(ln2_in, 16)

            def expert_loads(w, names, q):
                for i in range(2):
                    sp.dma_start(w[i], rows(t_in[names[0]][l][2 * q + i])).then_inc(names[1][i], 16)

            w_gates, w_ups, w_downs = ("moe_w_gate", eg_in), ("moe_w_up", eu_in), ("moe_w_down", ed_in)
            expert_loads(e_gate, w_gates, 0)
            expert_loads(e_up, w_ups, 0)
            filled(sp, 7, "tail", 1)
            expert_loads(e_down, w_downs, 0)
            sp.wait_ge(L["ln_ready"], at("ln_ready", "tail", 4))
            sp.dma_start(tok3(x_mid), x_tok).then_inc(xmid_ready, 16)
            sp.wait_ge(xmid_ready, 16)
            host(sp, "moe", [go["layer"]])
            most_chosen = sp.value_load(most[0:1, 0:1], min_val=0, max_val=SEQ)
            with sp.Fori(0, PASSES) as ps:
                with sp.If(most_chosen > ps * SLOTS):
                    host(sp, "pass", [go["passed"]], start=False)
                    for b in STAGES:
                        sp.sem_inc(efree[b], 1)
                    sp.sem_inc(go["pass"], 1)
                    with sp.Fori(1, PAIRS) as q:
                        sp.wait_ge(efull["gate"], q)
                        expert_loads(e_gate, w_gates, q)
                        sp.wait_ge(efull["up"], q)
                        expert_loads(e_up, w_ups, q)
                        sp.wait_ge(efull["y1"], q)
                        expert_loads(e_down, w_downs, q)
                    host(sp, "passed", [range(pass_first, pass_last + 1), go["pass"]], start=False)
                    with sp.If(most_chosen > (ps + 1) * SLOTS):
                        expert_loads(e_gate, w_gates, 0)
                        expert_loads(e_up, w_ups, 0)
                        expert_loads(e_down, w_downs, 0)
                    sp.sem_inc(go["passed"], 1)
                sp.sem_inc(tick, 1)
            for t in range(TT):
                sp.dma_start(y_in[:, t, :], y_moe.rearrange("(t p k) d -> t p (k d)", p=P, k=2)[t]).then_inc(y_in_s, 16)
            host(sp, "end", [])
        sp.dma_start(tok3(out[0]), x_tok).then_inc(out_done, 16)
        sp.wait_ge(out_done, 16)

    @block.tensor
    def _(pe):
        ch = Chain(pe, chains["pe"])
        pe.wait_ge(setup_in, 80)
        with pe.Fori(0, DEPTH) as l:
            meet(pe, "layer")

            def transpose_x(phase, u):
                for k in range(KD):
                    claim(pe, k, phase, u)
                    for t in range(TT):
                        mm = pe.transpose(psum[:, k, t * P:(t + 1) * P], x_tok[:, t, k * P:(k + 1) * P], ident)
                    mm.then_inc(full[k], 1)

            transpose_x("front", 0)
            pe.wait_ge(wssm_in, 16)
            for c in range(4):
                if c == 0:
                    for k in range(KD):
                        emptied(pe, k, "front", 0)
                for k in range(KD):
                    mm = pe.matmul(psum[:, c, :], w_ssm[:, k, c * P:(c + 1) * P], xT[:, k, :], start=(k == 0), stop=(k == KD - 1))
                mm.then_inc(full[c], 1)
            pe.wait_ge(wmla_in, 16)
            for t in range(TT):
                for k in range(KD):
                    mm = pe.matmul(psum[:, 4 + t, 0:MLA_COLS], xT[:, k, t * P:(t + 1) * P], w_mla[:, k, :], start=(k == 0), stop=(k == KD - 1))
                mm.then_inc(full[4 + t], 1)
            pe.wait_ge(L["lora_ready"], 1)
            for j in range(3):
                claim(pe, j, "front", 2)
                for t in range(TT):
                    mm = pe.transpose(psum[:, j, t * P:(t + 1) * P], lora[:, t, j * P:(j + 1) * P], ident)
                mm.then_inc(full[j], 1)
            for j in range(3):
                emptied(pe, j, "front", 2)
            pe.wait_ge(wuq_in, 32)

            with pe.Fori(0, 4) as c:
                par_w = c % 2
                pe.wait_ge(L["pads_ready"], at("pads_ready", "heads", 1, c))
                for i in range(4):
                    claim(pe, 6, "heads", i, c)
                    for j in range(4):
                        mm = pe.transpose(psum[:, 6, j * P:(j + 1) * P], pads[:, i, j * P:(j + 1) * P], ident)
                    mm.then_inc(full[6], 1)
                for hh in range(2):
                    h = 2 * c + hh
                    u4, u5, u6, us = BASE4[hh], BASE5[hh], BASE6[hh], 3 * hh
                    claim(pe, 4, "heads", u4, c)
                    for t in range(TT):
                        for k in range(2):
                            mm = pe.matmul(psum[:, 4, t * 96:(t + 1) * 96], loraT[:, k, t * P:(t + 1) * P],
                                           uq[:, k, bass.ds(h * 96, 96)], start=(k == 0), stop=(k == 1))
                    mm.then_inc(full[4], 1)
                    claim(pe, 5, "heads", u5, c)
                    for t in range(TT):
                        mm = pe.matmul(psum[:, 5, t * P:(t + 1) * P], loraT[:, 2, t * P:(t + 1) * P],
                                       ukv[:, bass.ds(h * P, P)], start=True, stop=True)
                    mm.then_inc(full[5], 1)
                    if hh == 0:
                        pe.wait_ge(L["wd_ready"], at("wd_ready", "heads", 1, c))
                    for i, b in enumerate((6, 4)):
                        claim(pe, b, "heads", (u6, u4 + 1)[i], c)
                        for t in (2 * i, 2 * i + 1):
                            for k in range(KD):
                                wv = wd[:, bass.ds(par_w, 1), k, :].rearrange("p a (s n) -> p (a s) n", s=3)[:, :, hh * 64:hh * 64 + 64]
                                mm = pe.matmul(psum[:, b, (t % 2) * 192:(t % 2) * 192 + 192].rearrange("p (s n) -> p s n", s=3),
                                               xT[:, k, t * P:(t + 1) * P], wv, start=(k == 0), stop=(k == KD - 1))
                        mm.then_inc(full[b], 1)
                    pe.wait_ge(L["q_ready"], at("q_ready", "heads", hh + 1, c))
                    claim(pe, 5, "heads", u5 + 1, c)
                    for t in range(TT):
                        mm = pe.transpose(psum[0:96, 5, t * P:(t + 1) * P], q_h[:, t, :], ident)
                    mm.then_inc(full[5], 1)
                    pe.wait_ge(L["kv_ready"], at("kv_ready", "heads", hh + 1, c))
                    claim(pe, 6, "heads", u6 + 1, c)
                    for t in range(TT):
                        mm = pe.transpose(psum[0:96, 6, t * P:(t + 1) * P], k_h[:, t, :], ident)
                    mm.then_inc(full[6], 1)

                    def scores(q, k, u):
                        for t in range(TT):
                            claim(pe, t, "heads", us + u, c)
                            pe.matmul(psum[:, t, 0:(t + 1) * P], q[:, t * P:(t + 1) * P], k[:, 0:(t + 1) * P],
                                      start=True, stop=True).then_inc(full[t], 1)

                    def gate_tile(t):
                        if t == 0:
                            pe.wait_ge(gw_in, h * 32 + 32)
                        b, u = gate_at(hh, t)
                        claim(pe, b, "heads", u, c)
                        dst = psum[:, b, 0:GATE_W]
                        for k in range(KD):
                            pe.matmul(dst, xT[:, k, t * P:(t + 1) * P], gw[:, k, :], start=(k == 0), stop=False)
                        pe.matmul(dst, ones[0:1, :], gb[0:1, :], start=False, stop=True).then_inc(full[b], 1)

                    def attend(p, v, first4, first5, last6, ready):
                        for t in range(TT):
                            b, u = (4, first4 + t // 2) if t % 2 == 0 else (5, first5 + t // 2)
                            ready(t)
                            claim(pe, b, "heads", u, c)
                            for kb in range(t + 1):
                                mm = pe.transpose(psum[:, b, kb * P:(kb + 1) * P], causal_part(p, t, kb * P, (kb + 1) * P), ident)
                            mm.then_inc(full[b], 1)
                        claim(pe, 6, "heads", last6, c)
                        for t in range(TT):
                            b, u = (4, first4 + t // 2) if t % 2 == 0 else (5, first5 + t // 2)
                            emptied(pe, b, "heads", u, c)
                            for kb in range(t + 1):
                                mm = pe.matmul(psum[:, 6, t * 64:(t + 1) * 64], causal_part(pT, t, kb * P, (kb + 1) * P), v(kb),
                                               start=(kb == 0), stop=(kb == t))
                        mm.then_inc(full[6], 1)

                    emptied(pe, 5, "heads", u5 + 1, c)
                    emptied(pe, 6, "heads", u6 + 1, c)
                    scores(qT[0:96, :], kT[0:96, :], 0)
                    pe.wait_ge(L["diff_ready"], at("diff_ready", "heads", hh + 1, c))
                    for i, b, u in ((0, 4, u4 + 2), (1, 5, u5 + 2)):
                        claim(pe, b, "heads", u, c)
                        pe.sem_inc(tick, 1)
                        for t in range(TT):
                            mm = pe.transpose(psum[0:64, b, t * P:(t + 1) * P], d_h[:, t, i * 64:(i + 1) * 64], ident)
                        mm.then_inc(full[b], 1)
                    for j in range(2):
                        for i in range(2):
                            claim(pe, 6, "heads", u6 + 2 + 2 * j + i, c)
                            if hh == 0 and j == 0 and i == 0:
                                emptied(pe, 6, "heads", 3, c)
                            tile = 2 * hh + j
                            pe.matmul(psum[:, 6, :], bT[:, i, tile * P:(tile + 1) * P], uT[:, bass.ds(c, 1), :].rearrange("p a n -> p (a n)"),
                                      start=True, stop=True).then_inc(full[6], 1)
                    gate_tile(0)
                    attend(p1, lambda kb: v_h[:, kb, :], u4 + 3, u5 + 4, u6 + 6,
                           lambda t: emptied(pe, t, "heads", us, c))
                    emptied(pe, 4, "heads", u4 + 2, c)
                    emptied(pe, 5, "heads", u5 + 2, c)
                    scores(dqT[0:32, :], dkT[0:32, :], 1)
                    gate_tile(1)
                    scores(dqT[32:64, :], dkT[32:64, :], 2)

                    def c_products(j):
                        tile = 2 * hh + j
                        pe.wait_ge(L["h_ready"], at("h_ready", "heads", tile + 1, c))
                        if tile == 0:
                            claim(pe, 7, "heads", 0, c)
                        for i in range(2):
                            mm = pe.matmul(psum[32 * tile:32 * tile + 32, 7, :], cT[:, i, tile, :], hst[:, tile % 2, i, :],
                                           start=(i == 0), stop=(i == 1))
                        mm.then_inc(L["h_used"], 1)

                    c_products(0)
                    gate_tile(2)
                    gate_tile(3)
                    attend(p1, lambda kb: d_h[:, kb, 128:192], u4 + 6, u5 + 7, u6 + 8,
                           lambda t: pe.wait_ge(L["mix_ready"], at("mix_ready", "heads", 4 * hh + t + 1, c)))
                    c_products(1)
                pe.wait_ge(L["oa_ready"], at("oa_ready", "heads", 2, c))
                claim(pe, 4, "heads", 16, c)
                for t in range(TT):
                    mm = pe.transpose(psum[:, 4, t * P:(t + 1) * P], oa_tok[:, t, :], ident)
                mm.then_inc(full[4], 1)

            for i in range(4):
                claim(pe, i, "join", 0)
                for t in range(TT):
                    pe.wait_ge(L["ob_ready"], at("ob_ready", "join", t + 1))
                    mm = pe.transpose(psum[:, i, t * P:(t + 1) * P], ob_tok[:, t, 2 * i:2 * i + 2, :].rearrange("p a b -> p (a b)"), ident)
                mm.then_inc(full[i], 1)
            for i in range(4):
                emptied(pe, i, "join", 0)
            emptied(pe, 4, "heads", 16, 3)
            pe.wait_ge(L["gelu_done"], at("gelu_done", "join", 1))

            with pe.Fori(0, 2) as n:
                for i in range(3):
                    pe.wait_ge(wy_in[i], n * 16 + 16)
                    if i == 2:
                        pe.wait_ge(wy_in[3], n * 16 + 16)
                    for t in range(TT):
                        tok = slice(t * P, (t + 1) * P)
                        b, u = t % 2, 2 * i + t // 2
                        src = (oaT, obT, yT)[i]
                        if i == 2:
                            claim(pe, 4 + b, "merge", t // 2, n)
                            for k in range(4):
                                mm = pe.matmul(psum[:, 4 + b, :], src[:, k, tok], wy[3][:, k, :], start=(k == 0), stop=(k == 3))
                            mm.then_inc(full[4 + b], 1)
                        claim(pe, 2 + b, "merge", u, n)
                        for k in range(4):
                            mm = pe.matmul(psum[:, 2 + b, :], src[:, k, tok], wy[i][:, k, :], start=(k == 0), stop=(k == 3))
                        mm.then_inc(full[2 + b], 1)

            for k in range(KD):
                claim(pe, k, "tail", 0)
                for t in range(TT):
                    pe.wait_ge(L["merged_ready"], at("merged_ready", "merge", 9 + t, 1))
                    mm = pe.transpose(psum[:, k, t * P:(t + 1) * P], merged[:, t, k * P:(k + 1) * P], ident)
                mm.then_inc(full[k], 1)
            for k in range(KD):
                emptied(pe, k, "tail", 0)
            pe.wait_ge(wo_in, 16)
            for t in range(TT):
                for n in range(2):
                    b = 2 * t + n
                    for k in range(KD):
                        mm = pe.matmul(psum[:, b, :], xT[:, k, t * P:(t + 1) * P], w_o[:, k, n * BANK:(n + 1) * BANK], start=(k == 0), stop=(k == KD - 1))
                    mm.then_inc(full[b], 1)
            for k in range(KD):
                claim(pe, k, "tail", 2)
                for t in range(TT):
                    pe.wait_ge(L["ln_ready"], at("ln_ready", "tail", t + 1))
                    mm = pe.transpose(psum[:, k, t * P:(t + 1) * P], x_tok[:, t, k * P:(k + 1) * P], ident)
                mm.then_inc(full[k], 1)
            for k in range(KD):
                emptied(pe, k, "tail", 2)
            for t in range(TT):
                for k in range(KD):
                    mm = pe.matmul(psum[:, 0, t * EXPERTS:(t + 1) * EXPERTS], xT[:, k, t * P:(t + 1) * P], router_w[:, k, :], start=(k == 0), stop=(k == KD - 1))
            mm.then_inc(full[0], 1)
            pe.wait_ge(pick_ready, 1)
            for t in range(TT + 1):
                for s in range(min(t, TT - 1) + 1):
                    lhs = const("upper") if s == t else ones
                    mm = pe.matmul(psum[:, 1, t * EXPERTS:(t + 1) * EXPERTS], lhs, chosen[:, s, :], start=(s == 0), stop=(s == min(t, TT - 1)))
            mm.then_inc(full[1], 1)
            meet(pe, "moe")
            most_chosen = pe.value_load(most[0:1, 0:1], min_val=0, max_val=SEQ)
            with pe.Fori(0, PASSES) as ps:
                with pe.If(most_chosen > ps * SLOTS):
                    meet(pe, "pass")

                    def bank(stage):
                        return psum[:, ebank[stage], :]

                    def indices(q, par):
                        pe.wait_ge(sel_ready, q + 1)
                        for t in range(TT):
                            mm = pe.matmul(bank("idx")[:, 8 * par:8 * par + 4], sel[par][:, t].rearrange("p a b -> p (a b)"),
                                           payload[:, t, bass.ds(2 * q, 2), :].rearrange("p a b -> p (a b)"), start=(t == 0), stop=(t == TT - 1))
                        mm.then_inc(efull["idx"], 1)

                    def turn_x(q, par, landings):
                        pe.wait_ge(gathered[par], landings)
                        for i, stage in enumerate(("x0", "x1")):
                            pe.wait_ge(efree[stage], q + 1)
                            for j in range(4):
                                k = 4 * i + j
                                mm = pe.transpose(bank(stage)[:, j * P:(j + 1) * P], xg[par][:, k * P:(k + 1) * P], ident)
                            mm.then_inc(efull[stage], 1)

                    def product(stage, lhs, chunks, w, cols):
                        for k in range(chunks):
                            for i in range(2):
                                half = slice(i * SLOTS, (i + 1) * SLOTS)
                                mm = pe.matmul(psum[half, ebank[stage], :], lhs[:, k, half], w[i][:, k, cols],
                                               start=(k == 0), stop=(k == chunks - 1))
                        mm.then_inc(efull[stage], 1)

                    indices(0, 0)
                    turn_x(0, 0, 16)
                    with pe.Fori(0, PAIRS // 2) as two:
                        for par in range(2):
                            q = two * 2 + par
                            pe.wait_ge(efree["idx"], q + 1)
                            indices(q + 1, 1 - par)
                            for stage, w, landed in (("gate", e_gate, eg_in), ("up", e_up, eu_in)):
                                for i in range(2):
                                    pe.wait_ge(landed[i], q * 16 + 16)
                                if stage == "gate":
                                    pe.wait_ge(efree["x0"], q + 2)
                                    pe.wait_ge(efree["x1"], q + 2)
                                pe.wait_ge(efree[stage], q + 1)
                                product(stage, xgT, KD, w, slice(0, FF))
                            turn_x(q + 1, 1 - par, two * 16 + 16 + 16 * par)
                            pe.wait_ge(he_ready, q + 1)
                            pe.wait_ge(efree["h"], q + 1)
                            for j in range(KF):
                                mm = pe.transpose(bank("h")[:, j * P:(j + 1) * P], h_e[:, j * P:(j + 1) * P], ident)
                            mm.then_inc(efull["h"], 1)
                            for i in range(2):
                                pe.wait_ge(ed_in[i], q * 16 + 16)
                            pe.wait_ge(efree["h"], q + 2)
                            for n in range(2):
                                pe.wait_ge(efree[f"y{n}"], q + 1)
                                product(f"y{n}", hT, KF, e_down, slice(n * BANK, (n + 1) * BANK))
                    meet(pe, "passed")
                pe.sem_inc(tick, 1)
            meet(pe, "end")

    @block.scalar
    def _(act):
        ch = Chain(act, chains["act"])
        copy = lambda o, i: act.copy(o, i)
        act.wait_ge(setup_ang, 1)
        act.activation(rope_sc[:, 1], rope_ang[:, 0], ACT.Sin).then_inc(setup_trig, 1)
        act.activation(rope_sc[:, 0], rope_ang[:, 1], ACT.Sin, bias=half_pi, scale=-1.0).then_inc(setup_trig, 1)
        with act.Fori(0, DEPTH) as l:
            meet(act, "layer")
            ch.reset()
            for k in range(0, KD, 2):
                filled(act, k, "front", 0)
                copy(xT[:, k, :], psum[:, k, :]).then_inc(free[k], 1)
            act.wait_ge(small_in, 224)
            act.activation(dt_, dt_, ACT.Exp).then_inc(dt_ready, 1)
            act.wait_ge(lam_ready, 1)
            act.activation(lam[:, 0:2], lam[:, 2:4], ACT.Exp).then_inc(lam_exp, 1)
            for c in range(4):
                filled(act, c, "front", 1)
                copy(uT[:, c, :], psum[:, c, :]).then_inc(free[c], 1)
            for t in range(TT):
                filled(act, 4 + t, "front", 1)
                for i, (a, b) in enumerate(((0, Q_LORA), (Q_LORA, Q_LORA + KV_LORA))):
                    ch.then(act.activation(sqs[:, 0:b - a], psum[:, 4 + t, a:b], ACT.Square, accum_out=ssum[:, t, i:i + 1]))
            act.sem_inc(tick, 1)
            act.drain().then_inc(L["sq_sums"], 1)
            act.wait_ge(L["rms_mean"], 1)
            act.activation(rrt, rrt, ACT.Sqrt).then_inc(L["rms_root"], 1)
            act.wait_ge(ang_ready, 1)
            for an, tab in ((ang, fine), (angc, coarse)):
                flat = tab.rearrange("p s a b -> p s (a b)")
                ch.add(act.activation(an[:, 1], an[:, 0], ACT.Abs))
                ch.wait()
                ch.add(act.activation(flat[:, 1], an[:, 0], ACT.Sin, scale=TWO_PI))
                ch.add(act.activation(flat[:, 0], an[:, 1], ACT.Sin, bias=half_pi, scale=-TWO_PI))
            act.drain().then_inc(trig_ready, 1)
            for j in range(3):
                filled(act, j, "front", 2)
                copy(loraT[:, j, :], psum[:, j, :]).then_inc(free[j], 1)

            with act.Fori(0, 4) as c:
                ch.reset()
                for i in range(2):
                    filled(act, 6, "heads", i, c)
                    copy(bT[:, i, :], psum[:, 6, :]).then_inc(free[6], 1)
                for i in range(2):
                    filled(act, 6, "heads", 2 + i, c)
                    for j in range(4):
                        ins = copy(cT[:, i, j, :], psum[:, 6, j * 160:j * 160 + 32])
                        if j < 3:
                            ch.add(ins)
                    ins.then_inc(free[6], 1)
                for hh in range(2):
                    u4, u5, u6, us = BASE4[hh], BASE5[hh], BASE6[hh], 3 * hh
                    filled(act, 5, "heads", u5, c)
                    kv = psum[:, 5, :].rearrange("p (t n) -> p t n", t=TT)
                    if hh == 0:
                        act.wait_ge(krope_ready, 1)
                    ch.add(copy(k_h[:, :, 0:NOPE], kv[:, :, 0:NOPE]))
                    ch.add(copy(k_h[:, :, NOPE:96], krope))
                    copy(v_h, kv[:, :, NOPE:P]).then_inc(free[5], 1)
                    act.drain().then_inc(L["kv_ready"], 1)
                    for i, b in enumerate((6, 4)):
                        filled(act, b, "heads", (u6, u4 + 1)[i], c)
                        copy(d_h[:, 2 * i:2 * i + 2, :], psum[:, b, 0:384].rearrange("p (t n) -> p t n", t=2)).then_inc(free[b], 1)
                    act.drain().then_inc(L["diff_copied"], 1)
                    filled(act, 5, "heads", u5 + 1, c)
                    copy(qT[0:96, :], psum[0:96, 5, :]).then_inc(free[5], 1)
                    filled(act, 4, "heads", u4 + 2, c)
                    copy(dqT[0:64, :], psum[0:64, 4, :]).then_inc(free[4], 1)

                    def take_bu(j):
                        tile = 2 * hh + j
                        for i in range(2):
                            filled(act, 6, "heads", u6 + 2 + 2 * j + i, c)
                            copy(bu[:, tile % 2, i, :], psum[:, 6, :]).then_inc(free[6], 1)

                    def exps(n, p, scale):
                        act.wait_ge(L["max_ready"], at("max_ready", "heads", us + n + 1, c))
                        for t in range(TT):
                            act.activation(causal_part(p, t), psum[:, t, 0:(t + 1) * P], ACT.Exp, bias=soft[:, n, t:t + 1],
                                           scale=scale, accum_out=soft[:, 3 + n, t:t + 1]).then_inc(free[t], 1)

                    def take_p(b, u, t):
                        filled(act, b, "heads", u, c)
                        copy(causal_part(pT, t), psum[:, b, 0:(t + 1) * P]).then_inc(free[b], 1)

                    def take_gate(t):
                        b, u = gate_at(hh, t)
                        filled(act, b, "heads", u, c)
                        act.wait_ge(L["gate_room"], at("gate_room", "heads", 4 * hh + t - 1, c))
                        act.activation(gout[:, t % 2, :], psum[:, b, 0:GATE_W], ACT.Sigmoid).then_inc(free[b], 1)

                    take_bu(0)
                    exps(0, p1, SCALE_A)
                    take_bu(1)
                    take_gate(0)
                    for t in range(TT):
                        take_p(4 + t % 2, (u4 + 3, u5 + 4)[t % 2] + t // 2, t)
                    exps(1, p1, SCALE_B)
                    take_gate(1)
                    exps(2, p2, SCALE_B)
                    take_gate(2)
                    take_gate(3)
                    filled(act, 6, "heads", u6 + 6, c)
                    for t in (1, 3):
                        take_p(5, u5 + 7 + t // 2, t)
                filled(act, 4, "heads", 16, c)
                act.wait_ge(x_saved, 16)
                copy(oaT[:, bass.ds(c, 1), :].rearrange("p a n -> p (a n)"), psum[:, 4, :]).then_inc(free[4], 1)

            ch.reset()
            act.wait_ge(L["rms_mean"], at("rms_mean", "join", 1))
            act.activation(ms_b, ms_b, ACT.Sqrt).then_inc(L["rms_root"], 1)
            act.wait_ge(L["y_ready"], at("y_ready", "join", 0))
            act.activation(yT, yT, ACT.Gelu_apprx_tanh).then_inc(L["gelu_done"], 1)

            with act.Fori(0, 2) as n:
                for t in range(TT):
                    b = t % 2
                    filled(act, 4 + b, "merge", t // 2, n)
                    act.wait_ge(L["merged_ready"], at("merged_ready", "merge", 7 + t, n))
                    act.activation(sg[:, b, :], psum[:, 4 + b, :], ACT.Sigmoid).then_inc(free[4 + b], 1)

            def roots(st, phase):
                for t in range(TT):
                    act.wait_ge(L["ln_var"], at("ln_var", phase, t + 1))
                    act.activation(st[:, t, 14:15], st[:, t, 13:14], ACT.Sqrt).then_inc(L["ln_root"], 1)

            for k in range(0, KD, 2):
                filled(act, k, "tail", 0)
                copy(xT[:, k, :], psum[:, k, :]).then_inc(free[k], 1)
            roots(ln_st, "tail")
            for k in range(0, KD, 2):
                filled(act, k, "tail", 2)
                copy(xT[:, k, :], psum[:, k, :]).then_inc(free[k], 1)
            filled(act, 0, "tail", 3)
            act.activation(sc, psum[:, 0, 0:TT * EXPERTS].rearrange("p (t e) -> p t e", t=TT), ACT.Sigmoid).then_inc(free[0], 1)
            meet(act, "moe")
            most_chosen = act.value_load(most[0:1, 0:1], min_val=0, max_val=SEQ)
            with act.Fori(0, PASSES) as ps:
                with act.If(most_chosen > ps * SLOTS):
                    meet(act, "pass")

                    def take_x(q):
                        act.wait_ge(efull["x0"], q + 1)
                        copy(xgT[:, 0:4, :].rearrange("p a b -> p (a b)"), psum[:, ebank["x0"], :]).then_inc(efree["x0"], 1)

                    take_x(0)
                    with act.Fori(0, PAIRS // 2) as two:
                        for par in range(2):
                            q = two * 2 + par
                            act.wait_ge(efull["gate"], q + 1)
                            act.wait_ge(efree["up"], q + 1)
                            act.activation(silu, psum[:, ebank["gate"], :], ACT.Silu).then_inc(efree["gate"], 1)
                            take_x(q + 1)
                            act.wait_ge(efull["h"], q + 1)
                            copy(hT.rearrange("p a b -> p (a b)"), psum[:, ebank["h"], :]).then_inc(efree["h"], 1)
                            act.wait_ge(efull["y0"], q + 1)
                            act.wait_ge(scattered[par], two * 16 + 16)
                            copy(yb[par][:, 0:BANK], psum[:, ebank["y0"], :]).then_inc(efree["y0"], 1)
                    meet(act, "passed")
                act.sem_inc(tick, 1)
            roots(ln2_st, "last")
            meet(act, "end")

    @block.vector
    def _(v):
        ch = Chain(v, chains["dve"])
        tt, ts, stt = v.tensor_tensor, v.tensor_scalar, v.scalar_tensor_tensor
        v.wait_ge(setup_in, 80)
        ch.then(v.tensor_copy(rope_pos, pos_i[:]))
        ch.then(tt(rope_ang[:, 0], S3(rope_pos.unsqueeze(2), P, TT, 20), S3(const("inv").unsqueeze(1), P, TT, 20), ALU.mult))
        ch.then(ts(rope_ang[:, 1], rope_ang[:, 0], 1 / TWO_PI, ROUND, ALU.mult, ALU.add))
        ch.then(ts(rope_ang[:, 1], rope_ang[:, 1], -ROUND, None, ALU.add))
        ch.then(stt(out=rope_ang[:, 0], in0=rope_ang[:, 1], scalar=-PI_HI, in1=rope_ang[:, 0], op0=ALU.mult, op1=ALU.add))
        ch.then(stt(out=rope_ang[:, 0], in0=rope_ang[:, 1], scalar=-PI_LO, in1=rope_ang[:, 0], op0=ALU.mult, op1=ALU.add))
        ch.then(ts(rope_ang[:, 0], rope_ang[:, 0], PI_MAX, -PI_MAX, ALU.min, ALU.max))
        ch.then(ts(rope_ang[:, 1], rope_ang[:, 0], -1.0, None, ALU.mult))
        ch.then(tt(rope_ang[:, 1], rope_ang[:, 1], rope_ang[:, 0], ALU.max))
        v.memset(half_pi, math.pi / 2).then_inc(setup_ang, 1)
        v.wait_ge(setup_trig, 2)
        for tab, i in (((cc_a, cc_b), 0), ((ss_a, ss_b), 1)):
            for s in range(2):
                ch.add(v.tensor_copy(tab[0][:, :, s, :], rope_sc[:, i, :, 0:16]))
                ch.add(v.tensor_copy(tab[1][:, :, 4 * s:4 * s + 4], rope_sc[:, i, :, 16:20]))
        for i in range(2):
            ch.add(v.memset(xg[i], 0.0))
        with v.Fori(0, DEPTH) as l:
            meet(v, "layer")
            ch.reset()
            for k in range(1, KD, 2):
                filled(v, k, "front", 0)
                v.tensor_copy(xT[:, k, :], psum[:, k, :]).then_inc(free[k], 1)
            v.wait_ge(small_in, 224)
            ch.then(tt(rtmp[:, 0, 0:2, :], lam_in[:, 0:4:2, :], lam_in[:, 1:4:2, :], ALU.mult))
            v.tensor_reduce(lam[:, 2:4], rtmp[:, 0, 0:2, :], AXX, ALU.add).then_inc(lam_ready, 1)
            ch.add(tt(sm[:, 14], a_re, a_re, ALU.mult))
            ch.then(tt(sm[:, 15], a_im, a_im, ALU.mult))
            ch.then(tt(sm[:, 14], sm[:, 14], sm[:, 15], ALU.add))
            v.reciprocal(inv_a, sm[:, 14]).then_inc(inv_ready, 1)
            ts(subln, subln, lyr[:, 1:2], None, ALU.mult).then_inc(subln_ready, 1)
            v.wait_ge(lam_exp, 1)
            ch.then(tt(lam[:, 2:3], lam[:, 0:1], lam[:, 1:2], ALU.subtract))
            ch.then(tt(lam[:, 0:1], lam[:, 2:3], lyr[:, 0:1], ALU.add))
            v.wait_ge(L["sq_sums"], 1)
            ch.add(ts(rrt[:, :, 0:1], ssum[:, :, 0:1], 1 / Q_LORA, RMS_EPS, ALU.mult, ALU.add))
            ch.then(ts(rrt[:, :, 1:2], ssum[:, :, 1:2], 1 / KV_LORA, RMS_EPS, ALU.mult, ALU.add))
            v.sem_inc(L["rms_mean"], 1)
            v.wait_ge(L["rms_root"], 1)
            ch.then(v.reciprocal(ssum, rrt))
            for t in range(TT):
                ch.add(stt(out=lora[:, t, 0:Q_LORA], in0=psum[:, 4 + t, 0:Q_LORA], scalar=ssum[:, t, 0:1], in1=qn_bc, op0=ALU.mult, op1=ALU.mult))
                ch.add(stt(out=lora[:, t, Q_LORA:384], in0=psum[:, 4 + t, Q_LORA:384], scalar=ssum[:, t, 1:2], in1=kvn_bc, op0=ALU.mult, op1=ALU.mult))
            kr = psum[:, 4:8, 384:416]
            ch.add(tt(rtmp[:, 0], kr, cc_a.rearrange("p t a b -> p t (a b)"), ALU.mult))
            ch.then(tt(rtmp[:, 1], kr, ss_a.rearrange("p t a b -> p t (a b)"), ALU.mult))
            for t in range(TT):
                v.sem_inc(free[4 + t], 1)
            v.sem_inc(L["lora_ready"], 1)
            ch.add(tt(krope[:, :, 0:16], rtmp[:, 0, :, 0:16], rtmp[:, 1, :, 16:32], ALU.subtract))
            ch.then(tt(krope[:, :, 16:32], rtmp[:, 0, :, 16:32], rtmp[:, 1, :, 0:16], ALU.add))
            v.sem_inc(krope_ready, 1)

            with v.Fori(0, 4) as c:
                ch.reset()
                for hh in range(2):
                    u4, u5, u6, us = BASE4[hh], BASE5[hh], BASE6[hh], 3 * hh
                    filled(v, 4, "heads", u4, c)
                    q = psum[:, 4, 0:384].rearrange("p (t n) -> p t n", t=TT)
                    t0, t1 = (tmp_h[:, i].rearrange("p (t n) -> p t n", t=TT) for i in range(2))
                    ch.add(v.tensor_copy(q_h[:, :, 0:NOPE], q[:, :, 0:NOPE]))
                    ch.add(tt(t0, q[:, :, NOPE:96], cc_a.rearrange("p t a b -> p t (a b)"), ALU.mult))
                    ch.then(tt(t1, q[:, :, NOPE:96], ss_a.rearrange("p t a b -> p t (a b)"), ALU.mult))
                    v.sem_inc(free[4], 1)
                    ch.add(tt(q_h[:, :, 64:80], t0[:, :, 0:16], t1[:, :, 16:32], ALU.subtract))
                    ch.then(tt(q_h[:, :, 80:96], t0[:, :, 16:32], t1[:, :, 0:16], ALU.add))
                    v.sem_inc(L["q_ready"], 1)
                    v.wait_ge(L["diff_copied"], at("diff_copied", "heads", hh + 1, c))
                    dq = d_h[:, :, 0:128].rearrange("p t (s n) -> p t s n", n=HD)
                    t2, t3 = (tmp_h[:, 2 + i].rearrange("p (t s n) -> p t s n", t=TT, n=8) for i in range(2))
                    ch.add(tt(t2, dq[:, :, :, 0:8], S3(cc_b.unsqueeze(2), P, TT, 4, 8), ALU.mult))
                    ch.then(tt(t3, dq[:, :, :, 0:8], S3(ss_b.unsqueeze(2), P, TT, 4, 8), ALU.mult))
                    ch.add(tt(dq[:, :, :, 0:4], t2[:, :, :, 0:4], t3[:, :, :, 4:8], ALU.subtract))
                    ch.then(tt(dq[:, :, :, 4:8], t2[:, :, :, 4:8], t3[:, :, :, 0:4], ALU.add))
                    v.sem_inc(L["diff_ready"], 1)
                    filled(v, 6, "heads", u6 + 1, c)
                    v.tensor_copy(kT[0:96, :], psum[0:96, 6, :]).then_inc(free[6], 1)

                    def maxima(n, scale):
                        for t in range(TT):
                            filled(v, t, "heads", us + n, c)
                            d = psum[:, t, t * P:(t + 1) * P]
                            ch.add(tt(d, d, const("causal"), ALU.add))
                        ch.wait()
                        for t in range(TT):
                            ch.add(v.tensor_reduce(soft[:, 6 + n, t:t + 1], psum[:, t, 0:(t + 1) * P], AXX, ALU.max))
                        ch.wait()
                        ch.then(ts(soft[:, n, :], soft[:, 6 + n, :], -scale, None, ALU.mult))
                        v.sem_inc(L["max_ready"], 1)

                    def scans(j):
                        tile = 2 * hh + j
                        v.wait_ge(L["rot_ready"], at("rot_ready", "heads", tile + 1, c))
                        emptied(v, 6, "heads", u6 + 3 + 2 * j, c)
                        cos, sin, br, bi = rot[:, tile % 2, 0], rot[:, tile % 2, 1], bu[:, tile % 2, 0], bu[:, tile % 2, 1]
                        ch.add(tt(xab[:, 0], br, cos, ALU.mult))
                        ch.then(tt(xab[:, 1], bi, sin, ALU.mult))
                        ch.add(tt(xab[:, 0], xab[:, 0], xab[:, 1], ALU.add))
                        ch.add(tt(bi, bi, cos, ALU.mult))
                        ch.then(tt(br, br, sin, ALU.mult))
                        ch.then(tt(bi, bi, br, ALU.subtract))
                        if tile > 0:
                            v.wait_ge(L["g_used"], at("g_used", "heads", tile, c))
                        r = S3(radius[:, bass.ds(4 * c + tile, 1)], P, SEQ)
                        for i in range(2):
                            ch.add(v.tensor_tensor_scan(gsc[:, i, :], r, (xab[:, 0], bi)[i], 0.0, ALU.mult, ALU.add))
                        ch.wait()
                        v.sem_inc(L["scan_ready"], 1)

                    maxima(0, SCALE_A)
                    filled(v, 5, "heads", u5 + 2, c)
                    v.tensor_copy(dkT[0:64, :], psum[0:64, 5, :]).then_inc(free[5], 1)
                    scans(0)
                    emptied(v, 3, "heads", us, c)
                    ch.then(v.reciprocal(soft[:, 9, :], soft[:, 3, :]))
                    filled(v, 6, "heads", u6 + 6, c)
                    ch.then(tt(oa_tok[:, :, hh * 64:hh * 64 + 64], psum[:, 6, 0:256].rearrange("p (t n) -> p t n", t=TT),
                               S3(soft[:, 9, :].unsqueeze(2), P, TT, 64), ALU.mult))
                    v.sem_inc(free[6], 1)
                    v.sem_inc(L["oa_ready"], 1)
                    maxima(1, SCALE_B)
                    maxima(2, SCALE_B)
                    scans(1)
                    emptied(v, 3, "heads", us + 2, c)
                    ch.then(v.reciprocal(soft[:, 9:11, :], soft[:, 4:6, :]))
                    ch.then(ts(soft[:, 11, :], soft[:, 10, :], lam[:, 0:1], None, ALU.mult))
                    for t in range(TT):
                        w = (t + 1) * P
                        ch.then(ts(causal_part(p2, t), causal_part(p2, t), soft[:, 11, t:t + 1], None, ALU.mult))
                        ch.then(stt(out=causal_part(p1, t), in0=causal_part(p1, t), scalar=soft[:, 9, t:t + 1], in1=causal_part(p2, t), op0=ALU.mult, op1=ALU.subtract))
                        v.sem_inc(L["mix_ready"], 1)
                    for t in (0, 2):
                        filled(v, 4, "heads", u4 + 6 + t // 2, c)
                        v.tensor_copy(causal_part(pT, t), psum[:, 4, 0:(t + 1) * P]).then_inc(free[4], 1)
                    filled(v, 6, "heads", u6 + 8, c)
                    o = psum[:, 6, 0:256].rearrange("p (t n) -> p t n", t=TT)
                    ob = ob_tok[:, :, bass.ds(2 * c + hh, 1), :].rearrange("p t a n -> p t (a n)")
                    ch.then(v.tensor_copy(tmp_o, o))
                    v.sem_inc(free[6], 1)
                    ch.add(v.tensor_copy(ob, tmp_o))
                    t4 = tmp_h[:, 0:2].rearrange("p a (t n) -> p (a t) n", t=2)
                    ch.then(tt(t4, tmp_o, tmp_o, ALU.mult))
                    ch.then(v.tensor_reduce(ms_b[:, :, bass.ds(2 * c + hh, 1)].rearrange("p t a -> p (t a)"), t4, AXX, ALU.add))
                v.wait_ge(L["h_used"], at("h_used", "heads", 4, c))
                yc, uc = (a[:, bass.ds(c, 1), :].rearrange("p a n -> p (a n)") for a in (yT, uT))
                ch.then(stt(out=yc, in0=uc, scalar=d_col[:, bass.ds(c, 1)], in1=psum[:, 7, :], op0=ALU.mult, op1=ALU.add))
                v.sem_inc(free[7], 1)
                v.sem_inc(L["y_ready"], 1)

            ch.reset()
            ch.then(ts(ms_b, ms_b, 1 / 64, SUB_EPS, ALU.mult, ALU.add))
            v.sem_inc(L["rms_mean"], 1)
            v.wait_ge(L["rms_root"], at("rms_root", "join", 1))
            ch.then(v.reciprocal(ms_b, ms_b))
            for t in range(TT):
                ch.then(tt(ob_tok[:, t], ob_tok[:, t], S3(ms_b[:, t, :].unsqueeze(2), P, HEADS, 64), ALU.mult))
                ch.then(tt(ob_tok[:, t], ob_tok[:, t], S3(subln.unsqueeze(1), P, HEADS, 64), ALU.mult))
                v.sem_inc(L["ob_ready"], 1)
            for i in range(4):
                filled(v, i, "join", 0)
                v.tensor_copy(obT[:, i, :], psum[:, i, :]).then_inc(free[i], 1)

            with v.Fori(0, 2) as n:
                ch.reset()
                for i in range(3):
                    for t in range(TT):
                        b, u = t % 2, 2 * i + t // 2
                        m = merged[:, t, bass.ds(n * BANK, BANK)]
                        gate = gates[:, t, bass.ds(n * BANK + i * D_MODEL, BANK)]
                        if t == 0:
                            v.wait_ge(gates_in[i], 16)
                        filled(v, 2 + b, "merge", u, n)
                        if i == 0:
                            ch.then(tt(m, gate, psum[:, 2 + b, :], ALU.mult))
                            v.sem_inc(free[2 + b], 1)
                        elif i == 1:
                            ch.then(tt(mtmp, gate, psum[:, 2 + b, :], ALU.mult))
                            v.sem_inc(free[2 + b], 1)
                            ch.then(tt(m, m, mtmp, ALU.add))
                        else:
                            emptied(v, 4 + b, "merge", t // 2, n)
                            ch.then(tt(mtmp, sg[:, b, :], psum[:, 2 + b, :], ALU.mult))
                            v.sem_inc(free[2 + b], 1)
                            ch.then(tt(mtmp, mtmp, gate, ALU.mult))
                            ch.then(tt(m, m, mtmp, ALU.add))
                        v.sem_inc(L["merged_ready"], 1)

            def layernorm(st, g, b, t, phase):
                x = x_tok[:, t, :]
                for i in range(2):
                    ch.add(v.bn_stats(st[:, t, 6 * i:6 * i + 6], x[:, i * BANK:(i + 1) * BANK]))
                ch.wait()
                ch.then(v.bn_aggr(st[:, t, 12:14], st[:, t, 0:12]))
                ch.then(ts(st[:, t, 13:14], st[:, t, 13:14], LN_EPS, None, ALU.add))
                v.sem_inc(L["ln_var"], 1)
                v.wait_ge(L["ln_root"], at("ln_root", phase, t + 1))
                ch.then(v.reciprocal(st[:, t, 15:16], st[:, t, 14:15]))
                ch.then(ts(x, x, st[:, t, 12:13], st[:, t, 15:16], ALU.subtract, ALU.mult))
                ch.then(tt(x, x, g, ALU.mult))
                ch.then(tt(x, x, b, ALU.add))
                v.sem_inc(L["ln_ready"], 1)

            ch.reset()
            for k in range(1, KD, 2):
                filled(v, k, "tail", 0)
                v.tensor_copy(xT[:, k, :], psum[:, k, :]).then_inc(free[k], 1)
            v.wait_ge(x_back, 16)
            v.wait_ge(ln_in, 32)
            for t in range(TT):
                for n in range(2):
                    filled(v, 2 * t + n, "tail", 1)
                    xs = x_tok[:, t, n * BANK:(n + 1) * BANK]
                    ch.then(stt(out=xs, in0=xs, scalar=ALPHA, in1=psum[:, 2 * t + n, :], op0=ALU.mult, op1=ALU.add))
                    v.sem_inc(free[2 * t + n], 1)
                layernorm(ln_st, ln_g, ln_b, t, "tail")
            for k in range(1, KD, 2):
                filled(v, k, "tail", 2)
                v.tensor_copy(xT[:, k, :], psum[:, k, :]).then_inc(free[k], 1)
            emptied(v, 0, "tail", 3)
            E4 = lambda a: a.rearrange("p t (g j) -> p t g j", j=EPER)
            r0, r1, r2, r3, r4, r5 = (rt[:, i].rearrange("p (t e) -> p t e", t=TT) for i in range(6))
            g0, g1, g2, g3 = (r[:, :, 0:8] for r in (r0, r1, r2, r3))
            g4, g5 = r4[:, :, 0:8], r4[:, :, 8:16]
            ch.then(tt(bs, sc, S3(router_b.unsqueeze(1), P, TT, EXPERTS), ALU.add))
            a, b, c_, d = (E4(bs)[:, :, :, j] for j in range(4))
            ch.add(tt(g0, a, b, ALU.max))
            ch.add(tt(g1, a, b, ALU.min))
            ch.add(tt(g2, c_, d, ALU.max))
            ch.then(tt(g3, c_, d, ALU.min))
            ch.add(tt(g4, g0, g2, ALU.max))
            ch.add(tt(g5, g0, g2, ALU.min))
            ch.then(tt(g1, g1, g3, ALU.max))
            ch.then(tt(g5, g5, g1, ALU.max))
            ch.then(tt(g0, g4, g5, ALU.add))

            def first_best(values, prio, width, val, tmp, onehot):
                ch.then(v.tensor_reduce(val, values, AXX, ALU.max))
                ch.then(tt(tmp, values, S3(val.unsqueeze(2), P, TT, width), ALU.is_equal))
                ch.then(tt(tmp, tmp, S3(prio.unsqueeze(1), P, TT, width), ALU.mult))
                ch.then(v.tensor_reduce(val, tmp, AXX, ALU.max))
                ch.then(tt(onehot, tmp, S3(val.unsqueeze(2), P, TT, width), ALU.is_equal))

            first_best(g0, const("gprio"), 8, rs[:, 0], g1, g2)
            group = S3(g2.unsqueeze(3), P, TT, EGROUPS, EPER)
            ch.add(tt(E4(r3), E4(bs), group, ALU.mult))
            ch.wait()
            ch.then(ts(g1, g2, -1.0, -NEG, ALU.add, ALU.mult))
            ch.then(tt(E4(r3), E4(r3), S3(g1.unsqueeze(3), P, TT, EGROUPS, EPER), ALU.add))
            first_best(r3, const("eprio"), EXPERTS, rs[:, 1], r4, oh1)
            ch.then(stt(out=r3, in0=oh1, scalar=2 * NEG, in1=r3, op0=ALU.mult, op1=ALU.add))
            first_best(r3, const("eprio"), EXPERTS, rs[:, 2], r4, oh2)
            ch.then(tt(chosen, oh1, oh2, ALU.add))
            v.sem_inc(pick_ready, 1)
            for i, oh in enumerate((oh1, oh2)):
                ch.then(tt(r3, oh, sc, ALU.mult))
                ch.then(v.tensor_reduce(rs[:, 3 + i], r3, AXX, ALU.add))
            ch.then(tt(rs[:, 5], rs[:, 3], rs[:, 4], ALU.add))
            ch.then(v.reciprocal(rs[:, 6], rs[:, 5]))
            for i in range(2):
                ch.add(tt(w_tok[:, i], rs[:, 3 + i], rs[:, 6], ALU.mult))
            ch.add(v.memset(payload, 0.0))
            ch.add(v.memset(slot_of, -1.0))
            ch.add(v.tensor_copy(slots_now, const("slot")))
            ch.then(ts(rs[:, 7], const("tok"), -FAR, None, ALU.add))
            ch.add(ts(payload[:, :, 0:EXPERTS, 0], S3(rs[:, 7].unsqueeze(2), P, TT, EXPERTS), 1.0, None, ALU.mult))
            ch.then(ts(rs[:, 0], const("tok"), 2.0, -FAR, ALU.mult, ALU.add))
            ch.then(tt(payload[:, :, 0:EXPERTS, 1], S3(rs[:, 0].unsqueeze(2), P, TT, EXPERTS), oh2, ALU.add))
            filled(v, 1, "tail", 3)
            before = psum[:, 1, 0:TT * EXPERTS].rearrange("p (t e) -> p t e", t=TT)
            ch.then(stt(out=r3, in0=before, scalar=1.0, in1=chosen, op0=ALU.add, op1=ALU.mult))
            ch.add(ts(slot_of[:, :, 0:EXPERTS], r3, -1.0, None, ALU.add))
            ch.then(v.tensor_reduce(rs[:, 1, 0:1], psum[:, 1, TT * EXPERTS:(TT + 1) * EXPERTS], AXX, ALU.max))
            ch.then(v.tensor_copy(most[:], rs[:, 1, 0:1]))
            v.sem_inc(free[1], 1)
            meet(v, "moe")
            most_chosen = v.value_load(most[0:1, 0:1], min_val=0, max_val=SEQ)
            with v.Fori(0, PASSES) as ps:
                with v.If(most_chosen > ps * SLOTS):
                    meet(v, "pass")

                    def select(q, par):
                        tt(sel[par], S3(slots_now.unsqueeze(1).unsqueeze(1), P, TT, 2, SLOTS),
                           S3(slot_of[:, :, bass.ds(2 * q, 2)].unsqueeze(3), P, TT, 2, SLOTS), ALU.is_equal).then_inc(sel_ready, 1)

                    def take_rows(q, par, column, rows_to):
                        for i in range(2):
                            half, at_ = slice(i * SLOTS, (i + 1) * SLOTS), 8 * par + 2 * i + column
                            ins = ts(rows_to[par][half, :], psum[half, ebank["idx"], at_:at_ + 1], FAR, None, ALU.add)
                            if i == 0:
                                ins.then_inc(tick, 1)
                        return ins

                    def take_x(q):
                        v.wait_ge(efull["x1"], q + 1)
                        v.tensor_copy(xgT[:, 4:8, :].rearrange("p a b -> p (a b)"), psum[:, ebank["x1"], :]).then_inc(efree["x1"], 1)

                    select(0, 0)
                    v.wait_ge(efull["idx"], 1)
                    take_rows(0, 0, 0, row_x).then_inc(rows_ready, 1)
                    take_x(0)
                    with v.Fori(0, PAIRS // 2) as two:
                        for par in range(2):
                            q = two * 2 + par
                            select(q + 1, 1 - par)
                            v.wait_ge(efull["idx"], q + 2)
                            take_rows(q + 1, 1 - par, 0, row_x).then_inc(rows_ready, 1)
                            v.wait_ge(efree["gate"], q + 2)
                            v.wait_ge(efull["up"], q + 1)
                            tt(h_e, silu, psum[:, ebank["up"], :], ALU.mult).then_inc(he_ready, 1)
                            v.wait_ge(he_ready, q + 1)
                            v.sem_inc(efree["up"], 1)
                            take_x(q + 1)
                            v.wait_ge(scattered[par], two * 16 + 16)
                            take_rows(q, par, 1, row_y).then_inc(efree["idx"], 1)
                            v.wait_ge(efull["y1"], q + 1)
                            v.tensor_copy(yb[par][:, BANK:], psum[:, ebank["y1"], :]).then_inc(efree["y1"], 1)
                    meet(v, "passed")
                    ch.reset()
                    ch.then(ts(slots_now, slots_now, float(SLOTS), None, ALU.add))
                v.sem_inc(tick, 1)
            ch.reset()
            v.wait_ge(y_in_s, 64)
            v.wait_ge(ln2_in, 32)
            for t in range(TT):
                x = x_tok[:, t, :]
                y1, y2 = y_in[:, t, 0:D_MODEL], y_in[:, t, D_MODEL:]
                ch.add(ts(y1, y1, w_tok[:, 0, t:t + 1], None, ALU.mult))
                ch.wait()
                ch.then(stt(out=y1, in0=y2, scalar=w_tok[:, 1, t:t + 1], in1=y1, op0=ALU.mult, op1=ALU.add))
                ch.then(stt(out=x, in0=x, scalar=ALPHA, in1=y1, op0=ALU.mult, op1=ALU.add))
                layernorm(ln2_st, ln2_g, ln2_b, t, "last")
            meet(v, "end")

    @block.gpsimd
    def _(g):
        ch = Chain(g, chains["pool"])
        tt, ts = g.tensor_tensor, g.tensor_scalar
        g.wait_ge(setup_in, 80)
        ch.then(ts(row_none[:], const("tok")[:, 0:1], FAR, None, ALU.add))
        with g.Fori(0, DEPTH) as l:
            meet(g, "layer")
            ch.reset()
            S = lambda i: sm[:, i]
            zr, zi, pr, pi, a, b, c_, d, rho, wr, wi = (S(i) for i in range(11))
            g.wait_ge(small_in, 224)
            g.wait_ge(dt_ready, 1)
            ch.add(tt(zr, a_re, dt_, ALU.mult))
            ch.then(tt(zi, a_im, dt_, ALU.mult))
            ch.add(ts(phi, zi, 1 / TWO_PI, None, ALU.mult))
            ch.add(ts(zr, zr, 2.0 ** -DOUBLINGS, None, ALU.mult))
            ch.then(ts(zi, zi, 2.0 ** -DOUBLINGS, None, ALU.mult))
            ch.add(ts(pr, zr, 1 / 6, 1.0, ALU.mult, ALU.add))
            ch.add(ts(rho, zr, 1 / 6, 1.0, ALU.mult, ALU.add))
            ch.then(ts(pi, zi, 1 / 6, None, ALU.mult))
            for k in (5, 4, 3, 2, 1):
                ch.add(tt(a, zr, pr, ALU.mult))
                ch.add(tt(b, zi, pi, ALU.mult))
                ch.add(tt(c_, zr, pi, ALU.mult))
                ch.add(tt(d, zi, pr, ALU.mult))
                ch.then(tt(rho, zr, rho, ALU.mult))
                o_r, o_i = (pr, pi) if k > 1 else (wr, wi)
                ch.add(tt(a, a, b, ALU.subtract))
                ch.then(tt(c_, c_, d, ALU.add))
                if k > 1:
                    ch.add(ts(rho, rho, 1 / k, 1.0, ALU.mult, ALU.add))
                    ch.add(ts(o_r, a, 1 / k, 1.0, ALU.mult, ALU.add))
                    ch.then(ts(o_i, c_, 1 / k, None, ALU.mult))
                else:
                    ch.add(ts(o_r, a, 1.0, None, ALU.mult))
                    ch.then(ts(o_i, c_, 1.0, None, ALU.mult))
            for _k in range(DOUBLINGS):
                ch.add(tt(a, wr, wr, ALU.mult))
                ch.add(tt(b, wi, wi, ALU.mult))
                ch.add(tt(c_, wr, wi, ALU.mult))
                ch.add(ts(d, wr, 2.0, None, ALU.mult))
                ch.add(tt(zr, rho, rho, ALU.mult))
                ch.then(ts(zi, rho, 2.0, None, ALU.mult))
                ch.add(tt(a, a, b, ALU.subtract))
                ch.add(tt(c_, c_, wi, ALU.add))
                ch.then(tt(rho, zr, zi, ALU.add))
                ch.add(tt(wr, a, d, ALU.add))
                ch.then(ts(wi, c_, 2.0, None, ALU.mult))
            ch.add(ts(radius, rho, 1.0, None, ALU.add))
            for an, steps, width in ((ang, const("fine"), FINE), (angc, const("coarse"), COARSE)):
                x0, x1 = (an[:, i].rearrange("p (s n) -> p s n", n=width) for i in (0, 1))
                ch.then(tt(x0, S3(phi.unsqueeze(2), P, STILES, width), S3(steps.unsqueeze(1), P, STILES, width), ALU.mult))
                ch.then(ts(x1, x0, ROUND, None, ALU.add))
                ch.then(ts(x1, x1, -ROUND, None, ALU.add))
                ch.then(tt(x0, x0, x1, ALU.subtract))
            g.sem_inc(ang_ready, 1)
            g.wait_ge(inv_ready, 1)
            ch.add(tt(a, wr, a_re, ALU.mult))
            ch.add(tt(b, wi, a_im, ALU.mult))
            ch.add(tt(c_, wi, a_re, ALU.mult))
            ch.then(tt(d, wr, a_im, ALU.mult))
            ch.add(tt(a, a, b, ALU.add))
            ch.then(tt(c_, c_, d, ALU.subtract))
            ch.add(tt(wr, a, inv_a, ALU.mult))
            ch.then(tt(wi, c_, inv_a, ALU.mult))
            qr, qi = (S3(w.unsqueeze(2), P, STILES, GROUP) for w in (wr, wi))
            ch.add(tt(btmp[:, 0], b_in[:, 0], qr, ALU.mult))
            ch.then(tt(btmp[:, 1], b_in[:, 1], qi, ALU.mult))
            ch.then(tt(bbar[:, 0], btmp[:, 0], btmp[:, 1], ALU.subtract))
            ch.add(tt(btmp[:, 0], b_in[:, 1], qr, ALU.mult))
            ch.then(tt(btmp[:, 1], b_in[:, 0], qi, ALU.mult))
            ch.then(tt(bbar[:, 1], btmp[:, 0], btmp[:, 1], ALU.add))
            ch.then(ts(c_nat[:, 1], c_nat[:, 1], -1.0, None, ALU.mult))
            g.wait_ge(trig_ready, 1)
            for j in range(3):
                g.wait_ge(free[j], at(f"free{j}", "front", 3))
            g.wait_ge(x_saved, 16)

            with g.Fori(0, 4) as c:
                ch.reset()

                def turns(tile):
                    def tab(which, i, width):
                        return which[:, i, bass.ds(4 * c + tile, 1), :].rearrange("p a n -> p (a n)")
                    cf, sf = (S3(tab(fine, i, FINE).unsqueeze(1), P, COARSE, FINE) for i in range(2))
                    cc, sc_ = (S3(tab(coarse, i, COARSE).unsqueeze(2), P, COARSE, FINE) for i in range(2))
                    V = lambda x: x.rearrange("p (a b) -> p a b", b=FINE)
                    ch.add(tt(V(rtm[:, 0]), cc, cf, ALU.mult))
                    ch.then(tt(V(rtm[:, 1]), sc_, sf, ALU.mult))
                    ch.then(tt(rot[:, tile % 2, 0], rtm[:, 0], rtm[:, 1], ALU.subtract))
                    ch.add(tt(V(rtm[:, 0]), sc_, cf, ALU.mult))
                    ch.then(tt(V(rtm[:, 1]), cc, sf, ALU.mult))
                    ch.then(tt(rot[:, tile % 2, 1], rtm[:, 0], rtm[:, 1], ALU.add))
                    g.sem_inc(L["rot_ready"], 1)

                def back(tile):
                    g.wait_ge(L["scan_ready"], at("scan_ready", "heads", tile + 1, c))
                    cos, sin, gr, gi = rot[:, tile % 2, 0], rot[:, tile % 2, 1], gsc[:, 0], gsc[:, 1]
                    ch.add(tt(rtm[:, 0], gr, cos, ALU.mult))
                    ch.then(tt(rtm[:, 1], gi, sin, ALU.mult))
                    if tile >= 2:
                        g.wait_ge(L["h_used"], at("h_used", "heads", tile - 1, c))
                    ch.then(tt(hst[:, tile % 2, 0], rtm[:, 0], rtm[:, 1], ALU.subtract))
                    ch.add(tt(rtm[:, 0], gr, sin, ALU.mult))
                    ch.then(tt(rtm[:, 1], gi, cos, ALU.mult))
                    g.sem_inc(L["g_used"], 1)
                    ch.then(tt(hst[:, tile % 2, 1], rtm[:, 0], rtm[:, 1], ALU.add))
                    g.sem_inc(L["h_ready"], 1)

                for i in range(2):
                    src = bbar[:, i, bass.ds(4 * c, 4), :]
                    ch.add(tt(pads[:, i].rearrange("p (j g q) -> p j g q", j=4, q=GROUP), S3(src.unsqueeze(2), P, 4, 8, GROUP),
                              S3(const("bmask").rearrange("p (j g) -> p j g", j=4).unsqueeze(3), P, 4, 8, GROUP), ALU.mult))
                    cn = c_nat[:, i, bass.ds(c, 1), :]
                    ch.add(tt(pads[:, 2 + i].rearrange("p (g n) -> p g n", g=8), S3(cn, P, 8, STATES),
                              S3(const("gmask").unsqueeze(2), P, 8, STATES), ALU.mult))
                ch.wait()
                g.sem_inc(L["pads_ready"], 1)
                turns(0)
                turns(1)
                back(0)
                turns(2)
                back(1)
                turns(3)
                back(2)
                back(3)
                filled(g, 6, "heads", 3, c)

            meet(g, "moe")
            most_chosen = g.value_load(most[0:1, 0:1], min_val=0, max_val=SEQ)
            with g.Fori(0, PASSES) as ps:
                with g.If(most_chosen > ps * SLOTS):
                    dma_sems = range(gathered[0].num, scattered[1].num + 1)
                    g.dma_reset(dma_sems)
                    g.sem_clear(dma_sems)
                    meet(g, "pass")

                    def gather(q, par):
                        g.wait_ge(rows_ready, q + 1)
                        g.sem_inc(tick, 1)
                        g.indirect_dma_start(out=xg[par], out_offset=None, in_=x_mid,
                                             in_offset=bass.IndirectOffsetOnAxis(ap=row_x[par][:, 0:1], axis=0),
                                             bounds_check=SEQ - 1, oob_is_err=False).then_inc(gathered[par], 16)

                    def scatter(data, rows_of, signal):
                        g.indirect_dma_start(out=y_moe, out_offset=bass.IndirectOffsetOnAxis(ap=rows_of[:, 0:1], axis=0),
                                             in_=data, in_offset=None,
                                             bounds_check=2 * SEQ - 1, oob_is_err=False).then_inc(signal, 16)

                    for i in range(2):
                        scatter(x_tok[:, 0, :], row_none, scattered[i])
                    gather(0, 0)
                    with g.Fori(0, PAIRS // 2) as two:
                        for par in range(2):
                            q = two * 2 + par
                            gather(q + 1, 1 - par)
                            for stage in ("idx", "y0", "y1"):
                                g.wait_ge(efree[stage], q + 2)
                            g.sem_inc(tick, 1)
                            scatter(yb[par], row_y[par], scattered[par])
                    for i in range(2):
                        g.wait_ge(scattered[i], 16 * (PAIRS // 2 + 1))
                    g.wait_ge(gathered[0], 16 * (PAIRS // 2 + 1))
                    g.wait_ge(gathered[1], 16 * (PAIRS // 2))
                    meet(g, "passed")
                g.sem_inc(tick, 1)
            meet(g, "end")

    ctx.close()


_INS = ["x", "positions", "w_in", "b_gate", "mla_q_norm", "mla_w_uq", "mla_kv_norm", "mla_w_ukv", "mla_w_out",
        "diff_lambda", "diff_subln", "diff_w_out", "ssm_a_re", "ssm_a_im", "ssm_log_dt", "ssm_b_re", "ssm_b_im",
        "ssm_c_re", "ssm_c_im", "ssm_d", "ssm_w_glu", "w_o", "ln_gain", "ln_bias", "router_w", "router_bias",
        "moe_w_gate", "moe_w_up", "moe_w_down"]


def kernel(**inputs):
    import concourse.bacc as _bacc
    from concourse.bass_utils import run_bass_kernel_spmd as _run

    nc = _bacc.Bacc("TRN2", target_bir_lowering=False, num_devices=1)
    arrays, aps = {}, {}
    for name in _INS:
        a = np.ascontiguousarray(inputs[name])
        arrays[f"in_{name}"] = a
        aps[name] = nc.dram_tensor(f"in_{name}", a.shape, mybir.dt.from_np(a.dtype), kind="ExternalInput").ap()
    tables = {}
    for name, a in (("constants", constant_table()), ("layers", layer_table())):
        arrays[name] = a
        tables[name] = nc.dram_tensor(name, a.shape, F32, kind="ExternalInput").ap()
    out = nc.dram_tensor("out", (1, SEQ, D_MODEL), F32, kind="ExternalOutput").ap()
    build(nc, aps, tables["constants"], tables["layers"], out)
    r = _run(nc, [arrays], core_ids=[0])
    return r.results[0]["out"]
```

```python
import math
from contextlib import ExitStack

import numpy as np

import concourse.bass as bass
from concourse import mybir

F32 = mybir.dt.float32
I32 = mybir.dt.int32
U32 = mybir.dt.uint32
ALU = mybir.AluOpType
ACT = mybir.ActivationFunctionType
AXX = mybir.AxisListType.X

P = 128
BANK = 512
DEPTH = 2
SEQ = 512
D_MODEL = 1024
TT = SEQ // P
KD = D_MODEL // P
Q_LORA, KV_LORA, ROPE_A, NOPE = 256, 128, 32, 64
HEADS = 8
HD = 32
ROT_B = HD // 4
MLA_COLS = Q_LORA + KV_LORA + ROPE_A
DIFF_COLS = HEADS * 2 * HD
OFF_DIFF = MLA_COLS
OFF_SSM = OFF_DIFF + 3 * DIFF_COLS
SSM_W, GROUP, GROUPS, STATES = 512, 16, 32, 64
OFF_GATE = OFF_SSM + SSM_W
STILES = GROUPS * STATES // P
FINE = 32
COARSE = SEQ // FINE
DOUBLINGS = 10
EXPERTS, EGROUPS, EPER, FF = 32, 8, 4, 512
KF = FF // P
SLOTS = P // 2
PASSES = SEQ // SLOTS
GATE_W = 3 * D_MODEL // HEADS
GATE_TILES = GATE_W // P
PAIRS = EXPERTS // 2
ALPHA = (2 * DEPTH) ** 0.25
LN_EPS, RMS_EPS, SUB_EPS = 1e-5, 1e-6, 1e-5
THETA = 500000.0
NEG = -1e30
FAR = 4096.0
ROUND = 12582912.0
TWO_PI = 2 * math.pi
PI_HI = 6.28125
PI_LO = TWO_PI - PI_HI
PI_MAX = 3.1415925
SCALE_A = (NOPE + ROPE_A) ** -0.5
SCALE_B = HD ** -0.5

CONST_W = dict(ident=P, upper=P, ones=P, slot=SLOTS, causal=P, gmask=8, bmask=32, inv=20, eprio=32,
               gprio=8, tok=TT, fine=FINE, coarse=COARSE)
CONST_AT, _n = {}, 0
for _k, _w in CONST_W.items():
    CONST_AT[_k] = _n
    _n += _w
CONST_COLS = _n


def constant_table():
    c = np.zeros((P, CONST_COLS), np.float32)
    p = np.arange(P)

    def put(name, v):
        c[:, CONST_AT[name]:CONST_AT[name] + CONST_W[name]] = v

    put("ident", np.eye(P))
    put("upper", p[:, None] < p[None, :])
    put("ones", 1.0)
    put("slot", p[None, :SLOTS])
    put("causal", np.where(p[None, :] > p[:, None], NEG, 0.0))
    put("gmask", (p[:, None] // GROUP) == np.arange(8)[None, :])
    jj, g = np.divmod(np.arange(32), 8)
    put("bmask", g[None, :] == 2 * jj[None, :] + (p[:, None] >= STATES))
    inv = [np.float32(THETA) ** (-np.arange(0, r, 2, dtype=np.float32) / np.float32(r)) for r in (ROPE_A, ROT_B)]
    put("inv", np.concatenate(inv)[None, :])
    put("eprio", EXPERTS - np.arange(EXPERTS)[None, :])
    put("gprio", EGROUPS - np.arange(EGROUPS)[None, :])
    put("tok", np.arange(TT)[None, :] * P + p[:, None])
    put("fine", np.arange(FINE)[None, :])
    put("coarse", np.arange(COARSE)[None, :] * FINE)
    return c


def layer_table():
    li = np.array([0.8 - 0.6 * math.exp(-0.3 * l) for l in range(DEPTH)])
    return np.broadcast_to(np.stack([li, 1.0 - li], 1)[:, None, :], (DEPTH, P, 2)).astype(np.float32).copy()


STEPS = dict(front=1, heads=4, join=1, merge=2, tail=1, last=1)
RAISED = dict(
    b0=(3, 7, 1, 0, 2, 0), b1=(3, 7, 1, 0, 2, 0), b2=(3, 7, 1, 6, 2, 0), b3=(2, 7, 1, 6, 2, 0),
    b4=(2, 19, 0, 2, 4, 0), b5=(2, 16, 0, 2, 4, 0), b6=(2, 16, 0, 0, 1, 0), full7=(2, 0, 0, 0, 1, 0),
    b7=(2, 1, 0, 0, 1, 0),
    sq_sums=(1, 0, 0, 0, 0, 0), rms_mean=(1, 0, 1, 0, 0, 0), rms_root=(1, 0, 1, 0, 0, 0),
    lora_ready=(1, 0, 0, 0, 0, 0),
    q_ready=(0, 2, 0, 0, 0, 0), kv_ready=(0, 2, 0, 0, 0, 0), diff_copied=(0, 2, 0, 0, 0, 0),
    diff_ready=(0, 2, 0, 0, 0, 0), max_ready=(0, 6, 0, 0, 0, 0), mix_ready=(0, 8, 0, 0, 0, 0),
    oa_ready=(0, 2, 0, 0, 0, 0), pads_ready=(1, 1, 0, 0, 0, 0), rot_ready=(0, 4, 0, 0, 0, 0),
    scan_ready=(0, 4, 0, 0, 0, 0), h_ready=(0, 4, 0, 0, 0, 0),
    h_used=(0, 4, 0, 0, 0, 0), w_diff_ready=(0, 1, 0, 0, 0, 0),
    ob_ready=(0, 0, 4, 0, 0, 0), gelu_done=(0, 0, 1, 0, 0, 0),
    y_ready=(0, 1, 0, 0, 0, 0), g_used=(0, 4, 0, 0, 0, 0),
    gate_room=(2, 6, 0, 0, 0, 0),
    merged_ready=(0, 0, 0, 12, 0, 0),
    ln_var=(0, 0, 0, 0, 4, 0), ln_root=(0, 0, 0, 0, 4, 4), ln_ready=(0, 0, 0, 0, 4, 0),
)
for _b in range(7):
    RAISED[f"full{_b}"] = RAISED[f"b{_b}"]
    RAISED[f"free{_b}"] = RAISED[f"b{_b}"]
RAISED["free7"] = RAISED["b7"]


def at(name, phase, n, step=0):
    v = n
    for k, (ph, steps) in enumerate(STEPS.items()):
        if ph == phase:
            return v + step * RAISED[name][k]
        v += steps * RAISED[name][k]


BASE4, BASE5, BASE6 = (0, 9), (0, 8), (0, 8)
GATE_AT = ((5, 2), (4, 6), (5, 5))


def gate_at(hh, j):
    b, u = GATE_AT[j]
    return b, {4: BASE4, 5: BASE5, 6: BASE6}[b][hh] + u


class Chain:

    def __init__(self, eng, sem):
        self.eng, self.sem, self.n = eng, sem, 0

    def reset(self):
        self.eng.sem_clear(self.sem)
        self.n = 0

    def add(self, ins):
        ins.then_inc(self.sem, 1)
        self.n += 1
        return ins

    def wait(self):
        if self.n:
            self.eng.wait_ge(self.sem, self.n)

    def then(self, ins):
        self.add(ins)
        self.wait()


def build(nc, t_in, consts, layer_consts, out):
    ctx = ExitStack()
    sb = ctx.enter_context(nc.sbuf_tensor("sb", [P, 53100], F32))
    psum = ctx.enter_context(nc.psum_tensor("psum", [P, 8, BANK], F32))
    pos_i = ctx.enter_context(nc.sbuf_tensor("pos_i", [P, TT], I32))
    row_y = [ctx.enter_context(nc.sbuf_tensor(f"row_y{i}", [P, 1], U32)) for i in range(2)]
    row_none = ctx.enter_context(nc.sbuf_tensor("row_none", [P, 1], U32))
    most = ctx.enter_context(nc.sbuf_tensor("most", [P, 1], I32))
    x_old = nc.dram_tensor("x_old", [SEQ, D_MODEL], F32, kind="Internal").ap()
    gates_d = nc.dram_tensor("gates_d", [3 * D_MODEL, SEQ], F32, kind="Internal").ap()
    y_moe = nc.dram_tensor("y_moe", [2 * SEQ, D_MODEL], F32, kind="Internal").ap()

    class Area:
        def __init__(self, start, end):
            self.at, self.end = start, end

        def take(self, *dims):
            n = int(np.prod(dims))
            v = sb[:, self.at:self.at + n]
            self.at += n
            assert self.at <= self.end, (self.at, self.end)
            if len(dims) > 1:
                names = "abcd"[:len(dims)]
                spec = " ".join(names)
                v = v.rearrange(f"p ({spec}) -> p {spec}", **dict(zip(names, dims)))
            return v

    kept = Area(0, 53100)
    constants_sb = kept.take(CONST_COLS)

    def const(name):
        return constants_sb[:, CONST_AT[name]:CONST_AT[name] + CONST_W[name]]

    ident, ones = const("ident"), const("ones")
    xT = kept.take(KD, SEQ)
    uT = kept.take(4, SEQ)
    yT = kept.take(4, SEQ)
    x_at = kept.at
    x_tok = kept.take(TT, D_MODEL)
    oT = Area(x_at, x_at + 4096)
    oaT, obT = oT.take(4, SEQ), oT.take(4, SEQ)
    cc_a, ss_a = kept.take(TT, 2, 16), kept.take(TT, 2, 16)
    cc_b, ss_b = kept.take(TT, 8), kept.take(TT, 8)
    router_w = kept.take(KD, EXPERTS)
    router_b = kept.take(EXPERTS)
    lambda_init = kept.take(2)
    small = kept.take(64)
    lam = small[:, 0:4]
    rope_pos = kept.take(TT)
    half_pi, ln_eps = kept.take(1), kept.take(1)
    base = kept.at

    front_and_heads = Area(base, 53100)
    w_diff = front_and_heads.take(2, KD, 3 * P)
    w_uq, w_ukv = front_and_heads.take(2, HEADS * 96), front_and_heads.take(HEADS * 128)
    loraT = front_and_heads.take(3, SEQ)
    krope = front_and_heads.take(TT, ROPE_A)
    norms_at = front_and_heads.at
    qn_bc, kvn_bc, subln = front_and_heads.take(Q_LORA), front_and_heads.take(KV_LORA), front_and_heads.take(2 * HD)
    lam_in = front_and_heads.take(4, HD)
    a_re, a_im, dt_, inv_a = (front_and_heads.take(STILES) for _ in range(4))
    radius, phi = front_and_heads.take(STILES), front_and_heads.take(STILES)
    bbar = front_and_heads.take(2, STILES, GROUP)
    c_nat = front_and_heads.take(2, 4, STATES)
    d_col = front_and_heads.take(4)
    fine, coarse = front_and_heads.take(2, STILES, FINE), front_and_heads.take(2, STILES, COARSE)
    ms_b = front_and_heads.take(TT, HEADS)
    ob_tok = front_and_heads.take(TT, HEADS, 2 * HD)
    heads_at = front_and_heads.at
    rope = Area(base, 53100)
    rope_ang, rope_sc = rope.take(2, TT, 20), rope.take(2, TT, 20)
    front_only = Area(heads_at, 53100)
    w_ssm, w_mla = front_only.take(KD, SSM_W), front_only.take(KD, MLA_COLS)
    lora = front_only.take(TT, Q_LORA + KV_LORA)
    b_in = front_only.take(2, STILES, GROUP)
    sqs, ssum, rrt = front_only.take(P * 2), front_only.take(TT, 2), front_only.take(TT, 2)
    rtmp = front_only.take(3, TT, 32)
    ssm_vec = front_only.take(16, STILES)
    ang = front_only.take(3, STILES * FINE)
    angc = front_only.take(3, STILES * COARSE)
    btmp = front_only.take(2, STILES, GROUP)
    heads_only = Area(heads_at, 53100)
    q_h, k_h, v_h = heads_only.take(TT, 96), heads_only.take(TT, 96), heads_only.take(TT, 64)
    qT, kT = heads_only.take(SEQ), heads_only.take(SEQ)
    diff_qkv = heads_only.take(TT, 3 * 64)
    dqT, dkT = heads_only.take(SEQ), heads_only.take(SEQ)
    p1, p2, pT = (heads_only.take(P * TT * (TT + 1) // 2) for _ in range(3))

    def causal_part(p, t, a=0, b=None):
        start = P * t * (t + 1) // 2
        return p[:, start + a:start + (b if b else (t + 1) * P)]

    w_gate = heads_only.take(KD, GATE_W)
    over_gains = Area(norms_at, norms_at + Q_LORA + KV_LORA)
    gate_bias, tmp_o = over_gains.take(GATE_TILES), over_gains.take(TT, 64)
    gout = heads_only.take(2, SEQ)
    oa_tok = heads_only.take(TT, P)
    tmp_h = heads_only.take(4, TT * 32)
    softmax_st = heads_only.take(12, TT)
    pads = Area(x_at + 2048, x_at + 4096).take(4, 512)
    bT, cT = heads_only.take(2, 512), heads_only.take(2, 4, 32)
    rot = heads_only.take(2, 2, SEQ)
    turn_tmp = heads_only.take(2, SEQ)
    bu = heads_only.take(2, 2, SEQ)
    turned = heads_only.take(2, SEQ)
    scanned = heads_only.take(2, SEQ)
    states = heads_only.take(2, 2, SEQ)
    merge_and_tail = Area(base, 53100)
    w_branch = [merge_and_tail.take(4, BANK) for _ in range(4)]
    w_o_at = merge_and_tail.at
    mergedT = merge_and_tail.take(KD, SEQ)
    w_o = merge_and_tail.take(KD, D_MODEL)
    gates_at = merge_and_tail.at
    gates = merge_and_tail.take(3 * KD, SEQ)
    misc_at = merge_and_tail.at
    glu_gate = merge_and_tail.take(2, SEQ)
    merge_tmp = merge_and_tail.take(SEQ)
    ln_g, ln_b = merge_and_tail.take(D_MODEL), merge_and_tail.take(D_MODEL)
    ln_st, ln2_st = merge_and_tail.take(TT, 16), merge_and_tail.take(TT, 16)
    experts = Area(base, 53100)
    e_gate = [experts.take(KD, FF) for _ in range(2)]
    assert experts.at == w_o_at
    e_down = [experts.take(KF, D_MODEL) for _ in range(2)]
    result = [experts.take(D_MODEL) for _ in range(2)]
    experts.at = gates_at
    e_up = [experts.take(KD, FF) for _ in range(2)]
    e_misc = Area(experts.at, misc_at + 3 * SEQ)
    sel = [e_misc.take(TT, 2, SLOTS) for _ in range(2)]
    hiddenT = e_misc.take(KF, P)
    hidden, silu = e_misc.take(FF), e_misc.take(FF)
    tokensT = e_misc.take(KD, P)
    routing = Area(x_at - 4096, x_at)
    EP = EXPERTS + 2
    router_p, biased, route_tmp = routing.take(TT, EXPERTS), routing.take(TT, EXPERTS), routing.take(5, TT * EXPERTS)
    oh1, oh2, chosen = routing.take(TT, EXPERTS), routing.take(TT, EXPERTS), routing.take(TT, EXPERTS)
    slot_of, payload = routing.take(TT, EP), routing.take(TT, EP)
    slots_now = routing.take(SLOTS)
    w_tok = routing.take(2, TT)
    tok_vec = routing.take(8, TT)
    ln2_g, ln2_b = routing.take(D_MODEL), routing.take(D_MODEL)
    y_in = Area(base, 53100).take(TT, 2 * D_MODEL)

    def sem(name):
        return ctx.enter_context(nc.semaphore(name))

    tables_in, setup_in = sem("tables_in"), sem("setup_in")
    setup_ang = sem("setup_ang")
    setup_trig = sem("setup_trig")
    small_in, w_ssm_in, w_mla_in = sem("small_in"), sem("w_ssm_in"), sem("w_mla_in")
    front_first, front_last = small_in.num, w_mla_in.num
    layer_first = sem("layer_first").num
    full = [sem(f"full{b}") for b in range(8)]
    free = [sem(f"free{b}") for b in range(8)]
    raised = {n: sem(n) for n in RAISED if n[0:4] not in ("full", "free") and not (n[0] == "b" and n[1:].isdigit())}
    w_lora_in = sem("w_lora_in")
    w_diff_in = [sem(f"w_diff_in{i}") for i in range(2)]
    x_saved, w_o_in, x_back, ln_in, ln2_in = (sem(n) for n in ("x_saved", "w_o_in", "x_back", "ln_in", "ln2_in"))
    y_in_s = [sem(f"y_in{t}") for t in range(TT)]
    alpha_x, x_y1, x_sum, mean_ready = (sem(n) for n in ("alpha_x", "x_y1", "x_sum", "mean_ready"))
    w_gate_in, gates_saved = sem("w_gate_in"), sem("gates_saved")
    gates_in = [sem(f"gates_in{i}") for i in range(3)]
    w_branch_in = [sem(f"w_branch_in{i}") for i in range(4)]
    dt_ready, lam_ready, lam_exp, ang_ready, trig_ready, disc_ready, coef_ready = (
        sem(n) for n in ("dt_ready", "lam_ready", "lam_exp", "ang_ready", "trig_ready", "disc_ready", "coef_ready"))
    y1_ready, krope_ready, subln_ready = sem("y1_ready"), sem("krope_ready"), sem("subln_ready")
    pick_ready = sem("pick_ready")
    layer_last = sem("layer_last").num
    pass_first = sem("pass_first").num
    STAGES = ("idx", "x0", "x1", "gate", "up", "h", "y0", "y1")
    efull = {b: sem(f"efull_{b}") for b in STAGES}
    efree = {b: sem(f"efree_{b}") for b in STAGES}
    ebank = {b: k for k, b in enumerate(STAGES)}
    sel_ready, he_ready = sem("sel_ready"), sem("he_ready")
    eg_in, eu_in, ed_in = ([sem(f"{n}_in{i}") for i in range(2)] for n in ("eg", "eu", "ed"))
    pass_last = sem("pass_last").num
    scattered = [sem(f"scattered{i}") for i in range(2)]
    arr = {n: sem(f"arrive_{n}") for n in ("layer", "moe", "pass", "passed", "end")}
    go = {n: sem(f"go_{n}") for n in ("layer", "moe", "pass", "passed", "end")}
    tick = sem("tick")
    chains = {n: sem(f"chain_{n}") for n in ("act", "dve", "pool")}
    out_done = sem("out_done")

    def meet(eng, name):
        eng.drain().then_inc(arr[name], 1)
        eng.wait_ge(go[name], 1)
        eng.sem_inc(tick, 1)

    def host(sp, name, clears, start=True):
        sp.wait_ge(arr[name], 4)
        sp.sem_clear(arr[name])
        for r in clears:
            sp.sem_clear(r)
        if start:
            sp.sem_inc(go[name], 1)

    def claim(pe, b, phase, u, step=0):
        v = at(f"free{b}", phase, u, step)
        if not (isinstance(v, int) and v == 0):
            pe.wait_ge(free[b], v)

    def filled(eng, b, phase, u, step=0):
        eng.wait_ge(full[b], at(f"full{b}", phase, u + 1, step))

    def emptied(eng, b, phase, u, step=0):
        eng.wait_ge(free[b], at(f"free{b}", phase, u + 1, step))

    x_d, w_in = t_in["x"], t_in["w_in"]
    b_gate_flat = t_in["b_gate"].rearrange("l a b -> l (a b)")
    tok3 = lambda d: d.rearrange("(t p) d -> p t d", p=P)
    rows = lambda d: d.rearrange("(k p) n -> p k n", p=P)
    bcast = lambda d: d.partition_broadcast(P)
    S3 = lambda v, *shape: v.to_broadcast(list(shape))

    ctx.enter_context(nc.allow_non_contiguous_dma(reason="small parameters, a number for each partition"))
    block = ctx.enter_context(nc.Block())

    @block.sync
    def _(sp):
        sp.dma_start(constants_sb, consts).then_inc(tables_in, 16)
        sp.dma_start(pos_i[:], t_in["positions"].rearrange("a (t p) -> p (a t)", p=P)).then_inc(tables_in, 16)
        sp.dma_start(x_tok, tok3(x_d[0])).then_inc(setup_in, 16)
        sp.dma_start(router_w, rows(t_in["router_w"])).then_inc(setup_in, 16)
        sp.dma_start(router_b, bcast(t_in["router_bias"])).then_inc(setup_in, 16)

        def front_loads(l):
            wl = w_in[l]
            loads = [
                (lambda_init, layer_consts[l]), (qn_bc, bcast(t_in["mla_q_norm"][l])), (kvn_bc, bcast(t_in["mla_kv_norm"][l])),
                (subln, bcast(t_in["diff_subln"][l])),
                (lam_in, bcast(t_in["diff_lambda"][l].rearrange("a b -> (a b)")).rearrange("p (a b) -> p a b", a=4)),
                (a_re, t_in["ssm_a_re"][l].rearrange("(t h) n -> (h n) t", h=2)),
                (a_im, t_in["ssm_a_im"][l].rearrange("(t h) n -> (h n) t", h=2)),
                (b_in[:, 0], t_in["ssm_b_re"][l].rearrange("(t h) n q -> (h n) t q", h=2)),
                (b_in[:, 1], t_in["ssm_b_im"][l].rearrange("(t h) n q -> (h n) t q", h=2)),
                (c_nat[:, 0], t_in["ssm_c_re"][l].rearrange("(c g) q n -> (g q) c n", g=8)),
                (c_nat[:, 1], t_in["ssm_c_im"][l].rearrange("(c g) q n -> (g q) c n", g=8)),
                (d_col, t_in["ssm_d"][l].rearrange("(c p) -> p c", p=P)),
            ]
            for h in range(2):
                dt_src = t_in["ssm_log_dt"][l].rearrange("(t h) -> h t", h=2)[h]
                loads.append((dt_[h * 64:h * 64 + 64, :], dt_src.partition_broadcast(64)))
            assert len(loads) == 14
            sp.dma_start(w_mla, rows(wl[:, 0:MLA_COLS])).then_inc(w_mla_in, 16)
            for dst, src in loads:
                sp.dma_start(dst, src).then_inc(small_in, 16)
            sp.dma_start(w_ssm, rows(wl[:, OFF_SSM:OFF_SSM + SSM_W])).then_inc(w_ssm_in, 16)

        front_loads(0)
        for b in STAGES:
            sp.sem_inc(efree[b], 1)
        sp.wait_ge(tables_in, 32)
        sp.wait_ge(setup_in, 48)
        with sp.Fori(0, DEPTH) as l:
            host(sp, "layer", [range(layer_first, layer_last + 1), go["moe"], go["end"]])
            wl = w_in[l]
            sp.dma_start(w_uq, rows(t_in["mla_w_uq"][l])).then_inc(w_lora_in, 16)
            sp.dma_start(w_ukv, t_in["mla_w_ukv"][l]).then_inc(w_lora_in, 16)
            sp.dma_start(tok3(x_old), x_tok).then_inc(x_saved, 16)
            diff_w = wl[:, OFF_DIFF:OFF_SSM].rearrange("(k p) (s c n) -> c s p k n", p=P, s=3, n=P)

            def load_diff(c, par):
                for i in range(3):
                    sp.dma_start(w_diff[:, par, :, i * P:(i + 1) * P], diff_w[c, i]).then_inc(w_diff_in[par], 16)

            def load_gate(b):
                sp.dma_start(w_gate, rows(wl[:, bass.ds(b * GATE_W + OFF_GATE, GATE_W)])).then_inc(w_gate_in, 16)
                sp.dma_start(gate_bias, b_gate_flat[bass.ds(l, 1), bass.ds(b * GATE_W, GATE_W)].rearrange("a (j p) -> p (a j)", p=P)).then_inc(w_gate_in, 16)

            def load_branch(i, n):
                w2 = [rows(t_in["mla_w_out"][l]), rows(t_in["diff_w_out"][l]), rows(t_in["ssm_w_glu"][l])][i]
                if n:
                    filled(sp, 3, "merge", 2 * i + 1, 0)
                sp.dma_start(w_branch[i], w2[:, :, n * BANK:(n + 1) * BANK]).then_inc(w_branch_in[i], 16)
                if i == 2:
                    sp.dma_start(w_branch[3], w2[:, :, D_MODEL + n * BANK:D_MODEL + (n + 1) * BANK]).then_inc(w_branch_in[3], 16)

            def serve_heads(c, par, last):
                sp.wait_ge(w_diff_in[par], 48 * (c // 2 + 1))
                sp.sem_inc(raised["w_diff_ready"], 1)
                for hh in range(2):
                    for j in range(GATE_TILES):
                        b, u = gate_at(hh, j)
                        emptied(sp, b, "heads", u, c)
                        sp.dma_start(gates_d[bass.ds((2 * c + hh) * GATE_W + j * P, P), :], gout[:, (hh + j) % 2, :]).then_inc(gates_saved, 16)
                        if hh == 1 and j == 0:
                            if not last:
                                load_diff(c + 2, par)
                            elif par == 1:
                                for i in range(3):
                                    load_branch(i, 0)
                        if j == GATE_TILES - 1 and not (last and par == 1 and hh == 1):
                            load_gate(2 * c + hh + 1)
                        sp.wait_ge(gates_saved, 16 * GATE_TILES * 2 * c + 16 * (GATE_TILES * hh + j + 1))
                        sp.sem_inc(raised["gate_room"], 1)

            for c in range(2):
                load_diff(c, c)
            sp.wait_ge(raised["pads_ready"], at("pads_ready", "heads", 0))
            sp.wait_ge(krope_ready, 1)
            sp.wait_ge(trig_ready, 1)
            for j in range(3):
                emptied(sp, j, "front", 2)
            load_gate(0)
            for _ in range(2):
                sp.sem_inc(raised["gate_room"], 1)
            for c in range(4):
                serve_heads(c, c % 2, c >= 2)
            sp.wait_ge(raised["rms_mean"], at("rms_mean", "join", 1))
            emptied(sp, 4, "heads", 18, 3)
            for i in range(3):
                mine = slice(i * KD, (i + 1) * KD)
                sp.dma_start(gates[:, mine, :], gates_d.rearrange("(c p) n -> p c n", p=P)[:, mine, :]).then_inc(gates_in[i], 16)
            for b in range(4):
                emptied(sp, b, "join", 0)
            sp.dma_start(w_o, rows(t_in["w_o"][l])).then_inc(w_o_in, 16)
            for i in range(3):
                load_branch(i, 1)
            filled(sp, 3, "merge", 5, 1)
            sp.wait_ge(x_saved, 16)
            sp.dma_start(x_tok, tok3(x_old)).then_inc(x_back, 16)
            filled(sp, 5, "merge", 1, 1)
            sp.wait_ge(raised["merged_ready"], at("merged_ready", "merge", 12, 1))
            sp.dma_start(ln_g, bcast(t_in["ln_gain"][l][0])).then_inc(ln_in, 16)
            sp.dma_start(ln_b, bcast(t_in["ln_bias"][l][0])).then_inc(ln_in, 16)
            sp.dma_start(ln2_g, bcast(t_in["ln_gain"][l][1])).then_inc(ln2_in, 16)
            sp.dma_start(ln2_b, bcast(t_in["ln_bias"][l][1])).then_inc(ln2_in, 16)

            def expert_loads(w, names, q):
                for i in range(2):
                    sp.dma_start(w[i], rows(t_in[names[0]][l][2 * q + i])).then_inc(names[1][i], 16)

            def down_loads(n, q):
                half = slice(n * BANK, (n + 1) * BANK)
                for i in range(2):
                    sp.dma_start(e_down[i][:, :, half], rows(t_in["moe_w_down"][l][2 * q + i])[:, :, half]).then_inc(ed_in[n], 16)

            w_gates, w_ups = ("moe_w_gate", eg_in), ("moe_w_up", eu_in)
            expert_loads(e_gate, w_gates, 0)
            expert_loads(e_up, w_ups, 0)
            filled(sp, 3, "tail", 1)
            for n in range(2):
                down_loads(n, 0)
            host(sp, "moe", [go["layer"], go["passed"], go["pass"], range(front_first, front_last + 1)])
            most_chosen = sp.value_load(most[0:1, 0:1], min_val=0, max_val=SEQ)

            def experts_pass():
                with sp.Fori(1, PAIRS) as q:
                    sp.wait_ge(efull["gate"], q)
                    expert_loads(e_gate, w_gates, q)
                    sp.wait_ge(efull["up"], q)
                    expert_loads(e_up, w_ups, q)
                    for n in range(2):
                        sp.wait_ge(efull[f"y{n}"], q)
                        down_loads(n, q)
                host(sp, "passed", [range(pass_first, pass_last + 1), go["pass"]], start=False)
                for b in STAGES:
                    sp.sem_inc(efree[b], 1)
                sp.sem_inc(go["passed"], 1)

            experts_pass()
            with sp.If(most_chosen > SLOTS):
                with sp.Fori(1, PASSES) as ps:
                    with sp.If(most_chosen > ps * SLOTS):
                        expert_loads(e_gate, w_gates, 0)
                        expert_loads(e_up, w_ups, 0)
                        for n in range(2):
                            down_loads(n, 0)
                        host(sp, "pass", [go["passed"]])
                        experts_pass()
                    sp.sem_inc(tick, 1)
            sp.sem_inc(tick, 1)
            for t in range(TT):
                sp.dma_start(y_in[:, t, :], y_moe.rearrange("(t p k) d -> t p (k d)", p=P, k=2)[t]).then_inc(y_in_s[t], 16)
            with sp.If(l < DEPTH - 1):
                front_loads((l + 1) % DEPTH)
            host(sp, "end", [])
        sp.dma_start(tok3(out[0]), x_tok).then_inc(out_done, 16)
        sp.wait_ge(out_done, 16)

    @block.tensor
    def _(pe):
        pe.wait_ge(tables_in, 32)
        pe.wait_ge(setup_in, 48)
        with pe.Fori(0, DEPTH) as l:
            meet(pe, "layer")

            def transpose_x(phase, u):
                for k in range(KD):
                    claim(pe, k, phase, u)
                    for t in range(TT):
                        mm = pe.transpose(psum[:, k, t * P:(t + 1) * P], x_tok[:, t, k * P:(k + 1) * P], ident)
                    mm.then_inc(full[k], 1)

            transpose_x("front", 0)
            pe.wait_ge(w_mla_in, 16)
            for k in range(KD):
                emptied(pe, k, "front", 0)
            for t in range(TT):
                for k in range(KD):
                    mm = pe.matmul(psum[:, 4 + t, 0:MLA_COLS], xT[:, k, t * P:(t + 1) * P], w_mla[:, k, :], start=(k == 0), stop=(k == KD - 1))
                mm.then_inc(full[4 + t], 1)
            pe.wait_ge(w_ssm_in, 16)
            for c in range(4):
                for k in range(KD):
                    mm = pe.matmul(psum[:, c, :], w_ssm[:, k, c * P:(c + 1) * P], xT[:, k, :], start=(k == 0), stop=(k == KD - 1))
                mm.then_inc(full[c], 1)
            pe.wait_ge(raised["lora_ready"], 1)
            for j in range(3):
                claim(pe, j, "front", 2)
                for t in range(TT):
                    mm = pe.transpose(psum[:, j, t * P:(t + 1) * P], lora[:, t, j * P:(j + 1) * P], ident)
                mm.then_inc(full[j], 1)
            for j in range(3):
                emptied(pe, j, "front", 2)
            pe.wait_ge(w_lora_in, 32)

            with pe.Fori(0, 4) as c:
                par_w = c % 2
                pe.wait_ge(raised["pads_ready"], at("pads_ready", "heads", 0, c))
                for i in range(4):
                    claim(pe, i, "heads", 0, c)
                    for j in range(4):
                        mm = pe.transpose(psum[:, i, j * P:(j + 1) * P], pads[:, i, j * P:(j + 1) * P], ident)
                    mm.then_inc(full[i], 1)
                for hh in range(2):
                    h = 2 * c + hh
                    u4, u5, u6, us = BASE4[hh], BASE5[hh], BASE6[hh], 1 + 3 * hh
                    claim(pe, 4, "heads", u4, c)
                    for t in range(TT):
                        for k in range(2):
                            mm = pe.matmul(psum[:, 4, t * 96:(t + 1) * 96], loraT[:, k, t * P:(t + 1) * P],
                                           w_uq[:, k, bass.ds(h * 96, 96)], start=(k == 0), stop=(k == 1))
                    mm.then_inc(full[4], 1)
                    claim(pe, 5, "heads", u5, c)
                    for t in range(TT):
                        mm = pe.matmul(psum[:, 5, t * P:(t + 1) * P], loraT[:, 2, t * P:(t + 1) * P],
                                       w_ukv[:, bass.ds(h * P, P)], start=True, stop=True)
                    mm.then_inc(full[5], 1)
                    if hh == 0:
                        pe.wait_ge(raised["w_diff_ready"], at("w_diff_ready", "heads", 1, c))

                    def diff_product(t):
                        b, u = (6, u6) if t < 2 else (4, u4 + 1)
                        if t % 2 == 0:
                            claim(pe, b, "heads", u, c)
                        for k in range(KD):
                            wv = w_diff[:, bass.ds(par_w, 1), k, :].rearrange("p a (s n) -> p (a s) n", s=3)[:, :, hh * 64:hh * 64 + 64]
                            mm = pe.matmul(psum[:, b, (t % 2) * 192:(t % 2) * 192 + 192].rearrange("p (s n) -> p s n", s=3),
                                           xT[:, k, t * P:(t + 1) * P], wv, start=(k == 0), stop=(k == KD - 1))
                        if t % 2:
                            mm.then_inc(full[b], 1)

                    diff_product(0)
                    diff_product(1)
                    pe.wait_ge(raised["q_ready"], at("q_ready", "heads", hh + 1, c))
                    claim(pe, 5, "heads", u5 + 1, c)
                    for t in range(TT):
                        mm = pe.transpose(psum[0:96, 5, t * P:(t + 1) * P], q_h[:, t, :], ident)
                    mm.then_inc(full[5], 1)
                    diff_product(2)
                    pe.wait_ge(raised["kv_ready"], at("kv_ready", "heads", hh + 1, c))
                    claim(pe, 6, "heads", u6 + 1, c)
                    for t in range(TT):
                        mm = pe.transpose(psum[0:96, 6, t * P:(t + 1) * P], k_h[:, t, :], ident)
                    mm.then_inc(full[6], 1)
                    diff_product(3)

                    def gate_tile(j, k0=0, k1=KD):
                        b, u = gate_at(hh, j)
                        if k0 == 0:
                            if j == 0:
                                pe.wait_ge(w_gate_in, h * 32 + 32)
                            claim(pe, b, "heads", u, c)
                        for k in range(k0, k1):
                            mm = pe.matmul(psum[:, b, :], w_gate[:, k, j * P:(j + 1) * P], xT[:, k, :], start=(k == 0), stop=(k == KD - 1))
                        if k1 == KD:
                            mm.then_inc(full[b], 1)

                    def scores(q, k, u):
                        for t in range(TT):
                            claim(pe, t, "heads", us + u, c)
                            pe.matmul(psum[:, t, 0:(t + 1) * P], q[:, t * P:(t + 1) * P], k[:, 0:(t + 1) * P],
                                      start=True, stop=True).then_inc(full[t], 1)

                    def attend(p, v, first4, first5, last6, ready):
                        for t in range(TT):
                            b, u = (4, first4 + t // 2) if t % 2 == 0 else (5, first5 + t // 2)
                            ready(t)
                            claim(pe, b, "heads", u, c)
                            for kb in range(t + 1):
                                mm = pe.transpose(psum[:, b, kb * P:(kb + 1) * P], causal_part(p, t, kb * P, (kb + 1) * P), ident)
                            mm.then_inc(full[b], 1)
                        claim(pe, 6, "heads", last6, c)
                        for t in range(TT):
                            b, u = (4, first4 + t // 2) if t % 2 == 0 else (5, first5 + t // 2)
                            emptied(pe, b, "heads", u, c)
                            for kb in range(t + 1):
                                mm = pe.matmul(psum[:, 6, t * 64:(t + 1) * 64], causal_part(pT, t, kb * P, (kb + 1) * P), v(kb),
                                               start=(kb == 0), stop=(kb == t))
                        mm.then_inc(full[6], 1)

                    emptied(pe, 5, "heads", u5 + 1, c)
                    emptied(pe, 6, "heads", u6 + 1, c)
                    scores(qT[0:96, :], kT[0:96, :], 0)

                    def b_product(j, i):
                        claim(pe, 6, "heads", u6 + (2, 3, 4, 6)[2 * j + i], c)
                        tile = 2 * hh + j
                        pe.matmul(psum[:, 6, :], bT[:, i, tile * P:(tile + 1) * P], uT[:, bass.ds(c, 1), :].rearrange("p a n -> p (a n)"),
                                  start=True, stop=True).then_inc(full[6], 1)

                    b_product(0, 0)
                    gate_tile(0, 0, 4)
                    pe.wait_ge(raised["diff_ready"], at("diff_ready", "heads", hh + 1, c))
                    for i in range(2):
                        b = 4
                        claim(pe, b, "heads", u4 + 2 + i, c)
                        pe.sem_inc(tick, 1)
                        for t in range(TT):
                            mm = pe.transpose(psum[0:64, b, t * P:(t + 1) * P], diff_qkv[:, t, i * 64:(i + 1) * 64], ident)
                        mm.then_inc(full[b], 1)
                        if i == 0:
                            b_product(0, 1)
                    gate_tile(0, 4, KD)
                    b_product(1, 0)
                    attend(p1, lambda kb: v_h[:, kb, :], u4 + 4, u5 + 3, u6 + 5,
                           lambda t: emptied(pe, t, "heads", us, c))
                    b_product(1, 1)
                    emptied(pe, 4, "heads", u4 + 3, c)
                    scores(dqT[0:32, :], dkT[0:32, :], 1)
                    gate_tile(1, 0, 4)
                    scores(dqT[32:64, :], dkT[32:64, :], 2)
                    gate_tile(1, 4, KD)

                    def c_products(j):
                        tile = 2 * hh + j
                        pe.wait_ge(raised["h_ready"], at("h_ready", "heads", tile + 1, c))
                        if tile == 0:
                            claim(pe, 7, "heads", 0, c)
                        for i in range(2):
                            mm = pe.matmul(psum[32 * tile:32 * tile + 32, 7, :], cT[:, i, tile, :], states[:, tile % 2, i, :],
                                           start=(i == 0), stop=(i == 1))
                        mm.then_inc(raised["h_used"], 1)

                    c_products(0)
                    gate_tile(2)
                    attend(p1, lambda kb: diff_qkv[:, kb, 128:192], u4 + 7, u5 + 6, u6 + 7,
                           lambda t: pe.wait_ge(raised["mix_ready"], at("mix_ready", "heads", 4 * hh + t + 1, c)))
                    c_products(1)
                pe.wait_ge(raised["oa_ready"], at("oa_ready", "heads", 2, c))
                claim(pe, 4, "heads", 18, c)
                for t in range(TT):
                    mm = pe.transpose(psum[:, 4, t * P:(t + 1) * P], oa_tok[:, t, :], ident)
                mm.then_inc(full[4], 1)

            for i in range(4):
                claim(pe, i, "join", 0)
            for t in range(TT):
                pe.wait_ge(raised["ob_ready"], at("ob_ready", "join", t + 1))
                for i in range(4):
                    mm = pe.transpose(psum[:, i, t * P:(t + 1) * P], ob_tok[:, t, 2 * i:2 * i + 2, :].rearrange("p a b -> p (a b)"), ident)
                    if t == TT - 1:
                        mm.then_inc(full[i], 1)
            emptied(pe, 4, "heads", 18, 3)

            with pe.Fori(0, 2) as n:
                for i in range(3):
                    pe.wait_ge(w_branch_in[i], n * 16 + 16)
                    if i == 2:
                        pe.wait_ge(w_branch_in[3], n * 16 + 16)
                    if i == 1:
                        for b in range(4):
                            emptied(pe, b, "join", 0)
                    if i == 2:
                        pe.wait_ge(raised["gelu_done"], at("gelu_done", "join", 1))
                    for f in range(4):
                        cols = slice(f * P, (f + 1) * P)
                        b, u = f % 2, 2 * i + f // 2
                        src = (oaT, obT, yT)[i]
                        if i == 2:
                            claim(pe, 4 + b, "merge", f // 2, n)
                            for k in range(4):
                                mm = pe.matmul(psum[:, 4 + b, :], w_branch[3][:, k, cols], src[:, k, :], start=(k == 0), stop=(k == 3))
                            mm.then_inc(full[4 + b], 1)
                        claim(pe, 2 + b, "merge", u, n)
                        for k in range(4):
                            mm = pe.matmul(psum[:, 2 + b, :], w_branch[i][:, k, cols], src[:, k, :], start=(k == 0), stop=(k == 3))
                        mm.then_inc(full[2 + b], 1)

            pe.wait_ge(raised["merged_ready"], at("merged_ready", "merge", 8, 1))
            pe.wait_ge(w_o_in, 16)

            def w_o_product(t):
                for n in range(2):
                    b = 2 * (t % 2) + n
                    claim(pe, b, "tail", t // 2)
                    for k in range(KD):
                        if t == 0 and n == 0 and k >= 4:
                            pe.wait_ge(raised["merged_ready"], at("merged_ready", "merge", 5 + k, 1))
                        mm = pe.matmul(psum[:, b, :], mergedT[:, k, t * P:(t + 1) * P], w_o[:, k, n * BANK:(n + 1) * BANK],
                                       start=(k == 0), stop=(k == KD - 1))
                    mm.then_inc(full[b], 1)

            def turn_tokens(t):
                pe.wait_ge(raised["ln_ready"], at("ln_ready", "tail", t + 1))
                for i in range(2):
                    claim(pe, 4 + i, "tail", t)
                    for j in range(4):
                        k = 4 * i + j
                        mm = pe.transpose(psum[:, 4 + i, j * P:(j + 1) * P], x_tok[:, t, k * P:(k + 1) * P], ident)
                    mm.then_inc(full[4 + i], 1)

            def route(t):
                for i in range(2):
                    emptied(pe, 4 + i, "tail", t)
                if t == 0:
                    claim(pe, 6, "tail", 0)
                for k in range(KD):
                    mm = pe.matmul(psum[:, 6, t * EXPERTS:(t + 1) * EXPERTS], xT[:, k, t * P:(t + 1) * P], router_w[:, k, :],
                                   start=(k == 0), stop=(k == KD - 1))
                if t == TT - 1:
                    mm.then_inc(full[6], 1)

            w_o_product(0)
            for t in range(1, TT):
                w_o_product(t)
                if t > 1:
                    route(t - 2)
                turn_tokens(t - 1)
            route(TT - 2)
            turn_tokens(TT - 1)
            route(TT - 1)
            pe.wait_ge(pick_ready, 1)
            claim(pe, 7, "tail", 0)
            before = psum[:, 7, 0:(TT + 1) * EXPERTS].rearrange("p (t e) -> p t e", e=EXPERTS)
            for s in range(TT):
                pe.matmul(before[:, s + 1:TT + 1, :], ones, S3(chosen[:, s:s + 1, :], P, TT - s, EXPERTS), start=(s == 0), stop=False)
                mm = pe.matmul(before[:, s, :], const("upper"), chosen[:, s, :], start=False, stop=(s == TT - 1))
            mm.then_inc(full[7], 1)
            meet(pe, "moe")
            most_chosen = pe.value_load(most[0:1, 0:1], min_val=0, max_val=SEQ)

            def experts_pass():
                def bank(stage):
                    return psum[:, ebank[stage], :]

                def dispatch(q, par):
                    pe.wait_ge(sel_ready, q + 1)
                    pe.wait_ge(efree["idx"], q + 1)
                    for t in range(TT):
                        mm = pe.matmul(bank("idx")[:, 0:2], sel[par][:, t].rearrange("p a b -> p (a b)"),
                                       payload[:, t, bass.ds(2 * q, 2)], start=(t == 0), stop=(t == TT - 1))
                    mm.then_inc(efull["idx"], 1)
                    for i, stage in enumerate(("x0", "x1")):
                        pe.wait_ge(efree[stage], q + 1)
                        for j in range(4):
                            k = 4 * i + j
                            for t in range(TT):
                                mm = pe.matmul(bank(stage)[:, j * P:(j + 1) * P], x_tok[:, t, k * P:(k + 1) * P],
                                               sel[par][:, t].rearrange("p a b -> p (a b)"), start=(t == 0), stop=(t == TT - 1))
                        mm.then_inc(efull[stage], 1)

                def product(stage, lhs, chunks, w, cols):
                    for k in range(chunks):
                        for i in range(2):
                            half = slice(i * SLOTS, (i + 1) * SLOTS)
                            mm = pe.matmul(psum[half, ebank[stage], :], lhs[:, k, half], w[i][:, k, cols],
                                           start=(k == 0), stop=(k == chunks - 1))
                    mm.then_inc(efull[stage], 1)

                dispatch(0, 0)
                with pe.Fori(0, PAIRS // 2) as two:
                    for par in range(2):
                        q = two * 2 + par
                        for stage, w, landed in (("gate", e_gate, eg_in), ("up", e_up, eu_in)):
                            for i in range(2):
                                pe.wait_ge(landed[i], q * 16 + 16)
                            if stage == "gate":
                                pe.wait_ge(efree["x0"], q + 2)
                                pe.wait_ge(efree["x1"], q + 2)
                            pe.wait_ge(efree[stage], q + 1)
                            product(stage, tokensT, KD, w, slice(0, FF))
                        pe.wait_ge(he_ready, q + 1)
                        pe.wait_ge(efree["h"], q + 1)
                        for j in range(KF):
                            mm = pe.transpose(bank("h")[:, j * P:(j + 1) * P], hidden[:, j * P:(j + 1) * P], ident)
                        mm.then_inc(efull["h"], 1)
                        pe.wait_ge(efree["h"], q + 2)
                        for n in range(2):
                            pe.wait_ge(ed_in[n], q * 32 + 32)
                            pe.wait_ge(efree[f"y{n}"], q + 1)
                            product(f"y{n}", hiddenT, KF, e_down, slice(n * BANK, (n + 1) * BANK))
                        dispatch(q + 1, 1 - par)
                meet(pe, "passed")

            experts_pass()
            with pe.If(most_chosen > SLOTS):
                with pe.Fori(1, PASSES) as ps:
                    with pe.If(most_chosen > ps * SLOTS):
                        meet(pe, "pass")
                        experts_pass()
                    pe.sem_inc(tick, 1)
            pe.sem_inc(tick, 1)
            meet(pe, "end")

    @block.scalar
    def _(act):
        ch = Chain(act, chains["act"])
        copy = lambda o, i: act.copy(o, i)
        act.wait_ge(setup_ang, 1)
        act.activation(rope_sc[:, 1], rope_ang[:, 0], ACT.Sin).then_inc(setup_trig, 1)
        act.activation(rope_sc[:, 0], rope_ang[:, 1], ACT.Sin, bias=half_pi, scale=-1.0).then_inc(setup_trig, 1)
        with act.Fori(0, DEPTH) as l:
            meet(act, "layer")
            ch.reset()
            for k in range(0, KD, 2):
                filled(act, k, "front", 0)
                copy(xT[:, k, :], psum[:, k, :]).then_inc(free[k], 1)
            act.wait_ge(small_in, 224)
            act.activation(dt_, dt_, ACT.Exp).then_inc(dt_ready, 1)
            act.wait_ge(lam_ready, 1)
            act.activation(lam[:, 0:2], lam[:, 2:4], ACT.Exp).then_inc(lam_exp, 1)
            for t in range(TT):
                filled(act, 4 + t, "front", 1)
                for i, (a, b) in enumerate(((0, Q_LORA), (Q_LORA, Q_LORA + KV_LORA))):
                    ch.then(act.activation(sqs[:, 0:b - a], psum[:, 4 + t, a:b], ACT.Square, accum_out=ssum[:, t, i:i + 1]))
            act.sem_inc(tick, 1)
            act.drain().then_inc(raised["sq_sums"], 1)
            act.wait_ge(raised["rms_mean"], 1)
            act.activation(rrt, rrt, ACT.Sqrt).then_inc(raised["rms_root"], 1)
            act.wait_ge(ang_ready, 1)
            for an, tab in ((ang, fine), (angc, coarse)):
                flat = tab.rearrange("p s a b -> p s (a b)")
                ch.add(act.activation(an[:, 1], an[:, 0], ACT.Abs))
                ch.wait()
                ch.add(act.activation(flat[:, 1], an[:, 0], ACT.Sin, scale=TWO_PI))
                ch.add(act.activation(flat[:, 0], an[:, 1], ACT.Sin, bias=half_pi, scale=-TWO_PI))
            act.drain().then_inc(trig_ready, 1)
            for c in range(4):
                filled(act, c, "front", 1)
                copy(uT[:, c, :], psum[:, c, :]).then_inc(free[c], 1)
            for j in range(3):
                filled(act, j, "front", 2)
                copy(loraT[:, j, :], psum[:, j, :]).then_inc(free[j], 1)

            with act.Fori(0, 4) as c:
                ch.reset()
                for i in range(2):
                    filled(act, i, "heads", 0, c)
                    copy(bT[:, i, :], psum[:, i, :]).then_inc(free[i], 1)
                for i in range(2):
                    filled(act, 2 + i, "heads", 0, c)
                    for j in range(4):
                        ins = copy(cT[:, i, j, :], psum[:, 2 + i, j * 160:j * 160 + 32])
                        if j < 3:
                            ch.add(ins)
                    ins.then_inc(free[2 + i], 1)
                for hh in range(2):
                    u4, u5, u6, us = BASE4[hh], BASE5[hh], BASE6[hh], 1 + 3 * hh
                    filled(act, 5, "heads", u5, c)
                    kv = psum[:, 5, :].rearrange("p (t n) -> p t n", t=TT)
                    if hh == 0:
                        act.wait_ge(krope_ready, 1)
                    ch.add(copy(k_h[:, :, 0:NOPE], kv[:, :, 0:NOPE]))
                    ch.add(copy(k_h[:, :, NOPE:96], krope))
                    copy(v_h, kv[:, :, NOPE:P]).then_inc(free[5], 1)
                    act.drain().then_inc(raised["kv_ready"], 1)

                    def take_diff(i):
                        b, u = ((6, u6), (4, u4 + 1))[i]
                        filled(act, b, "heads", u, c)
                        copy(diff_qkv[:, 2 * i:2 * i + 2, :], psum[:, b, 0:384].rearrange("p (t n) -> p t n", t=2)).then_inc(free[b], 1)

                    def take_bu(j, i):
                        filled(act, 6, "heads", u6 + (2, 3, 4, 6)[2 * j + i], c)
                        copy(bu[:, j, i, :], psum[:, 6, :]).then_inc(free[6], 1)

                    take_diff(0)
                    filled(act, 5, "heads", u5 + 1, c)
                    copy(qT[0:96, :], psum[0:96, 5, :]).then_inc(free[5], 1)
                    take_diff(1)
                    act.drain().then_inc(raised["diff_copied"], 1)
                    take_bu(0, 0)
                    filled(act, 4, "heads", u4 + 2, c)
                    copy(dqT[0:64, :], psum[0:64, 4, :]).then_inc(free[4], 1)

                    def exps(n, p, scale):
                        act.wait_ge(raised["max_ready"], at("max_ready", "heads", 3 * hh + n + 1, c))
                        for t in range(TT):
                            act.activation(causal_part(p, t), psum[:, t, 0:(t + 1) * P], ACT.Exp, bias=softmax_st[:, n, t:t + 1],
                                           scale=scale, accum_out=softmax_st[:, 3 + n, t:t + 1]).then_inc(free[t], 1)

                    def take_p(b, u, t):
                        filled(act, b, "heads", u, c)
                        copy(causal_part(pT, t), psum[:, b, 0:(t + 1) * P]).then_inc(free[b], 1)

                    def take_gate(j):
                        b, u = gate_at(hh, j)
                        filled(act, b, "heads", u, c)
                        act.wait_ge(raised["gate_room"], at("gate_room", "heads", GATE_TILES * hh + j - 1, c))
                        act.activation(gout[:, (hh + j) % 2, :], psum[:, b, :], ACT.Sigmoid, bias=gate_bias[:, j:j + 1]).then_inc(free[b], 1)

                    take_bu(0, 1)
                    exps(0, p1, SCALE_A)
                    take_gate(0)
                    take_bu(1, 0)
                    for t in range(TT):
                        take_p(4 + t % 2, (u4 + 4, u5 + 3)[t % 2] + t // 2, t)
                    take_bu(1, 1)
                    exps(1, p1, SCALE_B)
                    exps(2, p2, SCALE_B)
                    take_gate(1)
                    take_gate(2)
                    filled(act, 6, "heads", u6 + 5, c)
                    for t in (1, 3):
                        take_p(5, u5 + 6 + t // 2, t)
                filled(act, 4, "heads", 18, c)
                act.wait_ge(x_saved, 16)
                copy(oaT[:, bass.ds(c, 1), :].rearrange("p a n -> p (a n)"), psum[:, 4, :]).then_inc(free[4], 1)

            ch.reset()
            act.wait_ge(raised["rms_mean"], at("rms_mean", "join", 1))
            act.activation(ms_b, ms_b, ACT.Sqrt).then_inc(raised["rms_root"], 1)
            act.wait_ge(raised["y_ready"], at("y_ready", "join", 0))
            act.activation(yT, yT, ACT.Gelu_apprx_tanh).then_inc(raised["gelu_done"], 1)

            with act.Fori(0, 2) as n:
                for f in range(4):
                    b = f % 2
                    filled(act, 4 + b, "merge", f // 2, n)
                    act.wait_ge(raised["merged_ready"], at("merged_ready", "merge", 7 + f, n))
                    act.activation(glu_gate[:, b, :], psum[:, 4 + b, :], ACT.Sigmoid).then_inc(free[4 + b], 1)

            def root(st, phase, t):
                act.wait_ge(raised["ln_var"], at("ln_var", phase, t + 1))
                act.activation(st[:, t, 14:15], st[:, t, 13:14], ACT.Sqrt).then_inc(raised["ln_root"], 1)

            def take_xT(t):
                for i in range(2 if t < TT - 1 else 1):
                    filled(act, 4 + i, "tail", t)
                    copy(xT[:, 4 * i:4 * i + 4, t * P:(t + 1) * P], psum[:, 4 + i, :].rearrange("p (k n) -> p k n", k=4)).then_inc(free[4 + i], 1)

            for t in range(TT):
                root(ln_st, "tail", t)
                take_xT(t)
            filled(act, 6, "tail", 0)
            act.activation(router_p, psum[:, 6, 0:TT * EXPERTS].rearrange("p (t e) -> p t e", t=TT), ACT.Sigmoid).then_inc(free[6], 1)
            meet(act, "moe")
            most_chosen = act.value_load(most[0:1, 0:1], min_val=0, max_val=SEQ)

            def experts_pass():
                def take_x(q):
                    act.wait_ge(efull["x0"], q + 1)
                    copy(tokensT[:, 0:4, :].rearrange("p a b -> p (a b)"), psum[:, ebank["x0"], :]).then_inc(efree["x0"], 1)

                take_x(0)
                with act.Fori(0, PAIRS // 2) as two:
                    for par in range(2):
                        q = two * 2 + par
                        act.wait_ge(efull["gate"], q + 1)
                        act.wait_ge(efree["up"], q + 1)
                        act.activation(silu, psum[:, ebank["gate"], :], ACT.Silu).then_inc(efree["gate"], 1)
                        act.wait_ge(efull["h"], q + 1)
                        copy(hiddenT.rearrange("p a b -> p (a b)"), psum[:, ebank["h"], :]).then_inc(efree["h"], 1)
                        act.wait_ge(efull["y0"], q + 1)
                        act.wait_ge(scattered[par], two * 16 + 16)
                        copy(result[par][:, 0:BANK], psum[:, ebank["y0"], :]).then_inc(efree["y0"], 1)
                        take_x(q + 1)
                meet(act, "passed")

            experts_pass()
            with act.If(most_chosen > SLOTS):
                with act.Fori(1, PASSES) as ps:
                    with act.If(most_chosen > ps * SLOTS):
                        meet(act, "pass")
                        experts_pass()
                    act.sem_inc(tick, 1)
            act.sem_inc(tick, 1)
            act.activation(x_tok, x_tok, ACT.Copy, scale=ALPHA).then_inc(alpha_x, 1)

            def first_choice(t):
                act.wait_ge(y_in_s[t], 16)
                y1 = y_in[:, t, 0:D_MODEL]
                act.activation(y1, y1, ACT.Copy, scale=w_tok[:, 0, t:t + 1]).then_inc(y1_ready, 1)

            def moments(t):
                x, y1, st = x_tok[:, t, :], y_in[:, t, 0:D_MODEL], ln2_st[:, t]
                act.wait_ge(x_sum, t + 1)
                ch.then(act.activation(y1, x, ACT.Copy, scale=-1 / D_MODEL, accum_out=st[:, 0:1]))
                act.sem_inc(mean_ready, 1)
                ch.then(act.activation(y1, x, ACT.Square, bias=st[:, 0:1], accum_out=st[:, 1:2]))
                act.activation(st[:, 2:3], st[:, 1:2], ACT.Sqrt, scale=1 / D_MODEL, bias=ln_eps).then_inc(raised["ln_root"], 1)

            ch.reset()
            first_choice(0)
            first_choice(1)
            for t in range(TT):
                moments(t)
                if t + 2 < TT:
                    first_choice(t + 2)
            meet(act, "end")

    @block.vector
    def _(v):
        ch = Chain(v, chains["dve"])
        tt, ts, stt = v.tensor_tensor, v.tensor_scalar, v.scalar_tensor_tensor
        v.wait_ge(tables_in, 32)
        ch.then(v.tensor_copy(rope_pos, pos_i[:]))
        ch.then(tt(rope_ang[:, 0], S3(rope_pos.unsqueeze(2), P, TT, 20), S3(const("inv").unsqueeze(1), P, TT, 20), ALU.mult))
        ch.then(ts(rope_ang[:, 1], rope_ang[:, 0], 1 / TWO_PI, ROUND, ALU.mult, ALU.add))
        ch.then(ts(rope_ang[:, 1], rope_ang[:, 1], -ROUND, None, ALU.add))
        ch.then(stt(out=rope_ang[:, 0], in0=rope_ang[:, 1], scalar=-PI_HI, in1=rope_ang[:, 0], op0=ALU.mult, op1=ALU.add))
        ch.then(stt(out=rope_ang[:, 0], in0=rope_ang[:, 1], scalar=-PI_LO, in1=rope_ang[:, 0], op0=ALU.mult, op1=ALU.add))
        ch.then(ts(rope_ang[:, 0], rope_ang[:, 0], PI_MAX, -PI_MAX, ALU.min, ALU.max))
        ch.then(ts(rope_ang[:, 1], rope_ang[:, 0], -1.0, None, ALU.mult))
        ch.then(tt(rope_ang[:, 1], rope_ang[:, 1], rope_ang[:, 0], ALU.max))
        ch.add(v.memset(ln_eps, LN_EPS))
        v.memset(half_pi, math.pi / 2).then_inc(setup_ang, 1)
        v.wait_ge(setup_trig, 2)
        for tab, i in (((cc_a, cc_b), 0), ((ss_a, ss_b), 1)):
            for s in range(2):
                ch.add(v.tensor_copy(tab[0][:, :, s, :], rope_sc[:, i, :, 0:16]))
                ch.add(v.tensor_copy(tab[1][:, :, 4 * s:4 * s + 4], rope_sc[:, i, :, 16:20]))
        with v.Fori(0, DEPTH) as l:
            meet(v, "layer")
            ch.reset()
            for k in range(1, KD, 2):
                filled(v, k, "front", 0)
                v.tensor_copy(xT[:, k, :], psum[:, k, :]).then_inc(free[k], 1)
            v.wait_ge(small_in, 224)
            ch.then(tt(rtmp[:, 0, 0:2, :], lam_in[:, 0:4:2, :], lam_in[:, 1:4:2, :], ALU.mult))
            v.tensor_reduce(lam[:, 2:4], rtmp[:, 0, 0:2, :], AXX, ALU.add).then_inc(lam_ready, 1)
            ch.add(tt(ssm_vec[:, 14], a_re, a_re, ALU.mult))
            ch.then(tt(ssm_vec[:, 15], a_im, a_im, ALU.mult))
            ch.then(tt(ssm_vec[:, 14], ssm_vec[:, 14], ssm_vec[:, 15], ALU.add))
            ch.add(v.reciprocal(inv_a, ssm_vec[:, 14]))
            ts(subln, subln, lambda_init[:, 1:2], None, ALU.mult).then_inc(subln_ready, 1)
            v.wait_ge(lam_exp, 1)
            ch.then(tt(lam[:, 2:3], lam[:, 1:2], lam[:, 0:1], ALU.subtract))
            ch.then(tt(lam[:, 0:1], lam[:, 2:3], lambda_init[:, 0:1], ALU.subtract))
            zr, zi, pr, pi, a, b, c_, d, rho, wr, wi = (ssm_vec[:, i] for i in range(11))
            v.wait_ge(dt_ready, 1)
            ch.add(tt(zr, a_re, dt_, ALU.mult))
            ch.then(tt(zi, a_im, dt_, ALU.mult))
            ch.add(ts(zr, zr, 2.0 ** -DOUBLINGS, None, ALU.mult))
            ch.then(ts(zi, zi, 2.0 ** -DOUBLINGS, None, ALU.mult))
            ch.add(ts(pr, zr, 1 / 6, 1.0, ALU.mult, ALU.add))
            ch.add(ts(rho, zr, 1 / 6, 1.0, ALU.mult, ALU.add))
            ch.then(ts(pi, zi, 1 / 6, None, ALU.mult))
            for k in (5, 4, 3, 2, 1):
                ch.add(tt(a, zr, pr, ALU.mult))
                ch.add(tt(b, zi, pi, ALU.mult))
                ch.add(tt(c_, zr, pi, ALU.mult))
                ch.add(tt(d, zi, pr, ALU.mult))
                ch.then(tt(rho, zr, rho, ALU.mult))
                o_r, o_i = (pr, pi) if k > 1 else (wr, wi)
                ch.add(tt(a, a, b, ALU.subtract))
                ch.then(tt(c_, c_, d, ALU.add))
                if k > 1:
                    ch.add(ts(rho, rho, 1 / k, 1.0, ALU.mult, ALU.add))
                    ch.add(ts(o_r, a, 1 / k, 1.0, ALU.mult, ALU.add))
                    ch.then(ts(o_i, c_, 1 / k, None, ALU.mult))
                else:
                    ch.add(ts(o_r, a, 1.0, None, ALU.mult))
                    ch.then(ts(o_i, c_, 1.0, None, ALU.mult))
            for _ in range(DOUBLINGS):
                ch.add(tt(a, wr, wr, ALU.mult))
                ch.add(tt(b, wi, wi, ALU.mult))
                ch.add(tt(c_, wr, wi, ALU.mult))
                ch.add(ts(d, wr, 2.0, None, ALU.mult))
                ch.add(tt(zr, rho, rho, ALU.mult))
                ch.then(ts(zi, rho, 2.0, None, ALU.mult))
                ch.add(tt(a, a, b, ALU.subtract))
                ch.add(tt(c_, c_, wi, ALU.add))
                ch.then(tt(rho, zr, zi, ALU.add))
                ch.add(tt(wr, a, d, ALU.add))
                ch.then(ts(wi, c_, 2.0, None, ALU.mult))
            ch.then(ts(radius, rho, 1.0, None, ALU.add))
            v.sem_inc(disc_ready, 1)
            v.wait_ge(raised["sq_sums"], 1)
            ch.add(ts(rrt[:, :, 0:1], ssum[:, :, 0:1], 1 / Q_LORA, RMS_EPS, ALU.mult, ALU.add))
            ch.then(ts(rrt[:, :, 1:2], ssum[:, :, 1:2], 1 / KV_LORA, RMS_EPS, ALU.mult, ALU.add))
            v.sem_inc(raised["rms_mean"], 1)
            v.wait_ge(raised["rms_root"], 1)
            ch.then(v.reciprocal(ssum, rrt))
            for t in range(TT):
                ch.add(stt(out=lora[:, t, 0:Q_LORA], in0=psum[:, 4 + t, 0:Q_LORA], scalar=ssum[:, t, 0:1], in1=qn_bc, op0=ALU.mult, op1=ALU.mult))
                ch.add(stt(out=lora[:, t, Q_LORA:384], in0=psum[:, 4 + t, Q_LORA:384], scalar=ssum[:, t, 1:2], in1=kvn_bc, op0=ALU.mult, op1=ALU.mult))
            kr = psum[:, 4:8, 384:416]
            ch.add(tt(rtmp[:, 0], kr, cc_a.rearrange("p t a b -> p t (a b)"), ALU.mult))
            ch.then(tt(rtmp[:, 1], kr, ss_a.rearrange("p t a b -> p t (a b)"), ALU.mult))
            for t in range(TT):
                v.sem_inc(free[4 + t], 1)
            v.sem_inc(raised["lora_ready"], 1)
            ch.add(tt(krope[:, :, 0:16], rtmp[:, 0, :, 0:16], rtmp[:, 1, :, 16:32], ALU.subtract))
            ch.then(tt(krope[:, :, 16:32], rtmp[:, 0, :, 16:32], rtmp[:, 1, :, 0:16], ALU.add))
            v.sem_inc(krope_ready, 1)

            with v.Fori(0, 4) as c:
                ch.reset()
                for hh in range(2):
                    u4, u5, u6, us = BASE4[hh], BASE5[hh], BASE6[hh], 1 + 3 * hh
                    filled(v, 4, "heads", u4, c)
                    q = psum[:, 4, 0:384].rearrange("p (t n) -> p t n", t=TT)
                    t0, t1 = (tmp_h[:, i].rearrange("p (t n) -> p t n", t=TT) for i in range(2))
                    ch.add(v.tensor_copy(q_h[:, :, 0:NOPE], q[:, :, 0:NOPE]))
                    ch.add(tt(t0, q[:, :, NOPE:96], cc_a.rearrange("p t a b -> p t (a b)"), ALU.mult))
                    ch.then(tt(t1, q[:, :, NOPE:96], ss_a.rearrange("p t a b -> p t (a b)"), ALU.mult))
                    v.sem_inc(free[4], 1)
                    ch.add(tt(q_h[:, :, 64:80], t0[:, :, 0:16], t1[:, :, 16:32], ALU.subtract))
                    ch.then(tt(q_h[:, :, 80:96], t0[:, :, 16:32], t1[:, :, 0:16], ALU.add))
                    v.sem_inc(raised["q_ready"], 1)
                    filled(v, 6, "heads", u6 + 1, c)
                    v.tensor_copy(kT[0:96, :], psum[0:96, 6, :]).then_inc(free[6], 1)
                    v.wait_ge(raised["diff_copied"], at("diff_copied", "heads", hh + 1, c))
                    dq = diff_qkv[:, :, 0:128].rearrange("p t (s n) -> p t s n", n=HD)
                    t2, t3 = (tmp_h[:, 2 + i].rearrange("p (t s n) -> p t s n", t=TT, n=8) for i in range(2))
                    ch.add(tt(t2, dq[:, :, :, 0:8], S3(cc_b.unsqueeze(2), P, TT, 4, 8), ALU.mult))
                    ch.then(tt(t3, dq[:, :, :, 0:8], S3(ss_b.unsqueeze(2), P, TT, 4, 8), ALU.mult))
                    ch.add(tt(dq[:, :, :, 0:4], t2[:, :, :, 0:4], t3[:, :, :, 4:8], ALU.subtract))
                    ch.then(tt(dq[:, :, :, 4:8], t2[:, :, :, 4:8], t3[:, :, :, 0:4], ALU.add))
                    v.sem_inc(raised["diff_ready"], 1)

                    def maxima(n, scale):
                        for t in range(TT):
                            filled(v, t, "heads", us + n, c)
                            d = psum[:, t, t * P:(t + 1) * P]
                            ch.add(tt(d, d, const("causal"), ALU.add))
                        ch.wait()
                        for t in range(TT):
                            ch.add(v.tensor_reduce(softmax_st[:, 6 + n, t:t + 1], psum[:, t, 0:(t + 1) * P], AXX, ALU.max))
                        ch.wait()
                        ch.then(ts(softmax_st[:, n, :], softmax_st[:, 6 + n, :], -scale, None, ALU.mult))
                        v.sem_inc(raised["max_ready"], 1)

                    def scans(j):
                        tile = 2 * hh + j
                        v.wait_ge(raised["rot_ready"], at("rot_ready", "heads", tile + 1, c))
                        emptied(v, 6, "heads", u6 + (3, 6)[j], c)
                        cos, sin, br, bi = rot[:, tile % 2, 0], rot[:, tile % 2, 1], bu[:, tile % 2, 0], bu[:, tile % 2, 1]
                        ch.add(tt(turned[:, 0], br, cos, ALU.mult))
                        ch.then(tt(turned[:, 1], bi, sin, ALU.mult))
                        ch.add(tt(turned[:, 0], turned[:, 0], turned[:, 1], ALU.add))
                        ch.add(tt(bi, bi, cos, ALU.mult))
                        ch.then(tt(br, br, sin, ALU.mult))
                        ch.then(tt(bi, bi, br, ALU.subtract))
                        if tile > 0:
                            v.wait_ge(raised["g_used"], at("g_used", "heads", tile, c))
                        r = S3(radius[:, bass.ds(4 * c + tile, 1)], P, SEQ)
                        for i in range(2):
                            ch.add(v.tensor_tensor_scan(scanned[:, i, :], r, (turned[:, 0], bi)[i], 0.0, ALU.mult, ALU.add))
                        ch.wait()
                        v.sem_inc(raised["scan_ready"], 1)

                    maxima(0, SCALE_A)
                    filled(v, 4, "heads", u4 + 3, c)
                    v.tensor_copy(dkT[0:64, :], psum[0:64, 4, :]).then_inc(free[4], 1)
                    scans(0)
                    emptied(v, 3, "heads", us, c)
                    ch.then(v.reciprocal(softmax_st[:, 9, :], softmax_st[:, 3, :]))
                    filled(v, 6, "heads", u6 + 5, c)
                    ch.then(tt(oa_tok[:, :, hh * 64:hh * 64 + 64], psum[:, 6, 0:256].rearrange("p (t n) -> p t n", t=TT),
                               S3(softmax_st[:, 9, :].unsqueeze(2), P, TT, 64), ALU.mult))
                    v.sem_inc(free[6], 1)
                    v.sem_inc(raised["oa_ready"], 1)
                    maxima(1, SCALE_B)
                    maxima(2, SCALE_B)
                    scans(1)
                    emptied(v, 3, "heads", us + 2, c)
                    ch.then(v.reciprocal(softmax_st[:, 9:11, :], softmax_st[:, 4:6, :]))
                    ch.then(stt(out=softmax_st[:, 11, :], in0=softmax_st[:, 10, :], scalar=lam[:, 0:1], in1=softmax_st[:, 4, :], op0=ALU.mult, op1=ALU.mult))
                    for t in range(TT):
                        ch.then(stt(out=causal_part(p1, t), in0=causal_part(p2, t), scalar=softmax_st[:, 11, t:t + 1], in1=causal_part(p1, t), op0=ALU.mult, op1=ALU.add))
                        v.sem_inc(raised["mix_ready"], 1)
                    for t in (0, 2):
                        filled(v, 4, "heads", u4 + 7 + t // 2, c)
                        v.tensor_copy(causal_part(pT, t), psum[:, 4, 0:(t + 1) * P]).then_inc(free[4], 1)
                    filled(v, 6, "heads", u6 + 7, c)
                    o = psum[:, 6, 0:256].rearrange("p (t n) -> p t n", t=TT)
                    ob = ob_tok[:, :, bass.ds(2 * c + hh, 1), :].rearrange("p t a n -> p t (a n)")
                    ch.then(tt(tmp_o, o, S3(softmax_st[:, 9, :].unsqueeze(2), P, TT, 64), ALU.mult))
                    v.sem_inc(free[6], 1)
                    ch.add(tt(ob, tmp_o, S3(subln.unsqueeze(1), P, TT, 64), ALU.mult))
                    t4 = tmp_h[:, 0:2].rearrange("p a (t n) -> p (a t) n", t=2)
                    ch.then(tt(t4, tmp_o, tmp_o, ALU.mult))
                    ch.then(v.tensor_reduce(ms_b[:, :, bass.ds(2 * c + hh, 1)].rearrange("p t a -> p (t a)"), t4, AXX, ALU.add))
                v.wait_ge(raised["h_used"], at("h_used", "heads", 4, c))
                yc, uc = (a[:, bass.ds(c, 1), :].rearrange("p a n -> p (a n)") for a in (yT, uT))
                ch.then(stt(out=yc, in0=uc, scalar=d_col[:, bass.ds(c, 1)], in1=psum[:, 7, :], op0=ALU.mult, op1=ALU.add))
                v.sem_inc(free[7], 1)
                v.sem_inc(raised["y_ready"], 1)

            ch.reset()
            ch.then(ts(ms_b, ms_b, 1 / 64, SUB_EPS, ALU.mult, ALU.add))
            v.sem_inc(raised["rms_mean"], 1)
            v.wait_ge(raised["rms_root"], at("rms_root", "join", 1))
            ch.then(v.reciprocal(ms_b, ms_b))
            for t in range(TT):
                ch.then(tt(ob_tok[:, t], ob_tok[:, t], S3(ms_b[:, t, :].unsqueeze(2), P, HEADS, 64), ALU.mult))
                v.sem_inc(raised["ob_ready"], 1)
            for i in (2, 3, 0, 1):
                filled(v, i, "join", 0)
                if i == 2:
                    v.wait_ge(raised["pads_ready"], at("pads_ready", "join", 0))
                v.tensor_copy(obT[:, i, :], psum[:, i, :]).then_inc(free[i], 1)

            with v.Fori(0, 2) as n:
                ch.reset()
                for i in range(3):
                    for f in range(4):
                        b, u = f % 2, 2 * i + f // 2
                        m = mergedT[:, bass.ds(4 * n + f, 1), :].rearrange("p a n -> p (a n)")
                        gate = gates[:, bass.ds(4 * n + f + i * KD, 1), :].rearrange("p a n -> p (a n)")
                        if f == 0:
                            v.wait_ge(gates_in[i], 16)
                        filled(v, 2 + b, "merge", u, n)
                        if i == 0:
                            ch.then(tt(m, gate, psum[:, 2 + b, :], ALU.mult))
                            v.sem_inc(free[2 + b], 1)
                        elif i == 1:
                            ch.then(tt(merge_tmp, gate, psum[:, 2 + b, :], ALU.mult))
                            v.sem_inc(free[2 + b], 1)
                            ch.then(tt(m, m, merge_tmp, ALU.add))
                        else:
                            emptied(v, 4 + b, "merge", f // 2, n)
                            ch.then(tt(merge_tmp, glu_gate[:, b, :], psum[:, 2 + b, :], ALU.mult))
                            v.sem_inc(free[2 + b], 1)
                            ch.then(tt(merge_tmp, merge_tmp, gate, ALU.mult))
                            ch.then(tt(m, m, merge_tmp, ALU.add))
                        v.sem_inc(raised["merged_ready"], 1)

            def layernorm(st, g, b, t, phase):
                x = x_tok[:, t, :]
                for i in range(2):
                    ch.add(v.bn_stats(st[:, t, 6 * i:6 * i + 6], x[:, i * BANK:(i + 1) * BANK]))
                ch.wait()
                ch.then(v.bn_aggr(st[:, t, 12:14], st[:, t, 0:12]))
                ch.then(ts(st[:, t, 13:14], st[:, t, 13:14], LN_EPS, None, ALU.add))
                v.sem_inc(raised["ln_var"], 1)
                ch.then(stt(out=x, in0=x, scalar=st[:, t, 12:13], in1=g, op0=ALU.subtract, op1=ALU.mult))
                v.wait_ge(raised["ln_root"], at("ln_root", phase, t + 1))
                ch.then(v.reciprocal(st[:, t, 15:16], st[:, t, 14:15]))
                ch.then(stt(out=x, in0=x, scalar=st[:, t, 15:16], in1=b, op0=ALU.mult, op1=ALU.add))
                v.sem_inc(raised["ln_ready"], 1)

            ch.reset()
            v.wait_ge(x_back, 16)
            v.wait_ge(ln_in, 32)
            for t in range(TT):
                for n in range(2):
                    bank = 2 * (t % 2) + n
                    filled(v, bank, "tail", t // 2)
                    xs = x_tok[:, t, n * BANK:(n + 1) * BANK]
                    ch.then(stt(out=xs, in0=xs, scalar=ALPHA, in1=psum[:, bank, :], op0=ALU.mult, op1=ALU.add))
                    v.sem_inc(free[bank], 1)
                layernorm(ln_st, ln_g, ln_b, t, "tail")
            filled(v, 5, "tail", TT - 1)
            v.tensor_copy(xT[:, 4:8, (TT - 1) * P:], psum[:, 5, :].rearrange("p (k n) -> p k n", k=4)).then_inc(free[5], 1)
            emptied(v, 6, "tail", 0)
            E4 = lambda a: a.rearrange("p t (g j) -> p t g j", j=EPER)
            r0, r1, r2, r3, r4 = (route_tmp[:, i].rearrange("p (t e) -> p t e", t=TT) for i in range(5))
            g0, g1, g2, g3 = (r[:, :, 0:8] for r in (r0, r1, r2, r3))
            g4, g5 = r4[:, :, 0:8], r4[:, :, 8:16]
            ch.then(tt(biased, router_p, S3(router_b.unsqueeze(1), P, TT, EXPERTS), ALU.add))
            a, b, c_, d = (E4(biased)[:, :, :, j] for j in range(4))
            ch.add(tt(g0, a, b, ALU.max))
            ch.add(tt(g1, a, b, ALU.min))
            ch.add(tt(g2, c_, d, ALU.max))
            ch.then(tt(g3, c_, d, ALU.min))
            ch.add(tt(g4, g0, g2, ALU.max))
            ch.add(tt(g5, g0, g2, ALU.min))
            ch.then(tt(g1, g1, g3, ALU.max))
            ch.then(tt(g5, g5, g1, ALU.max))
            ch.then(tt(g0, g4, g5, ALU.add))

            def first_best(values, prio, width, val, tmp, onehot):
                ch.then(v.tensor_reduce(val, values, AXX, ALU.max))
                ch.then(tt(tmp, values, S3(val.unsqueeze(2), P, TT, width), ALU.is_equal))
                ch.then(tt(tmp, tmp, S3(prio.unsqueeze(1), P, TT, width), ALU.mult))
                ch.then(v.tensor_reduce(val, tmp, AXX, ALU.max))
                ch.then(tt(onehot, tmp, S3(val.unsqueeze(2), P, TT, width), ALU.is_equal))

            first_best(g0, const("gprio"), 8, tok_vec[:, 0], g1, g2)
            group = S3(g2.unsqueeze(3), P, TT, EGROUPS, EPER)
            ch.add(tt(E4(r3), E4(biased), group, ALU.mult))
            ch.wait()
            ch.then(ts(g1, g2, -1.0, -NEG, ALU.add, ALU.mult))
            ch.then(tt(E4(r3), E4(r3), S3(g1.unsqueeze(3), P, TT, EGROUPS, EPER), ALU.add))
            first_best(r3, const("eprio"), EXPERTS, tok_vec[:, 1], r4, oh1)
            ch.then(stt(out=r3, in0=oh1, scalar=2 * NEG, in1=r3, op0=ALU.mult, op1=ALU.add))
            first_best(r3, const("eprio"), EXPERTS, tok_vec[:, 2], r4, oh2)
            ch.then(tt(chosen, oh1, oh2, ALU.add))
            v.sem_inc(pick_ready, 1)
            for i, oh in enumerate((oh1, oh2)):
                ch.then(tt(r3, oh, router_p, ALU.mult))
                ch.then(v.tensor_reduce(tok_vec[:, 3 + i], r3, AXX, ALU.add))
            ch.then(tt(tok_vec[:, 5], tok_vec[:, 3], tok_vec[:, 4], ALU.add))
            ch.then(v.reciprocal(tok_vec[:, 6], tok_vec[:, 5]))
            for i in range(2):
                ch.add(tt(w_tok[:, i], tok_vec[:, 3 + i], tok_vec[:, 6], ALU.mult))
            ch.add(v.memset(payload, 0.0))
            ch.add(v.memset(slot_of, -1.0))
            ch.add(v.tensor_copy(slots_now, const("slot")))
            ch.then(ts(tok_vec[:, 0], const("tok"), 2.0, -FAR, ALU.mult, ALU.add))
            ch.then(tt(payload[:, :, 0:EXPERTS], S3(tok_vec[:, 0].unsqueeze(2), P, TT, EXPERTS), oh2, ALU.add))
            filled(v, 7, "tail", 0)
            before = psum[:, 7, 0:TT * EXPERTS].rearrange("p (t e) -> p t e", t=TT)
            ch.then(stt(out=r3, in0=before, scalar=1.0, in1=chosen, op0=ALU.add, op1=ALU.mult))
            ch.add(ts(slot_of[:, :, 0:EXPERTS], r3, -1.0, None, ALU.add))
            ch.then(v.tensor_reduce(tok_vec[:, 1, 0:1], psum[:, 7, TT * EXPERTS:(TT + 1) * EXPERTS], AXX, ALU.max))
            ch.then(v.tensor_copy(most[:], tok_vec[:, 1, 0:1]))
            v.sem_inc(free[7], 1)
            meet(v, "moe")
            most_chosen = v.value_load(most[0:1, 0:1], min_val=0, max_val=SEQ)

            def experts_pass():
                def select(q, par):
                    tt(sel[par], S3(slots_now.unsqueeze(1).unsqueeze(1), P, TT, 2, SLOTS),
                       S3(slot_of[:, :, bass.ds(2 * q, 2)].unsqueeze(3), P, TT, 2, SLOTS), ALU.is_equal).then_inc(sel_ready, 1)

                def take_rows(par):
                    for i in range(2):
                        half = slice(i * SLOTS, (i + 1) * SLOTS)
                        ins = ts(row_y[par][half, :], psum[half, ebank["idx"], i:i + 1], FAR, None, ALU.add)
                        if i == 0:
                            ins.then_inc(tick, 1)
                    return ins

                def take_x(q):
                    v.wait_ge(efull["x1"], q + 1)
                    v.tensor_copy(tokensT[:, 4:8, :].rearrange("p a b -> p (a b)"), psum[:, ebank["x1"], :]).then_inc(efree["x1"], 1)

                select(0, 0)
                take_x(0)
                with v.Fori(0, PAIRS // 2) as two:
                    for par in range(2):
                        q = two * 2 + par
                        select(q + 1, 1 - par)
                        v.wait_ge(efree["gate"], q + 2)
                        v.wait_ge(efull["up"], q + 1)
                        tt(hidden, silu, psum[:, ebank["up"], :], ALU.mult).then_inc(he_ready, 1)
                        v.wait_ge(he_ready, q + 1)
                        v.sem_inc(efree["up"], 1)
                        v.wait_ge(scattered[par], two * 16 + 16)
                        v.wait_ge(efull["idx"], q + 1)
                        take_rows(par).then_inc(efree["idx"], 1)
                        v.wait_ge(efull["y1"], q + 1)
                        v.tensor_copy(result[par][:, BANK:], psum[:, ebank["y1"], :]).then_inc(efree["y1"], 1)
                        take_x(q + 1)
                meet(v, "passed")

            experts_pass()
            with v.If(most_chosen > SLOTS):
                with v.Fori(1, PASSES) as ps:
                    with v.If(most_chosen > ps * SLOTS):
                        meet(v, "pass")
                        ch.reset()
                        ch.then(ts(slots_now, slots_now, float(SLOTS), None, ALU.add))
                        experts_pass()
                    v.sem_inc(tick, 1)
            v.sem_inc(tick, 1)
            ch.reset()
            v.wait_ge(ln2_in, 32)

            def combine(t):
                x = x_tok[:, t, :]
                v.wait_ge(y_in_s[t], 16)
                v.wait_ge(x_y1, t + 1)
                ch.then(stt(out=x, in0=y_in[:, t, D_MODEL:], scalar=w_tok[:, 1, t:t + 1], in1=x, op0=ALU.mult, op1=ALU.add))
                v.sem_inc(x_sum, 1)

            def normalise(t):
                x, xc, st = x_tok[:, t, :], y_in[:, t, D_MODEL:], ln2_st[:, t]
                v.wait_ge(mean_ready, t + 1)
                ch.add(stt(out=xc, in0=x, scalar=st[:, 0:1], in1=ln2_g, op0=ALU.add, op1=ALU.mult))
                v.wait_ge(raised["ln_root"], at("ln_root", "last", t + 1))
                ch.then(v.reciprocal(st[:, 3:4], st[:, 2:3]))
                ch.add(stt(out=x, in0=xc, scalar=st[:, 3:4], in1=ln2_b, op0=ALU.mult, op1=ALU.add))

            combine(0)
            for t in range(TT):
                if t + 1 < TT:
                    combine(t + 1)
                normalise(t)
            meet(v, "end")

    @block.gpsimd
    def _(g):
        ch = Chain(g, chains["pool"])
        tt, ts = g.tensor_tensor, g.tensor_scalar
        g.wait_ge(tables_in, 32)
        g.wait_ge(setup_in, 48)
        ch.then(ts(row_none[:], const("tok")[:, 0:1], FAR, None, ALU.add))
        with g.Fori(0, DEPTH) as l:
            meet(g, "layer")
            ch.reset()
            g.wait_ge(small_in, 224)
            g.wait_ge(dt_ready, 1)
            ch.then(tt(ssm_vec[:, 11], a_im, dt_, ALU.mult))
            ch.then(ts(phi, ssm_vec[:, 11], 1 / TWO_PI, None, ALU.mult))
            for an, steps, width in ((ang, const("fine"), FINE), (angc, const("coarse"), COARSE)):
                x0, x1 = (an[:, i].rearrange("p (s n) -> p s n", n=width) for i in (0, 1))
                ch.then(tt(x0, S3(phi.unsqueeze(2), P, STILES, width), S3(steps.unsqueeze(1), P, STILES, width), ALU.mult))
                ch.then(ts(x1, x0, ROUND, None, ALU.add))
                ch.then(ts(x1, x1, -ROUND, None, ALU.add))
                ch.then(tt(x0, x0, x1, ALU.subtract))
            g.sem_inc(ang_ready, 1)
            g.wait_ge(disc_ready, 1)
            a, b, c_, d, wr, wi = (ssm_vec[:, i] for i in (4, 5, 6, 7, 9, 10))
            ch.add(tt(a, wr, a_re, ALU.mult))
            ch.add(tt(b, wi, a_im, ALU.mult))
            ch.add(tt(c_, wi, a_re, ALU.mult))
            ch.then(tt(d, wr, a_im, ALU.mult))
            ch.add(tt(a, a, b, ALU.add))
            ch.then(tt(c_, c_, d, ALU.subtract))
            ch.add(tt(wr, a, inv_a, ALU.mult))
            ch.then(tt(wi, c_, inv_a, ALU.mult))
            qr, qi = (S3(w.unsqueeze(2), P, STILES, GROUP) for w in (wr, wi))
            ch.add(tt(btmp[:, 0], b_in[:, 0], qr, ALU.mult))
            ch.then(tt(btmp[:, 1], b_in[:, 1], qi, ALU.mult))
            ch.then(tt(bbar[:, 0], btmp[:, 0], btmp[:, 1], ALU.subtract))
            ch.add(tt(btmp[:, 0], b_in[:, 1], qr, ALU.mult))
            ch.then(tt(btmp[:, 1], b_in[:, 0], qi, ALU.mult))
            ch.then(tt(bbar[:, 1], btmp[:, 0], btmp[:, 1], ALU.add))
            ch.then(ts(c_nat[:, 1], c_nat[:, 1], -1.0, None, ALU.mult))
            def make_pads(c):
                for i in range(2):
                    src = bbar[:, i, bass.ds(4 * c, 4), :]
                    ch.add(tt(pads[:, i].rearrange("p (j g q) -> p j g q", j=4, q=GROUP), S3(src.unsqueeze(2), P, 4, 8, GROUP),
                              S3(const("bmask").rearrange("p (j g) -> p j g", j=4).unsqueeze(3), P, 4, 8, GROUP), ALU.mult))
                    cn = c_nat[:, i, bass.ds(c, 1), :]
                    ch.add(tt(pads[:, 2 + i].rearrange("p (g n) -> p g n", g=8), S3(cn, P, 8, STATES),
                              S3(const("gmask").unsqueeze(2), P, 8, STATES), ALU.mult))
                ch.wait()
                g.sem_inc(raised["pads_ready"], 1)

            filled(g, KD - 1, "front", 0)
            g.wait_ge(x_saved, 16)
            make_pads(0)
            g.wait_ge(trig_ready, 1)
            for j in range(3):
                emptied(g, j, "front", 2)
            with g.Fori(0, 4) as c:
                ch.reset()

                def turns(tile):
                    def tab(which, i, width):
                        return which[:, i, bass.ds(4 * c + tile, 1), :].rearrange("p a n -> p (a n)")
                    cf, sf = (S3(tab(fine, i, FINE).unsqueeze(1), P, COARSE, FINE) for i in range(2))
                    cc, sc_ = (S3(tab(coarse, i, COARSE).unsqueeze(2), P, COARSE, FINE) for i in range(2))
                    V = lambda x: x.rearrange("p (a b) -> p a b", b=FINE)
                    ch.add(tt(V(turn_tmp[:, 0]), cc, cf, ALU.mult))
                    ch.then(tt(V(turn_tmp[:, 1]), sc_, sf, ALU.mult))
                    ch.then(tt(rot[:, tile % 2, 0], turn_tmp[:, 0], turn_tmp[:, 1], ALU.subtract))
                    ch.add(tt(V(turn_tmp[:, 0]), sc_, cf, ALU.mult))
                    ch.then(tt(V(turn_tmp[:, 1]), cc, sf, ALU.mult))
                    ch.then(tt(rot[:, tile % 2, 1], turn_tmp[:, 0], turn_tmp[:, 1], ALU.add))
                    g.sem_inc(raised["rot_ready"], 1)

                def back(tile):
                    g.wait_ge(raised["scan_ready"], at("scan_ready", "heads", tile + 1, c))
                    cos, sin, gr, gi = rot[:, tile % 2, 0], rot[:, tile % 2, 1], scanned[:, 0], scanned[:, 1]
                    ch.add(tt(turn_tmp[:, 0], gr, cos, ALU.mult))
                    ch.then(tt(turn_tmp[:, 1], gi, sin, ALU.mult))
                    if tile >= 2:
                        g.wait_ge(raised["h_used"], at("h_used", "heads", tile - 1, c))
                    ch.then(tt(states[:, tile % 2, 0], turn_tmp[:, 0], turn_tmp[:, 1], ALU.subtract))
                    ch.add(tt(turn_tmp[:, 0], gr, sin, ALU.mult))
                    ch.then(tt(turn_tmp[:, 1], gi, cos, ALU.mult))
                    g.sem_inc(raised["g_used"], 1)
                    ch.then(tt(states[:, tile % 2, 1], turn_tmp[:, 0], turn_tmp[:, 1], ALU.add))
                    g.sem_inc(raised["h_ready"], 1)

                turns(0)
                turns(1)
                back(0)
                filled(g, 3, "heads", 0, c)
                make_pads((c + 1) % 4)
                turns(2)
                back(1)
                turns(3)
                back(2)
                back(3)

            def reset_dma_sems():
                dma_sems = range(scattered[0].num, scattered[1].num + 1)
                g.dma_reset(dma_sems)
                g.sem_clear(dma_sems)

            reset_dma_sems()
            meet(g, "moe")
            most_chosen = g.value_load(most[0:1, 0:1], min_val=0, max_val=SEQ)

            def experts_pass():
                def scatter(data, rows_of, signal):
                    g.indirect_dma_start(out=y_moe, out_offset=bass.IndirectOffsetOnAxis(ap=rows_of[:, 0:1], axis=0),
                                         in_=data, in_offset=None,
                                         bounds_check=2 * SEQ - 1, oob_is_err=False).then_inc(signal, 16)

                for i in range(2):
                    scatter(x_tok[:, 0, :], row_none, scattered[i])
                with g.Fori(0, PAIRS // 2) as two:
                    for par in range(2):
                        q = two * 2 + par
                        for stage in ("idx", "y0", "y1"):
                            g.wait_ge(efree[stage], q + 2)
                        g.sem_inc(tick, 1)
                        scatter(result[par], row_y[par], scattered[par])
                for i in range(2):
                    g.wait_ge(scattered[i], 16 * (PAIRS // 2 + 1))
                meet(g, "passed")

            experts_pass()
            with g.If(most_chosen > SLOTS):
                with g.Fori(1, PASSES) as ps:
                    with g.If(most_chosen > ps * SLOTS):
                        reset_dma_sems()
                        meet(g, "pass")
                        experts_pass()
                    g.sem_inc(tick, 1)
            g.sem_inc(tick, 1)
            g.wait_ge(alpha_x, 1)
            for t in range(TT):
                g.wait_ge(y1_ready, t + 1)
                tt(x_tok[:, t, :], x_tok[:, t, :], y_in[:, t, 0:D_MODEL], ALU.add).then_inc(x_y1, 1)
            meet(g, "end")

    ctx.close()


_INS = ["x", "positions", "w_in", "b_gate", "mla_q_norm", "mla_w_uq", "mla_kv_norm", "mla_w_ukv", "mla_w_out",
        "diff_lambda", "diff_subln", "diff_w_out", "ssm_a_re", "ssm_a_im", "ssm_log_dt", "ssm_b_re", "ssm_b_im",
        "ssm_c_re", "ssm_c_im", "ssm_d", "ssm_w_glu", "w_o", "ln_gain", "ln_bias", "router_w", "router_bias",
        "moe_w_gate", "moe_w_up", "moe_w_down"]


def kernel(**inputs):
    import concourse.bacc as _bacc
    from concourse.bass_utils import run_bass_kernel_spmd as _run

    nc = _bacc.Bacc("TRN2", target_bir_lowering=False, num_devices=1)
    arrays, aps = {}, {}
    for name in _INS:
        a = np.ascontiguousarray(inputs[name])
        arrays[f"in_{name}"] = a
        aps[name] = nc.dram_tensor(f"in_{name}", a.shape, mybir.dt.from_np(a.dtype), kind="ExternalInput").ap()
    tables = {}
    for name, a in (("constants", constant_table()), ("layers", layer_table())):
        arrays[name] = a
        tables[name] = nc.dram_tensor(name, a.shape, F32, kind="ExternalInput").ap()
    out = nc.dram_tensor("out", (1, SEQ, D_MODEL), F32, kind="ExternalOutput").ap()
    build(nc, aps, tables["constants"], tables["layers"], out)
    r = _run(nc, [arrays], core_ids=[0])
    return r.results[0]["out"]
```
